# Optimizing a Trainium2 kernel written in Bass

```python
import math
import numpy as np
import jax, jax.numpy as jnp
from jax import lax

D_MODEL = 1024
BATCH = 1
SEQ = 512
DEPTH = 1

HEAD_DIM = 64
NSA_HEADS = 8
NSA_KV_HEADS = 2
NSA_GROUP = NSA_HEADS // NSA_KV_HEADS
CMP_LEN = 32
CMP_STRIDE = 16
CMP_HID = 128
SLC_LEN = 64
SLC_TOPN = 16
WINDOW = 512
DSA_HEADS = 8
DSA_KV_RANK = 128
IDX_HEADS = 8
IDX_DIM = 64
DSA_TOPK_MAX = 256
N_EXPERTS = 32
MOE_TOPK = 4
D_EXPERT = 1024
SWIGLU_LIMIT = 7.0
SWIGLU_ALPHA = 1.702
REL_BUCKETS = 32
REL_MAX_DIST = 128
N_BIAS_HEADS = NSA_HEADS + DSA_HEADS
Q_BLOCK = 128
MOE_ROW_BLOCK = 128
NORM_EPS = 1e-6
NEG = -1e30

kernel_name = 'hybrid_nsa_dsa_moe_block'

def _in_widths():
    kv = NSA_KV_HEADS * HEAD_DIM
    return (NSA_HEADS * HEAD_DIM, kv, kv, kv, kv, kv, kv, NSA_HEADS * 3,
            DSA_HEADS * HEAD_DIM, DSA_KV_RANK, IDX_HEADS * IDX_DIM, IDX_DIM, IDX_HEADS,
            D_MODEL, D_MODEL)

def _split_offsets():
    offs, acc = [], 0
    for w in _in_widths()[:-1]:
        acc += w
        offs.append(acc)
    return offs

def rms_norm(x, g):
    xf = x.astype(jnp.float32)
    y = xf * lax.rsqrt(jnp.mean(xf * xf, axis=-1, keepdims=True) + NORM_EPS)
    return (y * g.astype(jnp.float32)).astype(x.dtype)

def masked_softmax(logits, mask):
    p = jax.nn.softmax(jnp.where(mask, logits, NEG), axis=-1)
    return jnp.where(mask, p, 0.0)

def rel_bucket(rel):
    n = jnp.maximum(rel, 0)
    exact = REL_BUCKETS // 2
    nf = jnp.maximum(n, 1).astype(jnp.float32)
    large = exact + (jnp.log(nf / exact) / math.log(REL_MAX_DIST / exact) * (REL_BUCKETS - exact)).astype(jnp.int32)
    large = jnp.minimum(large, REL_BUCKETS - 1)
    return jnp.where(n < exact, n, large)

def compress_blocks(x, pe, w1, b1, w2):
    B, S, G, dk = x.shape
    n_c = (S - CMP_LEN) // CMP_STRIDE + 1
    idx = np.arange(n_c, dtype=np.int32)[:, None] * CMP_STRIDE + np.arange(CMP_LEN, dtype=np.int32)[None, :]
    blk = x[:, idx] + pe[:, None, :]
    flat = blk.transpose(0, 1, 3, 2, 4).reshape(B, n_c, G, CMP_LEN * dk)
    return jax.nn.gelu(flat @ w1 + b1) @ w2

def nsa_attention(q, kc, vc, ks, vs, kw, vw, gates, tab):
    B, S, G, hg, dk = q.shape
    n_c = kc.shape[1]
    n_s = S // SLC_LEN
    n_top = min(SLC_TOPN, n_s)
    scale = dk ** -0.5
    f32 = jnp.float32
    c_start = np.arange(n_c, dtype=np.int32) * CMP_STRIDE
    c_last = c_start + (CMP_LEN - 1)
    s_start = np.arange(n_s, dtype=np.int32) * SLC_LEN
    overlap = jnp.asarray(((c_start[:, None] < s_start[None, :] + SLC_LEN) &
                           (c_start[:, None] + CMP_LEN > s_start[None, :])).astype(np.float32))
    ks_blk = ks.reshape(B, n_s, SLC_LEN, G, dk).transpose(0, 3, 1, 2, 4)
    vs_blk = vs.reshape(B, n_s, SLC_LEN, G, dk).transpose(0, 3, 1, 2, 4)
    kw_pad = jnp.pad(kw, ((0, 0), (WINDOW, 0), (0, 0), (0, 0)))
    vw_pad = jnp.pad(vw, ((0, 0), (WINDOW, 0), (0, 0), (0, 0)))
    n_win = Q_BLOCK + WINDOW
    rel_w = jnp.arange(Q_BLOCK)[:, None] - (jnp.arange(n_win) - WINDOW)[None, :]
    in_band = (rel_w >= 0) & (rel_w < WINDOW)
    bias_w = tab[rel_bucket(rel_w)].reshape(Q_BLOCK, n_win, G, hg).transpose(0, 2, 3, 1)
    tab_g = tab.reshape(REL_BUCKETS, G, hg).transpose(1, 0, 2)
    g_idx = jnp.arange(G)[None, :, None, None]
    blk_ids = jnp.arange(n_s, dtype=jnp.int32)
    take = jax.vmap(jax.vmap(lambda blocks, ix: blocks[ix]))

    def one_block(i):
        t0 = i * Q_BLOCK
        tpos = t0 + jnp.arange(Q_BLOCK, dtype=jnp.int32)
        qb = lax.dynamic_slice_in_dim(q, t0, Q_BLOCK, axis=1)
        gb = lax.dynamic_slice_in_dim(gates, t0, Q_BLOCK, axis=1)
        rel_c = tpos[:, None] - c_last[None, :]
        bias_c = tab[rel_bucket(rel_c)].reshape(Q_BLOCK, n_c, G, hg).transpose(0, 2, 3, 1)
        s_c = jnp.einsum('btghd,bcgd->btghc', qb, kc).astype(f32) * scale + bias_c
        p_c = masked_softmax(s_c, (rel_c >= 0)[:, None, None, :])
        o_c = jnp.einsum('btghc,bcgd->btghd', p_c.astype(vc.dtype), vc)
        imp = jnp.einsum('btghc,cj->btgj', p_c, overlap)
        cur = tpos // SLC_LEN
        forced = (blk_ids[None, :] == 0) | (blk_ids[None, :] == cur[:, None]) | (blk_ids[None, :] == cur[:, None] - 1)
        visible = blk_ids[None, :] <= cur[:, None]
        imp = jnp.where(forced[None, :, None, :], 1e6, jnp.where(visible[None, :, None, :], imp, -1e6))
        sel = lax.top_k(imp, n_top)[1].transpose(0, 2, 1, 3)
        n_k = n_top * SLC_LEN
        k_sel = take(ks_blk, sel).reshape(B, G, Q_BLOCK, n_k, dk)
        v_sel = take(vs_blk, sel).reshape(B, G, Q_BLOCK, n_k, dk)
        pos_sel = (sel[..., None] * SLC_LEN + jnp.arange(SLC_LEN, dtype=jnp.int32)).reshape(B, G, Q_BLOCK, n_k)
        rel_s = tpos[None, None, :, None] - pos_sel
        bias_s = tab_g[g_idx, rel_bucket(rel_s)].transpose(0, 1, 2, 4, 3)
        qg = qb.transpose(0, 2, 1, 3, 4)
        s_s = jnp.einsum('bgthd,bgtnd->bgthn', qg, k_sel).astype(f32) * scale + bias_s
        p_s = masked_softmax(s_s, (rel_s >= 0)[:, :, :, None, :])
        o_s = jnp.einsum('bgthn,bgtnd->bgthd', p_s.astype(v_sel.dtype), v_sel).transpose(0, 2, 1, 3, 4)
        kwb = lax.dynamic_slice_in_dim(kw_pad, t0, n_win, axis=1)
        vwb = lax.dynamic_slice_in_dim(vw_pad, t0, n_win, axis=1)
        kpos = t0 - WINDOW + jnp.arange(n_win, dtype=jnp.int32)
        mask_w = in_band & (kpos >= 0)[None, :]
        s_w = jnp.einsum('btghd,bkgd->btghk', qb, kwb).astype(f32) * scale + bias_w
        p_w = masked_softmax(s_w, mask_w[:, None, None, :])
        o_w = jnp.einsum('btghk,bkgd->btghd', p_w.astype(vwb.dtype), vwb)
        o = gb[..., 0:1] * o_c + gb[..., 1:2] * o_s + gb[..., 2:3] * o_w
        return o.reshape(B, Q_BLOCK, G * hg * dk)

    out = lax.map(one_block, jnp.arange(S // Q_BLOCK, dtype=jnp.int32))
    return out.transpose(1, 0, 2, 3).reshape(B, S, G * hg * dk)

def dsa_attention(q, k, v, iq, ik, iw, tab):
    B, S, H, dk = q.shape
    n_keep = min(DSA_TOPK_MAX, S // 4)
    scale = dk ** -0.5
    idx_scale = IDX_DIM ** -0.5
    f32 = jnp.float32
    key_pos = jnp.arange(S, dtype=jnp.int32)
    take = jax.vmap(lambda rows, ix: rows[ix])

    def one_block(i):
        t0 = i * Q_BLOCK
        tpos = t0 + jnp.arange(Q_BLOCK, dtype=jnp.int32)
        qb = lax.dynamic_slice_in_dim(q, t0, Q_BLOCK, axis=1)
        iqb = lax.dynamic_slice_in_dim(iq, t0, Q_BLOCK, axis=1)
        iwb = lax.dynamic_slice_in_dim(iw, t0, Q_BLOCK, axis=1)
        act = jax.nn.relu(jnp.einsum('bthd,bsd->bths', iqb, ik).astype(f32) * idx_scale)
        score = jnp.einsum('bths,bth->bts', act, iwb.astype(f32))
        causal = tpos[:, None] >= key_pos[None, :]
        score = jnp.where(causal[None], score, NEG)
        sel = lax.top_k(score, n_keep)[1]
        k_sel = take(k, sel)
        v_sel = take(v, sel)
        rel = tpos[None, :, None] - sel
        bias = tab[rel_bucket(rel)].transpose(0, 1, 3, 2)
        s = jnp.einsum('bthd,btnd->bthn', qb, k_sel).astype(f32) * scale + bias
        p = masked_softmax(s, (rel >= 0)[:, :, None, :])
        o = jnp.einsum('bthn,btnd->bthd', p.astype(v_sel.dtype), v_sel)
        return o.reshape(B, Q_BLOCK, H * dk)

    out = lax.map(one_block, jnp.arange(S // Q_BLOCK, dtype=jnp.int32))
    return out.transpose(1, 0, 2, 3).reshape(B, S, H * dk)

def clamped_swiglu(hu):
    glu, lin = hu[..., ::2], hu[..., 1::2]
    glu = jnp.minimum(glu, SWIGLU_LIMIT)
    lin = jnp.clip(lin, -SWIGLU_LIMIT, SWIGLU_LIMIT)
    return glu * jax.nn.sigmoid(SWIGLU_ALPHA * glu) * (lin + 1.0)

def moe_ffn(h, w_router, b_router, w_gate_up, b_gate_up, w_down, b_down):
    B, S, D = h.shape
    N = B * S
    NK = N * MOE_TOPK
    R = MOE_ROW_BLOCK
    xf = h.reshape(N, D)
    logits = (xf @ w_router).astype(jnp.float32) + b_router.astype(jnp.float32)
    top_val, top_e = lax.top_k(logits, MOE_TOPK)
    gate = jax.nn.softmax(top_val, axis=-1)
    flat_e = top_e.reshape(-1)
    flat_tok = jnp.repeat(jnp.arange(N, dtype=jnp.int32), MOE_TOPK)
    order = jnp.argsort(flat_e)
    se, st, sg = flat_e[order], flat_tok[order], gate.reshape(-1)[order]
    counts = jnp.bincount(flat_e, length=N_EXPERTS)
    padded = (counts + R - 1) // R * R
    pad_end = jnp.cumsum(padded)
    pad_start = pad_end - padded
    start = jnp.cumsum(counts) - counts
    dest = pad_start[se] + (jnp.arange(NK, dtype=jnp.int32) - start[se])
    n_rows = (NK + R - 1) // R * R + N_EXPERTS * R
    n_blocks = n_rows // R
    row_tok = jnp.full((n_rows,), N, jnp.int32).at[dest].set(st)
    row_gate = jnp.zeros((n_rows,), jnp.float32).at[dest].set(sg)
    blk_e = jnp.minimum(jnp.searchsorted(pad_end, jnp.arange(n_blocks, dtype=jnp.int32) * R, side='right'), N_EXPERTS - 1)
    x_pad = jnp.concatenate([xf, jnp.zeros((1, D), xf.dtype)], axis=0)

    def run_block(args):
        tok, g, e = args
        xb = x_pad[tok]
        hu = xb @ w_gate_up[e] + b_gate_up[e]
        y = clamped_swiglu(hu) @ w_down[e] + b_down[e]
        return y * g[:, None].astype(y.dtype)

    ys = lax.map(run_block, (row_tok.reshape(n_blocks, R), row_gate.reshape(n_blocks, R), blk_e))
    out = jnp.zeros((N + 1, D), ys.dtype).at[row_tok].add(ys.reshape(n_rows, D))
    return out[:N].reshape(B, S, D)

def hybrid_layer(x, attn_norm, w_in, nsa_q_norm, nsa_k_norm, cmp_k_pe, cmp_k_w1, cmp_k_b1, cmp_k_w2,
                 cmp_v_pe, cmp_v_w1, cmp_v_b1, cmp_v_w2, dsa_kv_norm, dsa_w_uk, dsa_w_uv, dsa_q_norm,
                 dsa_k_norm, w_branch_a, w_branch_b, w_out, rel_bias, ffn_norm, w_router, b_router,
                 w_gate_up, b_gate_up, w_down, b_down):
    B, S, _ = x.shape
    G, hg, dk = NSA_KV_HEADS, NSA_GROUP, HEAD_DIM
    h = rms_norm(x, attn_norm)
    (a_q, c_k, c_v, s_k, s_v, w_k, w_v, a_g, b_q, b_ckv, i_q, i_k, i_w, g_a, g_b) = jnp.split(h @ w_in, _split_offsets(), axis=-1)
    kv_shape = (B, S, G, dk)
    q_a = rms_norm(a_q.reshape(B, S, NSA_HEADS, dk), nsa_q_norm).reshape(B, S, G, hg, dk)
    kc = rms_norm(compress_blocks(c_k.reshape(kv_shape), cmp_k_pe, cmp_k_w1, cmp_k_b1, cmp_k_w2), nsa_k_norm)
    vc = compress_blocks(c_v.reshape(kv_shape), cmp_v_pe, cmp_v_w1, cmp_v_b1, cmp_v_w2)
    ks = rms_norm(s_k.reshape(kv_shape), nsa_k_norm)
    kw = rms_norm(w_k.reshape(kv_shape), nsa_k_norm)
    branch_gates = jax.nn.sigmoid(a_g).reshape(B, S, G, hg, 3)
    o_a = nsa_attention(q_a, kc, vc, ks, s_v.reshape(kv_shape), kw, w_v.reshape(kv_shape), branch_gates, rel_bias[:, :NSA_HEADS])
    q_b = rms_norm(b_q.reshape(B, S, DSA_HEADS, dk), dsa_q_norm)
    ckv = rms_norm(b_ckv, dsa_kv_norm)
    k_b = rms_norm(ckv @ dsa_w_uk, dsa_k_norm)
    v_b = ckv @ dsa_w_uv
    o_b = dsa_attention(q_b, k_b, v_b, i_q.reshape(B, S, IDX_HEADS, IDX_DIM), i_k, i_w * IDX_HEADS ** -0.5, rel_bias[:, NSA_HEADS:])
    merged = jax.nn.sigmoid(g_a) * (o_a @ w_branch_a) + jax.nn.sigmoid(g_b) * (o_b @ w_branch_b)
    x = x + merged @ w_out
    return x + moe_ffn(rms_norm(x, ffn_norm), w_router, b_router, w_gate_up, b_gate_up, w_down, b_down)

def setup_inputs(seed: int = 0) -> dict:
    key = jax.random.key(seed)
    ks = jax.random.split(key, 32)
    L, D, dk = DEPTH, D_MODEL, HEAD_DIM
    d_in = sum(_in_widths())
    f32 = jnp.float32

    def nrm(k, shape, scale):
        return jax.random.normal(k, shape, f32) * scale

    def gain(k, n):
        return 1.0 + 0.02 * jax.random.normal(k, (L, n), f32)

    return {
        'x': jax.random.normal(ks[0], (BATCH, SEQ, D), f32),
        'attn_norm': gain(ks[1], D),
        'w_in': nrm(ks[2], (L, D, d_in), D ** -0.5),
        'nsa_q_norm': gain(ks[3], dk),
        'nsa_k_norm': gain(ks[4], dk),
        'cmp_k_pe': nrm(ks[5], (L, CMP_LEN, dk), 0.1),
        'cmp_k_w1': nrm(ks[6], (L, CMP_LEN * dk, CMP_HID), (CMP_LEN * dk) ** -0.5),
        'cmp_k_b1': nrm(ks[7], (L, CMP_HID), 0.01),
        'cmp_k_w2': nrm(ks[8], (L, CMP_HID, dk), CMP_HID ** -0.5),
        'cmp_v_pe': nrm(ks[9], (L, CMP_LEN, dk), 0.1),
        'cmp_v_w1': nrm(ks[10], (L, CMP_LEN * dk, CMP_HID), (CMP_LEN * dk) ** -0.5),
        'cmp_v_b1': nrm(ks[11], (L, CMP_HID), 0.01),
        'cmp_v_w2': nrm(ks[12], (L, CMP_HID, dk), CMP_HID ** -0.5),
        'dsa_kv_norm': gain(ks[13], DSA_KV_RANK),
        'dsa_w_uk': nrm(ks[14], (L, DSA_KV_RANK, dk), DSA_KV_RANK ** -0.5),
        'dsa_w_uv': nrm(ks[15], (L, DSA_KV_RANK, dk), DSA_KV_RANK ** -0.5),
        'dsa_q_norm': gain(ks[16], dk),
        'dsa_k_norm': gain(ks[17], dk),
        'w_branch_a': nrm(ks[18], (L, NSA_HEADS * dk, D), (NSA_HEADS * dk) ** -0.5),
        'w_branch_b': nrm(ks[19], (L, DSA_HEADS * dk, D), (DSA_HEADS * dk) ** -0.5),
        'w_out': nrm(ks[20], (L, D, D), D ** -0.5),
        'rel_bias': nrm(ks[21], (REL_BUCKETS, N_BIAS_HEADS), 0.2),
        'ffn_norm': gain(ks[22], D),
        'w_router': nrm(ks[23], (L, D, N_EXPERTS), D ** -0.5),
        'b_router': nrm(ks[24], (L, N_EXPERTS), 0.01),
        'w_gate_up': nrm(ks[25], (L, N_EXPERTS, D, 2 * D_EXPERT), D ** -0.5),
        'b_gate_up': nrm(ks[26], (L, N_EXPERTS, 2 * D_EXPERT), 0.01),
        'w_down': nrm(ks[27], (L, N_EXPERTS, D_EXPERT, D), D_EXPERT ** -0.5),
        'b_down': nrm(ks[28], (L, N_EXPERTS, D), 0.01),
    }

def reference(x, attn_norm, w_in, nsa_q_norm, nsa_k_norm, cmp_k_pe, cmp_k_w1, cmp_k_b1, cmp_k_w2,
              cmp_v_pe, cmp_v_w1, cmp_v_b1, cmp_v_w2, dsa_kv_norm, dsa_w_uk, dsa_w_uv, dsa_q_norm,
              dsa_k_norm, w_branch_a, w_branch_b, w_out, rel_bias, ffn_norm, w_router, b_router,
              w_gate_up, b_gate_up, w_down, b_down):
    for l in range(DEPTH):
        x = hybrid_layer(x, attn_norm[l], w_in[l], nsa_q_norm[l], nsa_k_norm[l], cmp_k_pe[l], cmp_k_w1[l],
                         cmp_k_b1[l], cmp_k_w2[l], cmp_v_pe[l], cmp_v_w1[l], cmp_v_b1[l], cmp_v_w2[l],
                         dsa_kv_norm[l], dsa_w_uk[l], dsa_w_uv[l], dsa_q_norm[l], dsa_k_norm[l],
                         w_branch_a[l], w_branch_b[l], w_out[l], rel_bias, ffn_norm[l], w_router[l],
                         b_router[l], w_gate_up[l], b_gate_up[l], w_down[l], b_down[l])
    return x


_drawn_inputs = setup_inputs


def setup_inputs(seed=0):
    import zlib

    import numpy as np

    out = dict(_drawn_inputs(seed))
    spreads = {}
    factors = {'nsa_q_norm': 4.773,
     'nsa_k_norm': 4.259,
     'cmp_k_pe': 3.171,
     'cmp_k_b1': 8.0,
     'cmp_v_b1': 24.83,
     'dsa_kv_norm': 3.247,
     'dsa_q_norm': 3.641,
     'dsa_k_norm': 6.757,
     'b_gate_up': 8.0,
     'b_down': 21.638,
     'cmp_v_pe': 2.919,
     'b_router': 2.78}
    for name, (base, spread) in spreads.items():
        noise = np.random.default_rng([zlib.crc32(name.encode()), seed]).standard_normal(out[name].shape)
        drawn = base * np.exp(spread * noise) if base else spread * noise
        out[name] = __import__('jax').numpy.asarray(drawn.astype(out[name].dtype))
    for name, factor in factors.items():
        out[name] = (out[name] * factor).astype(out[name].dtype)
    return out
```

```python
import math

import numpy as np

import concourse.bass as bass
from concourse import mybir

F32 = mybir.dt.float32
F32R = mybir.dt.float32r
I32 = mybir.dt.int32
U32 = mybir.dt.uint32
ALU = mybir.AluOpType
ACT = mybir.ActivationFunctionType
AX = mybir.AxisListType

P = 128
S = 512
NT = S // P
D = 1024
DC = D // P
HD = 64
NH = 8
N_CMP = (S - 32) // 16 + 1
N_BUCKETS = 32
MASKED = -1e30
TAKEN = -3e38
KEEP = 128
EPS = 1e-6
NE = 32
TOPK = 4
BLOCK_ROWS = 128
SLOTS = S // BLOCK_ROWS
N_PAIRS = S * TOPK
PAD_PAIR = 4096
KB = 1024


def bias_one_hot():
    m = np.arange(5 * P)
    rel = (S - 1) - m
    n = np.maximum(rel, 0)
    exact = N_BUCKETS // 2
    nf = np.maximum(n, 1).astype(np.float32)
    large = exact + (np.log(nf / np.float32(exact)) / np.float32(math.log(128 / exact))
                     * np.float32(N_BUCKETS - exact)).astype(np.int32)
    bucket = np.where(n < exact, n, np.minimum(large, N_BUCKETS - 1))
    hot = (np.arange(N_BUCKETS + 1)[:, None] == np.where(rel < 0, N_BUCKETS, bucket)[None, :])
    return np.ascontiguousarray(hot.astype(np.float32))


def pre_moe(nc, io, sb, sem, bank, mem):
    ident, flip = mem["ident"], mem["flip"]
    iw = sb("iw", [P, NT, NH], 17)
    gates = sb("gates", [P, NT, NH * 3], 17.125)
    row_ok = sb("row_ok", [P, 1], 17.5)
    stat = sb("stat", [P, 4, 32], 17.75)
    neg_max = sb("neg_max", [P, P], 18.25)
    row_sum = sb("row_sum", [P, P], 18.75)
    coef = sb("coef", [P, P], 19.25)
    top8 = sb("top8", [P, 8], 19.75)
    x_in = sb("x_in", [P, NT, D], 0)
    h_rows = sb("h_rows", [P, NT, D], 188)
    bq_rows = sb("bq_rows", [P, NT * NH, HD], 0)
    aq_rows = sb("aq_rows", [P, NT * NH, HD], 8)
    k_rows = sb("k_rows", [P, NT, 5, HD], 188)
    ckv_rows = sb("ckv_rows", [P, NT, P], 193)
    junk = sb("junk", [P, 2048], 195)
    ckvT = sb("ckvT", [P, S], 203)
    craw = [sb("craw_k", [P, S], 193), sb("craw_v", [P, S], 203)]
    cT = sb("cT", [P, 2, 2, S], 195)
    w1 = sb("w1", [P, 2, 16, P], 0)
    idx_act = [sb(f"idx_act{i}", [P, S], 2 * i) for i in range(2)]
    hT_hi = sb("hT_hi", [P, DC, S], 20, F32R)
    hT_lo = sb("hT_lo", [P, DC, S], 36, F32R)
    w_raw = [sb(f"w_raw{i}", [P, 4, 512], 52 + 8 * i) for i in range(3)]
    w_hi = [sb(f"w_hi{i}", [P, 4, 512], 76 + 8 * i, F32R) for i in range(2)]
    w_lo = [sb(f"w_lo{i}", [P, 4, 512], 92 + 8 * i, F32R) for i in range(2)]
    bias = sb("bias", [P, 2 * NH, S], 108)
    hankel = [sb(f"hankel{i}", [P, 4, S], 140 + 8 * i) for i in range(2)]
    attn_gain = sb("attn_gain", [P, D], 156)
    square = sb("square", [P, D], 160)
    ckv_gain = sb("ckv_gain", [P, P], 164)
    w_ukv = sb("w_ukv", [P, 2 * HD], 164.5)
    tab = sb("tab", [N_BUCKETS + 1, 2 * NH], 165)
    hot = sb("hot", [N_BUCKETS + 1, 5 * P], 181)
    vec = sb("vec", [2 * NH, 5 * P], 183.5)
    aqT = sb("aqT", [P, 4, S], 140)
    bqT = sb("bqT", [P, 4, S], 148)
    kT = sb("kT", [P, 5, S], 156)
    iqT = sb("iqT", [P, 4, S], 166)
    ikT = sb("ikT", [P, S], 174)
    v_sel = sb("v_sel", [P, NT, 2 * HD], 176)
    v_win = sb("v_win", [P, NT, 2 * HD], 178)
    v_dsa = sb("v_dsa", [P, NT, HD], 180)
    score = [None, sb("score1", [P, 2 * P], 181), sb("score2", [P, 3 * P], 182), sb("score3", [P, 4 * P], 183.5)]
    bq_gain = sb("bq_gain", [P, HD], 186)
    aq_gain = sb("aq_gain", [P, HD], 186.25)
    k_gain = sb("k_gain", [P, 5, HD], 186.5)
    kcT = sb("kcT", [P, 2, N_CMP], 205)
    vc = sb("vc", [N_CMP, 2, HD], 205.25)
    hidT = sb("hidT", [P, 2, 2, N_CMP], 205.75)
    kc_rows = sb("kc_rows", [N_CMP, 2, HD], 206.25)
    w2 = sb("w2", [P, 2, HD], 206.75)
    pe = sb("pe", [P, 2, 16], 207.25)
    b1 = sb("b1", [P, 2], 207.375)
    hid_bias = sb("hid_bias", [P, 2], 207.40625)
    logit = [sb(f"logit{i}", [P, S], 166 + 2 * i) for i in range(5)]
    pT = [sb(f"pT{i}", [P, NT, 4, P], 76 + 8 * i) for i in range(2)]
    oT_hi = sb("oT_hi", [P, 8, S], 0, F32R)
    oT_lo = sb("oT_lo", [P, 8, S], 188, F32R)
    sig = sb("sig", [P, 2, NT, 512], 108)
    merged = sb("merged", [P, NT, D], 124)
    mT_hi = sb("mT_hi", [P, DC, S], 140, F32R)
    mT_lo = sb("mT_lo", [P, DC, S], 156, F32R)
    x2 = mem["x2"]

    x_loaded = [sem(f"x_loaded{t}") for t in range(NT)]
    gain_loaded, tab_loaded, small_loaded = sem("gain_loaded"), sem("tab_loaded"), sem("small_loaded")
    w_loaded = [sem(f"w_loaded{i}") for i in range(3)]
    consts_made = mem["consts_made"]
    tab_masked, vec_stored = sem("tab_masked"), sem("vec_stored")
    hankel_loaded = [sem(f"hankel_loaded{i}") for i in range(2)]
    ik_copied, w1_loaded, c_copied = sem("ik_copied"), sem("w1_loaded"), sem("c_copied")
    squared, mean_made, root_made, normed = sem("squared"), sem("mean_made"), sem("root_made"), sem("normed")
    hT_made, hT_lo_out, hT_hi_out = sem("hT_made"), sem("hT_lo_out"), sem("hT_hi_out")
    w_hi_made, w_lo_made = sem("w_hi_made"), sem("w_lo_made")
    proj_step, proj_out = sem("proj_step"), sem("proj_out")
    aux_made, aux_out = sem("aux_made"), sem("aux_out")
    idx_made, idx_relu, idx_added, causal_cut = sem("idx_made"), sem("idx_relu"), sem("idx_added"), sem("causal_cut")
    hid_biased, gains_scaled = sem("hid_biased"), sem("gains_scaled")
    sel_masked = sem("sel_masked")
    s_made, logit_made, exp_made = sem("s_made"), sem("logit_made"), sem("exp_made")
    mask_added, p_scaled = sem("mask_added"), sem("p_scaled")
    even_heads = sem("even_heads")
    pT_made, pT_out = sem("pT_made"), sem("pT_out")
    pv_made, o_hi_out, o_lo_out = sem("pv_made"), sem("o_hi_out"), sem("o_lo_out")
    gate_out, branch_out = sem("gate_out"), sem("branch_out")
    mT_made, mT_hi_out, mT_lo_out = sem("mT_made"), sem("mT_hi_out"), sem("mT_lo_out")
    x_reloaded, x2_made = sem("x_reloaded"), mem["x2_made"]
    dve_step, act_step = mem["dve_step"], mem["act_step"]
    SMALL_LOADS = 14

    w_in = io["w_in"][0].rearrange("(c p) n -> p c n", p=P)
    branch = [io[n][0].rearrange("(c p) n -> p c n", p=P) for n in ("w_branch_a", "w_branch_b")]
    w_out = io["w_out"][0].rearrange("(c p) n -> p c n", p=P)
    CKV, IW, IK = 0, P, P + NH
    GROUPS = [[(CKV, 1816, P), (IW, 2520, NH), (IK, 2456, HD)], [(0, 1944, 512)], [(0, 1304, 512)],
              [(0, 0, 512)], [(0, 512, 512)], [(0, 1024, 280)]]
    G_CKV, G_IQ, G_BQ, G_AQ, G_CS, G_W = range(6)
    units = [[(dst, w_in[:, 4 * half:4 * half + 4, src:src + n]) for dst, src, n in g]
             for g in GROUPS for half in range(2)]
    GATE, BRANCH, OUT = "gate", "branch", "out"
    MERGE = []
    for c in range(2):
        for ab in range(2):
            MERGE.append((GATE, ab, c, [len(units), len(units) + 1]))
            col = 2528 + ab * D + c * 512
            units += [[(0, w_in[:, 4 * half:4 * half + 4, col:col + 512])] for half in range(2)]
        for ab in range(2):
            MERGE.append((BRANCH, ab, c, [len(units)]))
            units += [[(0, branch[ab][:, :, c * 512:c * 512 + 512])]]
    for c in range(2):
        MERGE.append((OUT, 0, c, [len(units), len(units) + 1]))
        units += [[(0, w_out[:, 4 * half:4 * half + 4, c * 512:c * 512 + 512])] for half in range(2)]
    N_UNITS = len(units)
    P1_UNITS = 2 * len(GROUPS)
    NG = len(GROUPS)
    group_units = [[2 * g, 2 * g + 1] for g in range(NG)] + [m[3] for m in MERGE]
    steps_before = [sum(len(v) + 3 for v in group_units[:g]) for g in range(len(group_units) + 1)]

    def bank_made(g, t):
        return steps_before[g] + len(group_units[g]) + t

    def unit_used(u):
        g = next(i for i, v in enumerate(group_units) if u in v)
        return steps_before[g + 1] if u == group_units[g][-1] else steps_before[g] + 1

    def unit_loaded(u):
        return 16 * sum(len(units[v]) for v in range(u % 3, u + 1, 3))

    def unit_width(u):
        return max(dst + src.shape[-1] for dst, src in units[u])

    AUX = ["vec0", "vec1", "ik", "ckvT", "kv"] + [f"bias{h}" for h in range(2 * NH)] \
        + [f"bqT{c}" for c in range(4)] + ["ck", "cv"] + [f"aqT{c}" for c in range(4)] \
        + ["hid", "kcvc"] + [f"kT{j}" for j in range(5)] + ["kcT"]

    def aux(name):
        return bank[:, 6 + AUX.index(name) % 2, :]

    items, batches, groups = [], [], []
    col = 0
    for mixer in ("nsa", "dsa"):
        for qi in range(NT):
            for g4 in range(2):
                g = len(groups)
                first = len(items)
                for kind in (("cmp", "sel", "win") if mixer == "nsa" else ("dsa",)):
                    b = len(batches)
                    n = 1 if kind == "cmp" else 4
                    for h in range(n):
                        width = 4 if kind == "cmp" else 1
                        items.append(dict(kind=kind, qi=qi, g4=g4, h=h, head=4 * g4 + h, batch=b, group=g,
                                          col=col, cols=width, start=h == 0, end=h == n - 1))
                        col += width
                    batches.append(dict(kind=kind, qi=qi, g4=g4, group=g, last=len(items) - 1))
                groups.append(dict(mixer=mixer, qi=qi, g4=g4, last=len(items) - 1,
                                   batches=(batches[-1:] if mixer == "dsa" else batches[-3:])))
    N_ITEMS = len(items)
    NSA_ITEMS = sum(it["kind"] != "dsa" for it in items)
    masks = [n for n, it in enumerate(items) if it["kind"] == "dsa" and it["qi"] > 0]

    def keys(it):
        return 8 * it["qi"] + 7 if it["kind"] == "cmp" else (it["qi"] + 1) * P

    AHEAD = 4
    S_BANKS, PT_BANKS = (0, 1, 2, 5), (3, 4)

    def s_bank(n):
        return bank[:, S_BANKS[n % AHEAD], :]

    def pT_bank(n):
        return bank[:, PT_BANKS[n % 2], :]

    def cview(n):
        it = items[n]
        return logit[n % 5][:, 0:4 * keys(it)].rearrange("p (h k) -> p h k", h=4)

    def sview(n):
        it = items[n]
        return s_bank(n)[:, 0:4 * keys(it)].rearrange("p (h k) -> p h k", h=4)

    def bias_of(it):
        c0 = 384 - it["qi"] * P
        if it["kind"] == "cmp":
            k = keys(it)
            return bias[:, 4 * it["g4"]:4 * it["g4"] + 4, c0 + 31:c0 + 31 + 16 * (k - 1) + 1:16]
        return bias[:, it["head"] + (NH if it["kind"] == "dsa" else 0), c0:S]

    N_RELU = 3 * NH
    ROUNDS = KEEP // 8

    def sync(sp):
        for t in range(NT):
            sp.dma_start(x_in[:, t, :], io["x"][0, t * P:(t + 1) * P, :]).then_inc(x_loaded[t], 16)
            if t == 0:
                sp.dma_start(attn_gain[:], io["attn_norm"][0].partition_broadcast(P)).then_inc(gain_loaded, 16)
        for u in range(N_UNITS):
            if u >= 3:
                sp.wait_ge(w_hi_made, u - 2)
                sp.wait_ge(w_lo_made, u - 2)
            for dst, src in units[u]:
                sp.dma_start(w_raw[u % 3][:, :, dst:dst + src.shape[-1]], src).then_inc(w_loaded[u % 3], 16)
            if u == P1_UNITS + 3:
                sp.wait_ge(o_lo_out, len(groups))
                sp.dma_start(x2[:], io["x"][0].rearrange("(t p) d -> p t d", p=P)).then_inc(x_reloaded, 16)

    def pool(pl):
        pl.memset(ident[:], 1.0).then_inc(consts_made, 1)
        pl.memset(flip[:], 1.0).then_inc(consts_made, 1)
        pl.memset(row_ok[:], 1.0).then_inc(consts_made, 1)
        pl.wait_ge(consts_made, 3)
        pl.affine_select(out=ident[:], in_=ident[:], compare_op=ALU.is_equal, fill=0.0, base=0,
                         pattern=[[-1, P]], channel_multiplier=1).then_inc(consts_made, 1)
        pl.affine_select(out=flip[:], in_=flip[:], compare_op=ALU.is_equal, fill=0.0, base=1 - P,
                         pattern=[[1, P]], channel_multiplier=1).then_inc(consts_made, 1)
        pl.affine_select(out=row_ok[:], in_=row_ok[:], compare_op=ALU.is_ge, fill=0.0, base=-31,
                         pattern=[[0, 1]], channel_multiplier=1).then_inc(consts_made, 1)
        pl.wait_ge(aux_out, AUX.index("vec1") + 1)
        pl.dma_start(io["vec_dram"], vec[:]).then_inc(vec_stored, 16)
        pl.wait_ge(vec_stored, 16)
        for q in range(4):
            if q >= 2:
                pl.wait_ge(aux_made, AUX.index(f"bias{4 * q - 5}") + 1)
            src = bass.AP(io["vec_dram"].tensor, 4 * q * 5 * P, [[1, P], [5 * P, 4], [1, S]])
            pl.dma_start(hankel[q % 2][:], src).then_inc(hankel_loaded[q % 2], 16)
            if q == 1:
                pl.wait_ge(aux_out, AUX.index("ik") + 1)
                pl.dma_start(ikT[HD:P, :], ikT[0:HD, :]).then_inc(ik_copied, 16)
        for qi in range(1, NT):
            pl.wait_ge(idx_added, qi * NH)
            part = score[qi][:, qi * P:(qi + 1) * P]
            pl.affine_select(out=part, in_=part, compare_op=ALU.is_ge, fill=MASKED, base=0,
                             pattern=[[-1, P]], channel_multiplier=1).then_inc(causal_cut, 1)
        pl.wait_ge(aux_made, AUX.index("aqT3") + 1)
        for kv, name in enumerate(("cmp_k_w1", "cmp_v_w1")):
            pl.dma_start(w1[:, kv], io[name][0].rearrange("(c p) h -> p c h", p=P)).then_inc(w1_loaded, 16)
        pl.wait_ge(mean_made, 5)
        for kv in range(2):
            for g in range(2):
                pl.dma_start(cT[0:HD, kv, g, :], craw[kv][g * HD:(g + 1) * HD, :]).then_inc(c_copied, 16)
                pl.dma_start(cT[HD:P, kv, g, 0:S - 1], craw[kv][g * HD:(g + 1) * HD, 1:S]).then_inc(c_copied, 16)
        pl.wait_ge(idx_made, N_RELU)

        def add_mask(n):
            it = items[n]
            pl.wait_ge(sel_masked, it["qi"])
            pl.wait_ge(pT_made, n - 4)
            pl.tensor_tensor(logit[n % 5][:, 0:keys(it)], bias_of(it), score[it["qi"]][:], ALU.add)\
                .then_inc(mask_added, 1)

        for n in masks:
            add_mask(n)

    def tensor(te):
        def mm3(out, a, b, first, last):
            te.matmul(out, a[0], b[0], start=first, stop=False)
            te.matmul(out, a[0], b[1], start=False, stop=False)
            return te.matmul(out, a[1], b[0], start=False, stop=last)

        def transpose(out, a):
            n = a.shape[0]
            return te.matmul(out, a, ident[0:n, 0:n], is_transpose=True, start=True, stop=True)

        def transpose_twice(out, a):
            transpose(out[0:HD], a)
            n = a.shape[0]
            return te.matmul(out[HD:P], a, ident[0:n, 0:n], start=True, stop=True)

        def aux_begin(name):
            n = AUX.index(name)
            if n >= 2:
                te.wait_ge(aux_out, n - 1)
            return aux(name)

        def hT(k, lo, n):
            return hT_hi[:, k, lo:lo + n], hT_lo[:, k, lo:lo + n]

        def wt(u, kk, lo, n):
            return w_hi[u % 2][:, kk, lo:lo + n], w_lo[u % 2][:, kk, lo:lo + n]

        te.wait_ge(tab_loaded, 32)
        te.wait_ge(tab_masked, 1)
        te.matmul(aux_begin("vec0")[0:2 * NH, 0:512], tab[:], hot[:, 0:512], start=True, stop=True).then_inc(aux_made, 1)
        te.matmul(aux_begin("vec1")[0:2 * NH, 0:P], tab[:], hot[:, 512:5 * P], start=True, stop=True).then_inc(aux_made, 1)
        te.wait_ge(consts_made, 6)
        for j in range(8):
            t, half = j // 2, j % 2
            te.wait_ge(normed, t + 1)
            if j >= 4:
                te.wait_ge(hT_lo_out, j - 3)
            for c in range(4):
                last = transpose(bank[:, j % 4, c * P:(c + 1) * P], h_rows[:, t, (4 * half + c) * P:(4 * half + c + 1) * P])
            last.then_inc(hT_made, 1)
        te.wait_ge(hT_lo_out, 8)

        def project(g, u):
            half = u % 2
            te.wait_ge(w_lo_made, u + 1)
            extra = {G_CKV: [("ik", IK, HD)], G_CS: [("ck", 0, P), ("cv", P, P)]}.get(g, [])
            for name, lo, n in extra:
                dst = aux_begin(name) if half == 0 else aux(name)
                for kk in range(4):
                    k = 4 * half + kk
                    m = mm3(dst[0:n, :], wt(u, kk, lo, n), hT(k, 0, S), k == 0, k == 7)
                if half == 1:
                    m.then_inc(aux_made, 1)
            for t in range(4):
                if half == 0 and g > 0:
                    te.wait_ge(proj_out, 4 * (g - 1) + t + 1)
                for kk in range(4):
                    k = 4 * half + kk
                    if g == G_IQ:
                        m = mm3(bank[:, t, :], wt(u, kk, t * P, P), hT(k, 0, S), k == 0, k == 7)
                    else:
                        lo, n = {G_CKV: (0, P + NH), G_BQ: (0, 512), G_AQ: (0, 512), G_CS: (256, 256), G_W: (0, 280)}[g]
                        m = mm3(bank[:, t, 0:n], hT(k, t * P, P), wt(u, kk, lo, n), k == 0, k == 7)
                if half == 1 or t == 3:
                    m.then_inc(proj_step, 1)

        def project_group(g):
            project(g, 2 * g)
            project(g, 2 * g + 1)

        def flip_bias(heads):
            for h in heads:
                dst = aux_begin(f"bias{h}")
                te.wait_ge(hankel_loaded[(h // 4) % 2], 16 * (h // 8 + 1))
                te.matmul(dst, flip[:], hankel[(h // 4) % 2][:, h % 4, :], start=True, stop=True).then_inc(aux_made, 1)

        def transpose_q(name, rows):
            for c in range(4):
                dst = aux_begin(f"{name}{c}")
                for t in range(NT):
                    m = transpose(dst[:, t * P:(t + 1) * P], rows[:, t * NH + 2 * c:t * NH + 2 * c + 2, :].rearrange("p h d -> p (h d)"))
                m.then_inc(aux_made, 1)

        project_group(G_CKV)
        project_group(G_IQ)
        te.wait_ge(normed, NT + 1)
        dst = aux_begin("ckvT")
        for t in range(NT):
            m = transpose(dst[:, t * P:(t + 1) * P], ckv_rows[:, t, :])
        m.then_inc(aux_made, 1)
        dst = aux_begin("kv")
        te.wait_ge(small_loaded, SMALL_LOADS * 16)
        te.wait_ge(aux_out, AUX.index("ckvT") + 1)
        for t in range(NT):
            m = te.matmul(dst[:, t * P:(t + 1) * P], ckvT[:, t * P:(t + 1) * P], w_ukv[:], start=True, stop=True)
        m.then_inc(aux_made, 1)
        flip_bias(range(0, 8))
        project_group(G_BQ)
        flip_bias(range(8, 16))
        project_group(G_AQ)
        te.wait_ge(normed, NT + 2)
        transpose_q("bqT", bq_rows)
        te.wait_ge(proj_out, 8)
        te.wait_ge(ik_copied, 16)
        for n in range(N_RELU):
            qi, h = n // NH + 1, n % NH
            if n >= 2:
                te.wait_ge(idx_relu, n - 1)
            half = slice((h % 2) * HD, (h % 2) * HD + HD)
            te.matmul(bank[:, 4 + n % 2, 0:(qi + 1) * P], iqT[half, h // 2, qi * P:(qi + 1) * P],
                      ikT[half, 0:(qi + 1) * P], start=True, stop=True).then_inc(idx_made, 1)
        project_group(G_CS)
        te.wait_ge(normed, NT + 3)
        transpose_q("aqT", aq_rows)
        project_group(G_W)
        te.wait_ge(w1_loaded, 32)
        te.wait_ge(c_copied, 8 * 16)
        dst = aux_begin("hid")
        for kv in range(2):
            for c in range(16):
                te.matmul(dst[:, 128 + kv:129 + kv], w1[:, kv, c, :], pe[:, kv, c:c + 1], start=c == 0, stop=c == 15)
            for c in range(16):
                m = te.matmul(dst[:, 62 * kv:62 * kv + 62].rearrange("p (g j) -> p g j", g=2), w1[:, kv, c, :],
                              cT[:, kv, :, 2 * c:2 * c + 16 * (N_CMP - 1) + 1:16], start=c == 0, stop=c == 15)
        m.then_inc(aux_made, 1)
        dst = aux_begin("kcvc")
        te.wait_ge(aux_out, AUX.index("hid") + 1)
        for kv in range(2):
            for g in range(2):
                m = te.matmul(dst[0:N_CMP, (2 * kv + g) * HD:(2 * kv + g + 1) * HD], hidT[:, kv, g, :], w2[:, kv, :],
                              start=True, stop=True)
        m.then_inc(aux_made, 1)
        te.wait_ge(normed, NT + 4)
        for j in range(5):
            dst = aux_begin(f"kT{j}")
            for t in range(NT):
                m = transpose_twice(dst[:, t * P:(t + 1) * P], k_rows[:, t, j, :])
            m.then_inc(aux_made, 1)
        dst = aux_begin("kcT")
        te.wait_ge(normed, NT + 5)
        for g in range(2):
            m = transpose_twice(dst[:, g * 32:g * 32 + N_CMP], kc_rows[:, g, :])
        m.then_inc(aux_made, 1)

        te.wait_ge(aux_out, len(AUX))
        te.wait_ge(proj_out, 4 * NG)
        te.wait_ge(idx_relu, N_RELU)

        def scores(n):
            it = items[n]
            if n >= AHEAD:
                te.wait_ge(logit_made, n - AHEAD + 1)
            q0 = it["qi"] * P
            for h in ((0, 2, 1, 3) if it["kind"] == "cmp" else [it["h"]]):
                if it["kind"] == "cmp" and h == 1:
                    te.wait_ge(even_heads, it["group"] + 1)
                head = 4 * it["g4"] + h
                half = slice((head % 2) * HD, (head % 2) * HD + HD)
                q = (bqT if it["kind"] == "dsa" else aqT)[half, head // 2, q0:q0 + P]
                if it["kind"] == "cmp":
                    m = te.matmul(sview(n)[:, h, :], q, kcT[half, it["g4"], 0:keys(it)], start=True, stop=True)
                    if h == 2:
                        m.then_inc(even_heads, 1)
                else:
                    j = {"sel": it["g4"], "win": 2 + it["g4"], "dsa": 4}[it["kind"]]
                    m = te.matmul(s_bank(n)[:, 0:keys(it)], q, kT[half, j, 0:keys(it)], start=True, stop=True)
            m.then_inc(s_made, 1)

        def transposes(n):
            it = items[n]
            te.wait_ge(p_scaled, n + 1)
            if n >= 2:
                te.wait_ge(pT_out, n - 1)
            b = pT_bank(n)
            if it["kind"] == "cmp":
                for h in range(4):
                    m = transpose(b[0:keys(it), h * P:(h + 1) * P], cview(n)[:, h, :])
            else:
                for kb in range(it["qi"] + 1):
                    m = transpose(b[:, kb * P:(kb + 1) * P], logit[n % 5][:, kb * P:(kb + 1) * P])
            m.then_inc(pT_made, 1)

        def weigh_values(b):
            ba = batches[b]
            gr = groups[ba["group"]]
            if ba["kind"] in ("cmp", "dsa") and ba["group"] >= 2:
                te.wait_ge(o_lo_out, ba["group"] - 1)
            te.wait_ge(pT_out, ba["last"] + 1)
            dst = bank[:, 6 + ba["group"] % 2, 0:2 * P]
            only = ba["kind"] == "dsa"
            n_kb = 1 if ba["kind"] == "cmp" else ba["qi"] + 1
            for kb in range(n_kb):
                for half in range(2):
                    g = slice(ba["g4"] * HD, ba["g4"] * HD + HD)
                    if ba["kind"] == "cmp":
                        nk = keys(ba)
                        v, p = vc[0:nk, ba["g4"], :], pT[b % 2][0:nk, 0, half:4:2, :]
                    else:
                        v = {"sel": v_sel[:, kb, g], "win": v_win[:, kb, g], "dsa": v_dsa[:, kb, :]}[ba["kind"]]
                        p = pT[b % 2][:, kb, half:4:2, :]
                    m = te.matmul(dst[half * HD:(half + 1) * HD, :].rearrange("p (h q) -> p h q", h=2), v, p,
                                  start=kb == 0 and ba["kind"] in ("cmp", "dsa"),
                                  stop=kb == n_kb - 1 and ba["kind"] in ("win", "dsa"))
            m.then_inc(pv_made, 1)

        for n in range(AHEAD):
            scores(n)
        for n in range(N_ITEMS + 1):
            if n < N_ITEMS:
                transposes(n)
            if n + AHEAD < N_ITEMS:
                scores(n + AHEAD)
            if n >= 1 and items[n - 1]["end"]:
                weigh_values(items[n - 1]["batch"])

        def merge_group(m_):
            kind, ab, c, us = MERGE[m_]
            g = NG + m_
            first_bank = 4 * (m_ % 2)
            if m_ >= 2:
                k2, _, c2, _ = MERGE[m_ - 2]
                te.wait_ge(*((gate_out, 4 * (2 * c2 + m_ % 2 + 1)) if k2 == GATE else (branch_out, 4 * (2 * c2 + m_ % 2 + 1))))
            for i, u in enumerate(us):
                te.wait_ge(w_lo_made, u + 1)
                for t in range(NT):
                    dst = bank[:, first_bank + t, :]
                    for kk in range(4):
                        first, last = i == 0 and kk == 0, u == us[-1] and kk == 3
                        if kind == GATE:
                            a = hT(4 * i + kk, t * P, P)
                        elif kind == BRANCH:
                            a = (oT_hi[:, 4 * ab + kk, t * P:(t + 1) * P], oT_lo[:, 4 * ab + kk, t * P:(t + 1) * P])
                        else:
                            a = (mT_hi[:, 4 * i + kk, t * P:(t + 1) * P], mT_lo[:, 4 * i + kk, t * P:(t + 1) * P])
                        m = mm3(dst, a, wt(u, kk, 0, 512), first, last)
                    if u == us[-1] or t == 3:
                        m.then_inc(proj_step, 1)

        te.wait_ge(o_lo_out, len(groups))
        for m_ in range(8):
            merge_group(m_)
        te.wait_ge(branch_out, 16)
        for j in range(8):
            t, half = j // 2, j % 2
            if j >= 4:
                te.wait_ge(mT_lo_out, j - 3)
            for c in range(4):
                m = transpose(bank[:, j % 4, c * P:(c + 1) * P], merged[:, t, (4 * half + c) * P:(4 * half + c + 1) * P])
            m.then_inc(mT_made, 1)
        te.wait_ge(mT_lo_out, 8)
        merge_group(8)
        merge_group(9)
        mem["transpose"] = transpose

    def scalar(ac):
        smalls = [
            (bq_gain[:], io["dsa_q_norm"][0].partition_broadcast(P)),
            (aq_gain[:], io["nsa_q_norm"][0].partition_broadcast(P)),
            (ckv_gain[:], io["dsa_kv_norm"][0].partition_broadcast(P)),
            (w_ukv[:, 0:HD], io["dsa_w_uk"][0]), (w_ukv[:, HD:2 * HD], io["dsa_w_uv"][0]),
            (w2[:, 0, :], io["cmp_k_w2"][0]), (w2[:, 1, :], io["cmp_v_w2"][0]),
            (pe[:], io["pe_cols"]), (b1[:], io["b1_cols"]),
            (k_gain[:, 4, :], io["dsa_k_norm"][0].partition_broadcast(P)),
        ] + [(k_gain[:, j, :], io["nsa_k_norm"][0].partition_broadcast(P)) for j in range(4)]
        assert len(smalls) == SMALL_LOADS
        ac.dma_start(tab[0:N_BUCKETS, :], io["rel_bias"]).then_inc(tab_loaded, 16)
        ac.dma_start(hot[:], io["bias_hot"]).then_inc(tab_loaded, 16)
        for dst, src in smalls:
            ac.dma_start(dst, src).then_inc(small_loaded, 16)

        def aux_copy(name, dst, src, func=ACT.Copy, inc=True, **kw):
            ac.wait_ge(aux_made, AUX.index(name) + 1)
            i = ac.activation(dst, src, func, **kw)
            if inc:
                i.then_inc(aux_out, 1)

        def root(n, cols, rows=P):
            ac.wait_ge(mean_made, n + 1)
            ac.activation(stat[0:rows, 2, 0:cols], stat[0:rows, 1, 0:cols], ACT.Sqrt).then_inc(root_made, 1)

        def split_unit(u):
            n = unit_width(u)
            ac.wait_ge(w_loaded[u % 3], unit_loaded(u))
            if u >= 2:
                ac.wait_ge(proj_step, unit_used(u - 2))
            ac.activation(w_hi[u % 2][:, :, 0:n], w_raw[u % 3][:, :, 0:n], ACT.Copy).then_inc(w_hi_made, 1)

        for t in range(NT):
            ac.wait_ge(x_loaded[t], 16)
            if t >= 1:
                ac.wait_ge(squared, t)
            ac.activation(square[:], x_in[:, t, :], ACT.Square, accum_out=stat[:, 0, t:t + 1]).then_inc(squared, 1)
        root(0, NT)
        aux_copy("vec0", vec[:, 0:512], aux("vec0")[0:2 * NH, 0:512])
        aux_copy("vec1", vec[:, 512:5 * P], aux("vec1")[0:2 * NH, 0:P])
        split_unit(0)
        for j in range(8):
            t, half = j // 2, j % 2
            ac.wait_ge(hT_made, j + 1)
            ac.activation(hT_hi[:, 4 * half:4 * half + 4, t * P:(t + 1) * P],
                          bank[:, j % 4, :].rearrange("p (c q) -> p c q", c=4), ACT.Copy).then_inc(hT_hi_out, 1)
        split_unit(1)

        def wait_bank(g, t):
            ac.wait_ge(proj_step, bank_made(g, t))

        def square_rows(rows):
            ac.activation(junk[:, 0:rows.shape[1] * rows.shape[2]].rearrange("p (a b) -> p a b", a=rows.shape[1]),
                          rows, ACT.Square).then_inc(squared, 1)

        for g in range(NG):
            if g + 1 < NG:
                split_unit(2 * g + 2)
                split_unit(2 * g + 3)
            for t in range(NT):
                wait_bank(g, t)
                b = bank[:, t, :]
                if g == G_CKV:
                    if t == 0:
                        ac.wait_ge(hT_lo_out, 8)
                    ac.activation(ckv_rows[:, t, :], b[:, 0:P], ACT.Copy).then_inc(act_step, 1)
                    ac.activation(iw[:, t, :], b[:, P:P + NH], ACT.Copy, scale=NH ** -0.5).then_inc(proj_out, 1)
                elif g == G_IQ:
                    ac.activation(iqT[:, t, :], b, ACT.Copy).then_inc(proj_out, 1)
                elif g in (G_BQ, G_AQ):
                    rows = bq_rows if g == G_BQ else aq_rows
                    ac.activation(rows[:, t * NH:(t + 1) * NH, :], b.rearrange("p (h d) -> p h d", h=NH), ACT.Copy).then_inc(proj_out, 1)
                elif g == G_CS:
                    ac.activation(k_rows[:, t, 0:2, :], b[:, 0:P].rearrange("p (h d) -> p h d", h=2), ACT.Copy).then_inc(act_step, 1)
                    ac.activation(v_sel[:, t, :], b[:, P:2 * P], ACT.Copy).then_inc(proj_out, 1)
                else:
                    ac.activation(k_rows[:, t, 2:4, :], b[:, 0:P].rearrange("p (h d) -> p h d", h=2), ACT.Copy).then_inc(act_step, 1)
                    ac.activation(v_win[:, t, :], b[:, P:2 * P], ACT.Copy).then_inc(act_step, 1)
                    ac.activation(gates[:, t, :], b[:, 2 * P:2 * P + 3 * NH], ACT.Sigmoid).then_inc(proj_out, 1)
            if g == G_CKV:
                ac.wait_ge(act_step, 4)
                square_rows(ckv_rows[:])
                root(1, NT)
                aux_copy("ik", ikT[0:HD, :], aux("ik")[0:HD, :])
            elif g == G_IQ:
                aux_copy("ckvT", ckvT[:], aux("ckvT"))
                v = aux("kv").rearrange("p (t n) -> p t n", t=NT)
                aux_copy("kv", k_rows[:, :, 4, :], v[:, :, 0:HD], inc=False)
                aux_copy("kv", v_dsa[:], v[:, :, HD:2 * HD])
                for h in range(8):
                    aux_copy(f"bias{h}", bias[:, h, :], aux(f"bias{h}"))
            elif g == G_BQ:
                ac.wait_ge(proj_out, 12)
                square_rows(bq_rows[:])
                root(2, NT * NH)
                for h in range(8, 16):
                    aux_copy(f"bias{h}", bias[:, h, :], aux(f"bias{h}"))
            elif g == G_AQ:
                ac.wait_ge(proj_out, 16)
                square_rows(aq_rows[:])
                root(3, NT * NH)
                for c in range(4):
                    aux_copy(f"bqT{c}", bqT[:, c, :], aux(f"bqT{c}"))
                ac.wait_ge(aux_made, AUX.index("bqT3") + 1)
                for n in range(N_RELU):
                    w = (n // NH + 2) * P
                    ac.wait_ge(idx_made, n + 1)
                    if n >= 2:
                        ac.wait_ge(idx_added, n - 1)
                    ac.activation(idx_act[n % 2][:, 0:w], bank[:, 4 + n % 2, 0:w], ACT.Relu, scale=HD ** -0.5).then_inc(idx_relu, 1)
            elif g == G_CS:
                ac.wait_ge(mean_made, 4)
                aux_copy("ck", craw[0][:], aux("ck"))
                aux_copy("cv", craw[1][:], aux("cv"))
                for c in range(4):
                    aux_copy(f"aqT{c}", aqT[:, c, :], aux(f"aqT{c}"))
        ac.wait_ge(act_step, 4 + 4 + 8)
        ac.wait_ge(proj_out, 24)
        square_rows(k_rows[:].rearrange("p t j d -> p (t j) d"))
        root(4, NT * 5)
        for kv in range(2):
            ac.wait_ge(aux_made, AUX.index("hid") + 1)
            ac.wait_ge(hid_biased, 1)
            i = ac.activation(hidT[:, kv].rearrange("p g j -> p (g j)"), aux("hid")[:, 62 * kv:62 * kv + 62],
                              ACT.Gelu_apprx_tanh, bias=hid_bias[:, kv:kv + 1])
        i.then_inc(aux_out, 1)
        v = aux("kcvc")[0:N_CMP, 0:2 * P].rearrange("p (a d) -> p a d", a=4)
        aux_copy("kcvc", kc_rows[:], v[:, 0:2, :], inc=False)
        aux_copy("kcvc", vc[:], v[:, 2:4, :])
        ac.wait_ge(aux_out, AUX.index("kcvc") + 1)
        ac.wait_ge(mean_made, 5)
        ac.activation(junk[0:N_CMP, 0:P].rearrange("p (a b) -> p a b", a=2), kc_rows[:], ACT.Square).then_inc(squared, 1)
        root(5, 2, N_CMP)
        for j in range(5):
            aux_copy(f"kT{j}", kT[:, j, :], aux(f"kT{j}"))
        aux_copy("kcT", kcT[:], aux("kcT")[:, 0:64].rearrange("p (g j) -> p g j", g=2)[:, :, 0:N_CMP])

        def move_pT(n):
            it = items[n]
            ac.wait_ge(pT_made, n + 1)
            if it["start"] and it["batch"] >= 2:
                ac.wait_ge(pv_made, it["batch"] - 1)
            if it["kind"] == "cmp":
                dst, src = pT[it["batch"] % 2][0:keys(it), 0, :, :], pT_bank(n)[0:keys(it), :].rearrange("p (h q) -> p h q", h=4)
            else:
                n_kb = it["qi"] + 1
                dst = pT[it["batch"] % 2][:, 0:n_kb, it["h"], :]
                src = pT_bank(n)[:, 0:n_kb * P].rearrange("p (k q) -> p k q", k=n_kb)
            ac.activation(dst, src, ACT.Copy).then_inc(pT_out, 1)

        for n in range(N_ITEMS + 5):
            if n < N_ITEMS:
                it = items[n]
                ac.wait_ge(logit_made, n + 1)
                if it["kind"] == "cmp":
                    ac.activation(cview(n), cview(n), ACT.Exp).then_inc(exp_made, 1)
                else:
                    v = logit[n % 5][:, 0:keys(it)]
                    c = it["col"]
                    ac.activation(v, v, ACT.Exp, bias=neg_max[:, c:c + 1], scale=-1.0,
                                  accum_out=row_sum[:, c:c + 1]).then_inc(exp_made, 1)
            if 2 <= n < N_ITEMS + 2:
                move_pT(n - 2)
            if n >= 4:
                for g, gr in enumerate(groups):
                    if gr["last"] == n - 4:
                        ac.wait_ge(pv_made, sum(1 for b in batches if b["group"] <= g))
                        ac.activation(*o_view(oT_hi, g), ACT.Copy).then_inc(o_hi_out, 1)

        for m_, (kind, ab, c, us) in enumerate(MERGE):
            if m_ == 0:
                split_unit(us[0])
                split_unit(us[1])
            nxt = MERGE[m_ + 1][3] if m_ + 1 < len(MERGE) else []
            for u in nxt:
                split_unit(u)
            if kind == GATE:
                for t in range(NT):
                    wait_bank(NG + m_, t)
                    if c == 1 and t == 0:
                        ac.wait_ge(branch_out, 4 * (ab + 1))
                    ac.activation(sig[:, ab, t, :], bank[:, 4 * (m_ % 2) + t, :], ACT.Sigmoid).then_inc(gate_out, 1)
            if m_ == 7:
                for j in range(8):
                    t, half = j // 2, j % 2
                    ac.wait_ge(mT_made, j + 1)
                    ac.activation(mT_hi[:, 4 * half:4 * half + 4, t * P:(t + 1) * P],
                                  bank[:, j % 4, :].rearrange("p (c q) -> p c q", c=4), ACT.Copy).then_inc(mT_hi_out, 1)

    def o_view(dst, g):
        gr = groups[g]
        c0 = (0 if gr["mixer"] == "nsa" else 4) + 2 * gr["g4"]
        return (dst[:, c0:c0 + 2, gr["qi"] * P:(gr["qi"] + 1) * P],
                bank[:, 6 + g % 2, 0:2 * P].rearrange("p (h q) -> p h q", h=2))

    def vector(ve):
        count = [0]

        def step(instruction):
            count[0] += 1
            instruction.then_inc(dve_step, 1)
            ve.wait_ge(dve_step, count[0])

        def mean(n, cols, width, rows=P):
            ve.tensor_scalar(stat[0:rows, 1, 0:cols], stat[0:rows, 0, 0:cols], 1.0 / width, EPS, ALU.mult, ALU.add)                .then_inc(mean_made, 1)

        def inverse(n, cols, rows=P):
            ve.wait_ge(root_made, n + 1)
            step(ve.reciprocal(stat[0:rows, 3, 0:cols], stat[0:rows, 2, 0:cols]))

        def norm_rows(n, rows, gain, sq=None, parts=P):
            _, a, b = rows.shape
            sq = junk[:, 0:a * b].rearrange("p (a b) -> p a b", a=a) if sq is None else sq
            ve.wait_ge(squared, NT - 1 + n + 1)
            step(ve.reduce_sum(stat[0:parts, 0, 0:a], sq, axis=AX.X))
            mean(n, a, b, parts)
            inverse(n, a, parts)
            step(ve.tensor_tensor(rows, rows, stat[0:parts, 3, 0:a].unsqueeze(2).to_broadcast([parts, a, b]), ALU.mult))
            ve.tensor_tensor(rows, rows, gain, ALU.mult).then_inc(normed, 1)

        def split_unit(u):
            n = unit_width(u)
            ve.wait_ge(w_hi_made, u + 1)
            ve.tensor_tensor(w_lo[u % 2][:, :, 0:n], w_raw[u % 3][:, :, 0:n], w_hi[u % 2][:, :, 0:n].bitcast(F32),
                             ALU.subtract).then_inc(w_lo_made, 1)

        ve.memset(tab[N_BUCKETS:N_BUCKETS + 1, :], MASKED).then_inc(tab_masked, 1)
        ve.wait_ge(squared, NT)
        mean(0, NT, D)
        inverse(0, NT)
        ve.wait_ge(gain_loaded, 16)
        for t in range(NT):
            ve.scalar_tensor_tensor(h_rows[:, t, :], x_in[:, t, :], stat[:, 3, t:t + 1], attn_gain[:], ALU.mult, ALU.mult)                .then_inc(normed, 1)
        ve.wait_ge(small_loaded, 16 * SMALL_LOADS)
        ve.tensor_scalar(bq_gain[:], bq_gain[:], HD ** -0.5, None, ALU.mult).then_inc(gains_scaled, 1)
        ve.tensor_scalar(aq_gain[:], aq_gain[:], HD ** -0.5, None, ALU.mult).then_inc(gains_scaled, 1)
        split_unit(0)
        for j in range(8):
            t, half = j // 2, j % 2
            ve.wait_ge(hT_hi_out, j + 1)
            v = (slice(None), slice(4 * half, 4 * half + 4), slice(t * P, (t + 1) * P))
            ve.tensor_tensor(hT_lo[v], bank[:, j % 4, :].rearrange("p (c q) -> p c q", c=4), hT_hi[v].bitcast(F32),
                             ALU.subtract).then_inc(hT_lo_out, 1)
        split_unit(1)
        split_unit(2)
        split_unit(3)
        norm_rows(1, ckv_rows[:], ckv_gain[:].unsqueeze(1).to_broadcast([P, NT, P]))
        split_unit(4)
        split_unit(5)
        split_unit(6)
        split_unit(7)
        ve.wait_ge(gains_scaled, 2)
        norm_rows(2, bq_rows[:], bq_gain[:].unsqueeze(1).to_broadcast([P, NT * NH, HD]))
        split_unit(8)
        split_unit(9)
        norm_rows(3, aq_rows[:], aq_gain[:].unsqueeze(1).to_broadcast([P, NT * NH, HD]))
        for n in range(N_RELU):
            qi, h = n // NH + 1, n % NH
            w = (qi + 1) * P
            ve.wait_ge(idx_relu, n + 1)
            if h == 0:
                if qi == 1:
                    ve.wait_ge(aux_made, AUX.index("bias15") + 1)
                ve.tensor_scalar(score[qi][:], idx_act[n % 2][:, 0:w], iw[:, qi, h:h + 1], None, ALU.mult).then_inc(idx_added, 1)
            else:
                ve.wait_ge(idx_added, n)
                ve.scalar_tensor_tensor(score[qi][:], idx_act[n % 2][:, 0:w], iw[:, qi, h:h + 1], score[qi][:],
                                        ALU.mult, ALU.add).then_inc(idx_added, 1)
        split_unit(10)
        split_unit(11)
        k_flat = k_rows[:].rearrange("p t j d -> p (t j) d")
        ve.wait_ge(squared, NT + 4)
        step(ve.reduce_sum(stat[:, 0, 0:5 * NT], junk[:, 0:5 * NT * HD].rearrange("p (a b) -> p a b", b=HD), axis=AX.X))
        mean(4, 5 * NT, HD)
        inverse(4, 5 * NT)
        step(ve.tensor_tensor(k_flat, k_flat, stat[:, 3, 0:5 * NT].unsqueeze(2).to_broadcast([P, 5 * NT, HD]), ALU.mult))
        ve.tensor_tensor(k_rows[:], k_rows[:], k_gain[:].unsqueeze(1).to_broadcast([P, NT, 5, HD]), ALU.mult).then_inc(normed, 1)
        ve.wait_ge(aux_made, AUX.index("hid") + 1)
        ve.tensor_tensor(hid_bias[:], aux("hid")[:, P:P + 2], b1[:], ALU.add).then_inc(hid_biased, 1)
        norm_rows(5, kc_rows[:], k_gain[0:N_CMP, 0:2, :], sq=junk[0:N_CMP, 0:P].rearrange("p (a b) -> p a b", a=2), parts=N_CMP)

        def top8_of(r):
            if r % ROUNDS == 0:
                ve.wait_ge(causal_cut, r // ROUNDS + 1)
            step(ve.max(top8[:], score[r // ROUNDS + 1][:]))

        def take_top8(r):
            sc = score[r // ROUNDS + 1][:]
            step(ve.match_replace(sc, top8[:], sc, TAKEN))
            if r % ROUNDS == ROUNDS - 1:
                ve.tensor_scalar(sc, sc, TAKEN / 2, MASKED, ALU.is_gt, ALU.mult).then_inc(sel_masked, 1)

        def make_logit(n):
            it = items[n]
            w = keys(it)
            if n in masks:
                ve.wait_ge(mask_added, masks.index(n) + 1)
            elif n >= 5:
                ve.wait_ge(pT_made, n - 4)
            ve.wait_ge(s_made, n + 1)
            c = it["col"]
            if it["kind"] == "cmp":
                step(ve.tensor_tensor(cview(n), sview(n), bias_of(it), ALU.add))
                step(ve.reduce_max(neg_max[:, c:c + 4], cview(n), axis=AX.X))
                ve.tensor_tensor(cview(n), cview(n), neg_max[:, c:c + 4].unsqueeze(2).to_broadcast([P, 4, w]), ALU.subtract)\
                    .then_inc(logit_made, 1)
            else:
                add = logit[n % 5][:, 0:w] if n in masks else bias_of(it)
                ve.tensor_tensor_reduce(out=logit[n % 5][:, 0:w], in0=s_bank(n)[:, 0:w], in1=add, scale=-1.0,
                                        scalar=-TAKEN, op0=ALU.add, op1=ALU.min, accum_out=neg_max[:, c:c + 1])\
                    .then_inc(logit_made, 1)

        def scale_p(n):
            it = items[n]
            c, w = it["col"], it["cols"]
            ve.wait_ge(exp_made, n + 1)
            co = coef[:, c:c + w]
            if it["kind"] == "cmp":
                step(ve.reduce_sum(row_sum[:, c:c + 4], cview(n), axis=AX.X))
            step(ve.reciprocal(co, row_sum[:, c:c + w]))
            if it["kind"] == "cmp":
                h0 = 12 * it["g4"]
                step(ve.tensor_tensor(co, co, gates[:, it["qi"], h0:h0 + 10:3], ALU.mult))
                if it["qi"] == 0:
                    step(ve.tensor_scalar(co, co, row_ok[:], None, ALU.mult))
                ve.tensor_tensor(cview(n), cview(n), co.unsqueeze(2).to_broadcast([P, 4, keys(it)]), ALU.mult)\
                    .then_inc(p_scaled, 1)
            else:
                v = logit[n % 5][:, 0:keys(it)]
                g = 3 * it["head"] + {"sel": 1, "win": 2}.get(it["kind"], 0)
                gate = gates[:, it["qi"], g:g + 1]
                if it["kind"] == "dsa":
                    ve.tensor_scalar(v, v, co, None, ALU.mult).then_inc(p_scaled, 1)
                else:
                    ve.tensor_scalar(v, v, co, gate, ALU.mult, ALU.mult).then_inc(p_scaled, 1)

        ve.wait_ge(idx_made, N_RELU)
        ve.wait_ge(proj_out, 4 * NG)
        ve.wait_ge(aux_out, len(AUX))
        for n in range(N_ITEMS + 5):
            if n < 3 * ROUNDS:
                top8_of(n)
            if n < N_ITEMS:
                make_logit(n)
            if n < 3 * ROUNDS:
                take_top8(n)
            if 1 <= n <= N_ITEMS:
                scale_p(n - 1)
            if n >= 4:
                for g, gr in enumerate(groups):
                    if gr["last"] == n - 4:
                        ve.wait_ge(o_hi_out, g + 1)
                        dst, src = o_view(oT_lo, g)
                        ve.tensor_tensor(dst, src, o_view(oT_hi, g)[0].bitcast(F32), ALU.subtract).then_inc(o_lo_out, 1)

        for m_, (kind, ab, c, us) in enumerate(MERGE):
            if m_ == 0:
                split_unit(us[0])
                split_unit(us[1])
            for u in (MERGE[m_ + 1][3] if m_ + 1 < len(MERGE) else []):
                split_unit(u)
            cols = slice(c * 512, c * 512 + 512)
            for t in range(NT):
                src = bank[:, 4 * (m_ % 2) + t, :]
                if kind == BRANCH:
                    ve.wait_ge(gate_out, 4 * (2 * c + ab) + t + 1)
                    ve.wait_ge(proj_step, bank_made(NG + m_, t))
                    if ab == 0:
                        ve.tensor_tensor(merged[:, t, cols], src, sig[:, 0, t, :], ALU.mult).then_inc(branch_out, 1)
                    else:
                        step(ve.tensor_tensor(sig[:, 1, t, :], src, sig[:, 1, t, :], ALU.mult))
                        ve.tensor_tensor(merged[:, t, cols], merged[:, t, cols], sig[:, 1, t, :], ALU.add).then_inc(branch_out, 1)
                elif kind == OUT:
                    ve.wait_ge(x_reloaded, 16)
                    ve.wait_ge(proj_step, bank_made(NG + m_, t))
                    ve.tensor_tensor(x2[:, t, cols], src, x2[:, t, cols], ALU.add).then_inc(x2_made, 1)
            if m_ == 7:
                for j in range(8):
                    t, half = j // 2, j % 2
                    ve.wait_ge(mT_hi_out, j + 1)
                    v = (slice(None), slice(4 * half, 4 * half + 4), slice(t * P, (t + 1) * P))
                    ve.tensor_tensor(mT_lo[v], bank[:, j % 4, :].rearrange("p (c q) -> p c q", c=4), mT_hi[v].bitcast(F32),
                                     ALU.subtract).then_inc(mT_lo_out, 1)
        mem["dve_count"] = count
        mem["step"] = step

    mem.update(proj_step=proj_step, mT_lo_out=mT_lo_out, w_lo_made=w_lo_made, n_units=N_UNITS,
               after_branches=steps_before[NG + 8], after_out=steps_before[NG + 10])
    return dict(sync=sync, pool=pool, tensor=tensor, scalar=scalar, vector=vector)


def moe(nc, io, out, sb, sem, bank, mem):
    ident, x2 = mem["ident"], mem["x2"]
    dve_step = mem["dve_step"]
    tri = sb("tri", [P, P], 0)
    ones = sb("ones", [P, P], 0.5)
    pairT = sb("pairT", [P, P], 1, I32)
    tokT = sb("tokT", [P, P], 1.5, I32)
    gateT = sb("gateT", [P, P], 2)
    hot64 = sb("hot64", [2 * NE, NE], 2.5)
    table_sb = sb("table_sb", [P, P, 2], 2.75)
    b_raw = sb("b_raw", [2 * NE, 3 * D], 4)
    b_parts = sb("b_parts", [2 * NE, 3 * D], 188, F32R)
    ffn_gain = sb("ffn_gain", [P, D], 124)
    square = sb("ffn_square", [P, D], 128)
    h2 = sb("h2", [P, NT, D], 140)
    h2T = sb("h2T", [P, DC, S], 156)
    w_router = sb("w_router_sb", [P, DC, NE], 132)
    b_router = sb("b_router_sb", [P, NE], 133)
    fstat = sb("fstat", [P, 4, NT], 133.25)
    onehot = sb("onehot", [P, NT, TOPK, NE], 200)
    picked = sb("picked", [P, NT, TOPK, NE], 202)
    logits = sb("logits", [P, NT, NE], 204)
    chosen = sb("chosen", [P, NT, NE], 204.5)
    place = sb("place", [P, NT, NE], 205)
    top_val = sb("top_val", [P, NT, 8], 205.5)
    top_idx = sb("top_idx", [P, NT, 8], 205.75, U32)
    top_f = sb("top_f", [P, NT, TOPK], 206)
    gate = sb("gate", [P, NT, TOPK], 206.125)
    gate_sum = sb("gate_sum", [P, NT], 206.25)
    dest_f = sb("dest_f", [P, NT * TOPK], 206.375)
    dest = sb("dest", [P, NT * TOPK], 206.5, I32)
    payload = sb("payload", [P, NT, TOPK, 2], 206.625)
    iota_e = sb("iota_e", [P, NE], 206.875)
    iota_i = sb("iota_i", [P, NE], 207, I32)
    iota_slot = sb("iota_slot", [P, NE], 207.25)
    busiest_f = sb("busiest_f", [P, 1], 3.75)
    busiest = sb("busiest", [P, 1], 3.78125, I32)
    pad = sb("pad", [P, 2 * P], 136)
    pair_i = sb("pair_i", [P, NT, TOPK], 137, I32)
    RAW, SPLIT = 6, 4
    raw = [sb(f"raw{i}", [P, 2048], 20 + 8 * i) for i in range(RAW)]
    hi = [sb(f"hi{i}", [P, 2048], 68 + 8 * i, F32R) for i in range(SPLIT)]
    lo = [sb(f"lo{i}", [P, 2048], 100 + 8 * i, F32R) for i in range(SPLIT)]
    xg = [sb(f"xg{i}", [P, D], 132 + 4 * i) for i in range(2)]
    xT_hi = [sb(f"xT_hi{i}", [P, DC, P], 140 + 4 * i, F32R) for i in range(2)]
    xT_lo = [sb(f"xT_lo{i}", [P, DC, P], 148 + 4 * i, F32R) for i in range(2)]
    aT_hi = sb("aT_hi", [P, DC, P], 156, F32R)
    aT_lo = sb("aT_lo", [P, DC, P], 160, F32R)
    sg = sb("sg", [P, D], 164)
    lin = sb("lin", [P, D], 168)
    ybuf = [sb(f"ybuf{i}", [P, D], 4 + 4 * i) for i in range(2)]
    glu = sb("glu", [P, D], 12)
    act_rows = sb("act_rows", [P, D], 200)
    pick = [sb(f"pick{i}", [2 * NE, P], 204 + 0.5 * i, F32R) for i in range(2)]
    tok_col = [sb(f"tok_col{i}", [P, 1], 205 + i / 32, I32) for i in range(2)]
    pair_col = [sb(f"pair_col{i}", [P, 1], 205.125 + i / 32, I32) for i in range(2)]
    gate_col = [sb(f"gate_col{i}", [P, 1], 205.25 + i / 32) for i in range(2)]
    ysum = [sb(f"ysum{k}", [P, NT, D], 20 + 16 * k) for k in range(TOPK)]
    hu = bank[:, 0:4, :].rearrange("p b n -> p (b n)")
    yb = bank[:, 4:6, :].rearrange("p b n -> p (b n)")

    gain_in, router_in, bias_in = sem("ffn_gain_in"), sem("router_in"), sem("bias_in")
    moe_consts, consts_f = sem("moe_consts"), sem("moe_consts_f")
    f_squared, f_mean, f_root, h2_made, h2_stored = sem("f_squared"), sem("f_mean"), sem("f_root"), sem("h2_made"), sem("h2_stored")
    h2T_made, h2T_out, logits_made = sem("h2T_made"), sem("h2T_out"), sem("logits_made")
    gate_diff, gate_exp, chosen_made, place_made = sem("gate_diff"), sem("gate_exp"), sem("chosen_made"), sem("place_made")
    padded, dest_made, tabled, table_in = sem("padded"), sem("dest_made"), sem("tabled"), sem("table_in")
    tableT_made, tableT_out = sem("tableT_made"), sem("tableT_out")
    b_hi_made, b_parts_made = sem("b_hi_made"), sem("b_parts_made")
    unit_in = [sem(f"unit_in{i}") for i in range(RAW)]
    unit_hi, unit_lo, unit_done = sem("unit_hi"), sem("unit_lo"), sem("unit_done")
    early_cols, late_cols = sem("early_cols"), sem("late_cols")
    xg_cleared = sem("xg_cleared")
    gathered = [sem(f"gathered{i}") for i in range(2)]
    rowsT_made, rowsT_hi, rowsT_lo = sem("rowsT_made"), sem("rowsT_hi"), sem("rowsT_lo")
    hu_made, glu_made, sg_made, act_made = sem("hu_made"), sem("glu_made"), sem("sg_made"), sem("act_made")
    lin_made = sem("lin_made")
    y_made, y_out = sem("y_made"), sem("y_out")
    y_stored = [sem(f"y_stored{i}") for i in range(2)]
    ysum_in = [sem(f"ysum_in{k}") for k in range(TOPK)]
    busiest_made, experts_done = sem("busiest_made"), sem("experts_done")
    MORE = SLOTS - 1
    RING = 4
    more_in = [sem(f"more_in{i}") for i in range(RING)]
    more_hi, more_lo, more_done = sem("more_hi"), sem("more_lo"), sem("more_done")
    more_cols, more_gathered, more_stored = sem("more_cols"), sem("more_gathered"), sem("more_stored")
    more_rowsT, more_rows_hi, more_rows_lo = sem("more_rowsT"), sem("more_rows_hi"), sem("more_rows_lo")
    more_hu, more_glu, more_sg, more_act = sem("more_hu"), sem("more_glu"), sem("more_sg"), sem("more_act")
    more_y, more_y_out = sem("more_y"), sem("more_y_out")
    summed, out_stored = sem("summed"), sem("out_stored")
    proj_step, after_branches = mem["proj_step"], mem["after_branches"]
    after_out = mem["after_out"]

    gate_up = io["w_gate_up"][0].rearrange("e (c p) n -> e p c n", p=P)
    down = io["w_down"][0].rearrange("e (c p) n -> e p c n", p=P)
    table = io["table"]
    y_pairs = io["y_pairs"]

    GU, DN = DC, DC // 2

    def first_unit(s):
        return 12 * s - 4 if not isinstance(s, int) or s > 0 else 0

    def slot(s, m, n):
        return (m if isinstance(s, int) and s == 0 else m - 4) % n

    def unit_loaded(s, m):
        if isinstance(s, int) and s == 0:
            return 16 * (m // RAW + 1)
        return 16 * (2 * s + (m - 4) // RAW + 1)

    def event_aT(s):
        return 4 * s if not (isinstance(s, int) and s == NE) else 4 * s - 2

    def more_blocks(eng, body, begin=None):
        eng.wait_ge(busiest_made, 1)
        most = eng.value_load(busiest[0:1, 0:1], min_val=0, max_val=S)
        with eng.If(most > BLOCK_ROWS):
            for p in range(2):
                eng.wait_ge(y_stored[p], 16 * NE // 2)
            if begin is not None:
                begin()
            with eng.Fori(0, NE) as e:
                for b in range(1, SLOTS):
                    body(e, SLOTS * e + b, MORE * e + (b - 1))

    def load_unit(sp, s, m, e_gu, e_dn, m_dn=None):
        u = first_unit(s) + m
        if not (isinstance(s, int) and s == 0 and m < RAW):
            sp.wait_ge(unit_hi, u - RAW + 1)
            sp.wait_ge(unit_lo, u - RAW + 1)
        k = slot(s, m, RAW)
        if m_dn is None and m < GU:
            sp.dma_start(raw[k][:], gate_up[bass.ds(e_gu, 1), :, m, :].rearrange("a p n -> (a p) n")).then_inc(unit_in[k], 16)
        else:
            j = m - GU if m_dn is None else m_dn
            sp.dma_start(raw[k][:].rearrange("p (c n) -> p c n", c=2),
                         down[bass.ds(e_dn, 1), :, 2 * j:2 * j + 2, :].rearrange("a p c n -> (a p) c n")).then_inc(unit_in[k], 16)

    def sync(sp):
        sp.wait_ge(proj_step, after_branches)
        sp.dma_start(b_raw[0:NE, 0:2 * D], io["b_gate_up"][0]).then_inc(bias_in, 16)
        sp.dma_start(b_raw[NE:2 * NE, 0:2 * D], io["b_gate_up"][0]).then_inc(bias_in, 16)
        sp.dma_start(b_raw[0:NE, 2 * D:3 * D], io["b_down"][0]).then_inc(bias_in, 16)
        sp.dma_start(b_raw[NE:2 * NE, 2 * D:3 * D], io["b_down"][0]).then_inc(bias_in, 16)
        for m in range(4):
            load_unit(sp, 0, m, 0, 0)
        sp.wait_ge(mem["mT_lo_out"], 8)
        sp.dma_start(ffn_gain[:], io["ffn_norm"][0].partition_broadcast(P)).then_inc(gain_in, 16)
        sp.dma_start(w_router[:], io["w_router"][0].rearrange("(c p) e -> p c e", p=P)).then_inc(router_in, 16)
        sp.dma_start(b_router[:], io["b_router"][0].partition_broadcast(P)).then_inc(router_in, 16)
        sp.wait_ge(mem["w_lo_made"], mem["n_units"])
        for m in range(4, 6):
            load_unit(sp, 0, m, 0, 0)
        for t in range(NT):
            sp.wait_ge(h2_made, t + 1)
            sp.dma_start(io["h2_dram"][t * P:(t + 1) * P, :], h2[:, t, :]).then_inc(h2_stored, 16)
        sp.wait_ge(tabled, 16 * NT * TOPK)
        sp.dma_start(table_sb[:].rearrange("p r c -> p (r c)"), table.rearrange("(b r) c -> b (r c)", r=P)).then_inc(table_in, 16)
        for m in range(6, 8):
            load_unit(sp, 0, m, 0, 0)
        with sp.Fori(0, NE // 2 - 1) as pair:
            i = 2 * pair + 1
            for s in (i, i + 1):
                for m in range(12):
                    load_unit(sp, s, m, s, s - 1)
        for m in range(12):
            load_unit(sp, NE - 1, m, NE - 1, NE - 2)
        for m in range(4):
            load_unit(sp, NE, m, 0, NE - 1, m_dn=m)

        def more_loads(e, column, n):
            for m in range(GU + DN):
                sp.wait_ge(more_lo, 12 * n + m + 1)
                if m < GU:
                    sp.dma_start(raw[m % RING][:], gate_up[bass.ds(e, 1), :, m, :].rearrange("a p n -> (a p) n"))\
                        .then_inc(more_in[m % RING], 16)
                else:
                    j = m - GU
                    sp.dma_start(raw[m % RING][:].rearrange("p (c n) -> p c n", c=2),
                                 down[bass.ds(e, 1), :, 2 * j:2 * j + 2, :].rearrange("a p c n -> (a p) c n"))\
                        .then_inc(more_in[m % RING], 16)

        more_blocks(sp, more_loads)
        sp.wait_ge(experts_done, 1)
        for k in range(TOPK):
            sp.dma_start(ysum[k][:], y_pairs[k * S:(k + 1) * S, :].rearrange("(t p) d -> p t d", p=P)).then_inc(ysum_in[k], 16)
        for t in range(NT):
            sp.wait_ge(summed, t + 1)
            sp.dma_start(out[0, t * P:(t + 1) * P, :], x2[:, t, :]).then_inc(out_stored, 16)
        sp.wait_ge(out_stored, 16 * NT)

    def pool(pl):
        pl.wait_ge(proj_step, after_branches)
        pl.memset(tri[:], 1.0).then_inc(moe_consts, 1)
        pl.memset(ones[:], 1.0).then_inc(moe_consts, 1)
        pl.memset(hot64[:], 0.0).then_inc(moe_consts, 1)
        pl.iota(iota_i[:], pattern=[[1, NE]], base=0, channel_multiplier=0).then_inc(moe_consts, 1)
        pl.wait_ge(moe_consts, 4)
        pl.affine_select(out=tri[:], in_=tri[:], compare_op=ALU.is_gt, fill=0.0, base=0,
                         pattern=[[1, P]], channel_multiplier=-1).then_inc(moe_consts, 1)
        pl.affine_select(out=hot64[:], in_=hot64[:], compare_op=ALU.not_equal, fill=1.0, base=0,
                         pattern=[[-1, NE]], channel_multiplier=1).then_inc(moe_consts, 1)
        pl.wait_ge(moe_consts, 6)
        pl.affine_select(out=hot64[:], in_=hot64[:], compare_op=ALU.not_equal, fill=1.0, base=-NE,
                         pattern=[[-1, NE]], channel_multiplier=1).then_inc(moe_consts, 1)
        pl.wait_ge(mem["mT_lo_out"], 8)
        pl.memset(pad[:], float(PAD_PAIR)).then_inc(moe_consts, 1)
        pl.iota(pair_i[:], pattern=[[P, NT], [S, TOPK]], base=0, channel_multiplier=1).then_inc(moe_consts, 1)
        pl.wait_ge(moe_consts, 9)
        pl.dma_start(table.rearrange("(b r) c -> b (r c)", r=P), pad[:]).then_inc(padded, 16)
        pl.wait_ge(padded, 16)
        pl.wait_ge(dest_made, 1)
        for j in range(NT * TOPK):
            pl.indirect_dma_start(table, bass.IndirectOffsetOnAxis(dest[:, j:j + 1], 0),
                                  payload[:, j // TOPK, j % TOPK, :], None).then_inc(tabled, 16)

        def wait_step(semaphore, value, met=(b_parts_made, 1)):
            value = value if isinstance(value, int) else pl.snap(value)
            pl.wait_ge(*met)
            pl.wait_ge(semaphore, value)

        def token_col(e, p):
            pl.tensor_copy(tok_col[p][:], tokT[:, bass.ds(SLOTS * e, 1)]).then_inc(early_cols, 1)
            pl.wait_ge(early_cols, e + 1)

        def early(e, p):
            pl.indirect_dma_start(xg[p][:], None, io["h2_dram"], bass.IndirectOffsetOnAxis(tok_col[p][:], 0),
                                  bounds_check=S - 1, oob_is_err=False).then_inc(gathered[p], 16)

        def late(e, p):
            pl.tensor_copy(pair_col[p][:], pairT[:, bass.ds(SLOTS * e, 1)]).then_inc(late_cols, 1)
            pl.tensor_copy(gate_col[p][:], gateT[:, bass.ds(SLOTS * e, 1)]).then_inc(late_cols, 1)
            pl.tensor_copy(pick[p][:], hot64[:, bass.ds(e, 1)].to_broadcast([2 * NE, P])).then_inc(late_cols, 1)

        def store(e, p):
            wait_step(y_out, e + 1)
            pl.indirect_dma_start(y_pairs, bass.IndirectOffsetOnAxis(pair_col[p][:], 0), ybuf[p][:], None,
                                  bounds_check=N_PAIRS - 1, oob_is_err=False).then_inc(y_stored[p], 16)

        def stored_before(e, p):
            wait_step(y_stored[p], 8 * (e - p))

        pl.wait_ge(dest_made, 1)
        pl.memset(xg[0][:], 0.0).then_inc(xg_cleared, 1)
        pl.memset(xg[1][:], 0.0).then_inc(xg_cleared, 1)
        pl.wait_ge(xg_cleared, 2)
        pl.wait_ge(tableT_out, 2)
        pl.wait_ge(h2_stored, 16 * NT)
        pl.wait_ge(b_parts_made, 1)
        token_col(0, 0)
        early(0, 0)
        token_col(1, 1)
        late(0, 0)
        early(1, 1)
        pl.wait_ge(rowsT_made, 2)
        token_col(2, 0)
        late(1, 1)
        early(2, 0)
        pl.wait_ge(rowsT_made, 4)
        token_col(3, 1)
        early(3, 1)
        store(0, 0)
        with pl.Fori(0, NE // 2 - 2) as pair:
            i = 2 * pair + 2
            for p, s in ((0, i), (1, i + 1)):
                stored_before(s, p)
                wait_step(rowsT_made, 4 * s)
                token_col(s + 2, p)
                late(s, p)
                early(s + 2, p)
                store(s - 1, 1 - p)
        for s in (NE - 2, NE - 1):
            stored_before(s, s % 2)
            late(s, s % 2)
            store(s - 1, 1 - s % 2)
        store(NE - 1, 1)
        for p in range(2):
            pl.wait_ge(y_stored[p], 16 * NE // 2)

        def more_rows(e, column, n):
            pl.tensor_copy(tok_col[0][:], tokT[:, bass.ds(column, 1)]).then_inc(more_cols, 1)
            pl.wait_ge(more_cols, 4 * n + 1)
            pl.tensor_copy(pair_col[0][:], pairT[:, bass.ds(column, 1)]).then_inc(more_cols, 1)
            pl.tensor_copy(gate_col[0][:], gateT[:, bass.ds(column, 1)]).then_inc(more_cols, 1)
            pl.tensor_copy(pick[0][:], hot64[:, bass.ds(e, 1)].to_broadcast([2 * NE, P])).then_inc(more_cols, 1)
            pl.indirect_dma_start(xg[0][:], None, io["h2_dram"], bass.IndirectOffsetOnAxis(tok_col[0][:], 0),
                                  bounds_check=S - 1, oob_is_err=False).then_inc(more_gathered, 16)
            wait_step(more_y_out, 4 * n + 1)
            pl.indirect_dma_start(y_pairs, bass.IndirectOffsetOnAxis(pair_col[0][:], 0), ybuf[0][:], None,
                                  bounds_check=N_PAIRS - 1, oob_is_err=False).then_inc(more_stored, 16)
            wait_step(more_stored, 16 * n + 16)

        more_blocks(pl, more_rows)
        pl.sem_inc(experts_done, 1)

    def tensor(te):
        def mm3(out, a, b, first, last=False):
            te.matmul(out, a[0], b[0], start=first, stop=False)
            te.matmul(out, a[0], b[1], start=False, stop=False)
            return te.matmul(out, a[1], b[0], start=False, stop=last)

        def transpose(out, a):
            return te.matmul(out, a, ident[:], is_transpose=True, start=True, stop=True)

        for j in range(8):
            t, half = j // 2, j % 2
            te.wait_ge(h2_made, t + 1)
            if j >= 4:
                te.wait_ge(h2T_out, j - 3)
            for c in range(4):
                m = transpose(bank[:, j % 4, c * P:(c + 1) * P], h2[:, t, (4 * half + c) * P:(4 * half + c + 1) * P])
            m.then_inc(h2T_made, 1)
        te.wait_ge(h2T_out, 8)
        te.wait_ge(router_in, 32)
        for t in range(NT):
            for k in range(DC):
                m = te.matmul(bank[:, 4, t * NE:(t + 1) * NE], h2T[:, k, t * P:(t + 1) * P], w_router[:, k, :],
                              start=k == 0, stop=k == DC - 1)
        m.then_inc(logits_made, 1)
        te.wait_ge(moe_consts, 9)
        te.wait_ge(chosen_made, 1)
        for t in range(NT):
            for u in range(t + 1):
                m = te.matmul(bank[:, 5, t * NE:(t + 1) * NE], (ones if u < t else tri)[:], chosen[:, u, :],
                              start=u == 0, stop=u == t)
        for u in range(NT):
            m = te.matmul(bank[:, 5, NT * NE:(NT + 1) * NE], ones[:], chosen[:, u, :], start=u == 0, stop=u == NT - 1)
        m.then_inc(place_made, 1)
        te.wait_ge(table_in, 16)
        for c in range(2):
            m = transpose(bank[:, 4, c * P:(c + 1) * P], table_sb[:, :, c])
        m.then_inc(tableT_made, 1)

        def rows_out(dst_event, src, s_is_first):
            for b in range(2):
                if not (s_is_first and b < 2 and isinstance(dst_event, int) and dst_event == 0):
                    te.wait_ge(rowsT_lo, dst_event + b - 1)
                for c in range(4):
                    m = transpose(bank[:, 6 + b, c * P:(c + 1) * P], src[:, (4 * b + c) * P:(4 * b + c + 1) * P])
                m.then_inc(rowsT_made, 1)

        def x_transpose(e_round, p, event, first=False):
            te.wait_ge(gathered[p], e_round)
            rows_out(event, xg[p], first)

        def gate_up_step(s, p, x_event_end, between=None):
            te.wait_ge(rowsT_lo, x_event_end)
            for m in range(GU):
                if m == 2 and between is not None:
                    between()
                k = slot(s, m, SPLIT)
                te.wait_ge(unit_lo, first_unit(s) + m + 1)
                for n in range(4):
                    c = slice(n * 512, n * 512 + 512)
                    i = mm3(bank[:, n, :], (xT_hi[p][:, m, :], xT_lo[p][:, m, :]), (hi[k][:, c], lo[k][:, c]), m == 0)
                i.then_inc(unit_done, 1)
            te.wait_ge(late_cols, 3 * (s + 1))
            for n in range(4):
                i = te.matmul(bank[:, n, :], pick[p][:], b_parts[:, n * 512:n * 512 + 512], start=False, stop=True)
            i.then_inc(hu_made, 1)

        def down_step(s, p, a_event, m0=GU):
            te.wait_ge(rowsT_lo, a_event + 2)
            if not (isinstance(s, int) and s == 1):
                te.wait_ge(y_out, s - 1)
            for m in range(DN):
                k = slot(s, m0 + m, SPLIT)
                te.wait_ge(unit_lo, first_unit(s) + m0 + m + 1)
                for c in range(2):
                    for n in range(2):
                        w = slice(c * D + n * 512, c * D + n * 512 + 512)
                        i = mm3(bank[:, 4 + n, :], (aT_hi[:, 2 * m + c, :], aT_lo[:, 2 * m + c, :]),
                                (hi[k][:, w], lo[k][:, w]), m == 0 and c == 0)
                i.then_inc(unit_done, 1)
            for n in range(2):
                i = te.matmul(bank[:, 4 + n, :], pick[p][:], b_parts[:, 2 * D + n * 512:2 * D + n * 512 + 512],
                              start=False, stop=True)
            i.then_inc(y_made, 1)

        te.wait_ge(b_parts_made, 1)
        te.wait_ge(tableT_out, 2)
        x_transpose(16, 0, 0, True)
        x_transpose(16, 1, 2)
        gate_up_step(0, 0, 2)

        def whole_step(s, p):
            def transposes():
                te.wait_ge(act_made, s)
                rows_out(4 * s, act_rows, False)
                x_transpose(8 * (s + 1) + (16 if p else 8), 1 - p, 4 * s + 2)

            te.wait_ge(lin_made, 2 * s - 1)
            gate_up_step(s, p, 4 * s, transposes)
            down_step(s, 1 - p, 4 * s)

        whole_step(1, 1)
        whole_step(2, 0)
        with te.Fori(0, NE // 2 - 2) as pair:
            i = 2 * pair + 3
            whole_step(i, 1)
            whole_step(i + 1, 0)
        te.wait_ge(act_made, NE - 1)
        rows_out(4 * (NE - 1), act_rows, False)
        gate_up_step(NE - 1, 1, 4 * (NE - 1))
        down_step(NE - 1, 0, 4 * (NE - 1))
        te.wait_ge(act_made, NE)
        rows_out(4 * NE - 2, act_rows, False)
        down_step(NE, 1, 4 * NE - 2, m0=0)

        def more_rows_out(n, src, first):
            for b in range(2):
                for c in range(4):
                    i = transpose(bank[:, 6 + b, c * P:(c + 1) * P], src[:, (4 * b + c) * P:(4 * b + c + 1) * P])
                i.then_inc(more_rowsT, 1)
            te.wait_ge(more_rows_lo, 4 * n + (2 if first else 4))

        def more_products(e, column, n):
            te.wait_ge(more_gathered, 16 * n + 16)
            more_rows_out(n, xg[0], True)
            for m in range(GU):
                te.wait_ge(more_lo, RING + 12 * n + m + 1)
                for q in range(4):
                    c = slice(q * 512, q * 512 + 512)
                    i = mm3(bank[:, q, :], (xT_hi[0][:, m, :], xT_lo[0][:, m, :]), (hi[m % RING][:, c], lo[m % RING][:, c]), m == 0)
                i.then_inc(more_done, 1)
            te.wait_ge(more_cols, 4 * n + 4)
            for q in range(4):
                i = te.matmul(bank[:, q, :], pick[0][:], b_parts[:, q * 512:q * 512 + 512], start=False, stop=True)
            i.then_inc(more_hu, 1)
            te.wait_ge(more_act, n + 1)
            more_rows_out(n, act_rows, False)
            for m in range(DN):
                k = (GU + m) % RING
                te.wait_ge(more_lo, RING + 12 * n + GU + m + 1)
                for c in range(2):
                    for q in range(2):
                        w = slice(c * D + q * 512, c * D + q * 512 + 512)
                        i = mm3(bank[:, 4 + q, :], (aT_hi[:, 2 * m + c, :], aT_lo[:, 2 * m + c, :]),
                                (hi[k][:, w], lo[k][:, w]), m == 0 and c == 0)
                i.then_inc(more_done, 1)
            for q in range(2):
                i = te.matmul(bank[:, 4 + q, :], pick[0][:], b_parts[:, 2 * D + q * 512:2 * D + q * 512 + 512],
                              start=False, stop=True)
            i.then_inc(more_y, 1)

        more_blocks(te, more_products, begin=lambda: te.sem_inc(more_done, RING))

    def scalar(ac):
        for t in range(NT):
            ac.wait_ge(mem["x2_made"], NT + t + 1)
            if t:
                ac.wait_ge(f_squared, t)
            else:
                ac.wait_ge(mem["mT_lo_out"], 8)
            ac.activation(square[:], x2[:, t, :], ACT.Square, accum_out=fstat[:, 0, t:t + 1]).then_inc(f_squared, 1)
        ac.wait_ge(f_mean, 1)
        ac.activation(fstat[:, 2, :], fstat[:, 1, :], ACT.Sqrt).then_inc(f_root, 1)
        for j in range(8):
            t, half = j // 2, j % 2
            ac.wait_ge(h2T_made, j + 1)
            ac.activation(h2T[:, 4 * half:4 * half + 4, t * P:(t + 1) * P],
                          bank[:, j % 4, :].rearrange("p (c q) -> p c q", c=4), ACT.Copy).then_inc(h2T_out, 1)
        ac.wait_ge(bias_in, 64)
        ac.activation(b_parts[:], b_raw[:], ACT.Copy).then_inc(b_hi_made, 1)
        ac.wait_ge(gate_diff, 1)
        ac.activation(gate[:], gate[:], ACT.Exp).then_inc(gate_exp, 1)

        def split(s, m):
            k = slot(s, m, SPLIT)
            ac.wait_ge(unit_in[slot(s, m, RAW)], unit_loaded(s, m))
            if not (isinstance(s, int) and s == 0 and m < SPLIT):
                ac.wait_ge(unit_done, first_unit(s) + m - SPLIT + 1)
            ac.activation(hi[k][:], raw[slot(s, m, RAW)][:], ACT.Copy).then_inc(unit_hi, 1)

        def rows_hi(event, dst):
            for b in range(2):
                ac.wait_ge(rowsT_made, event + b + 1)
                ac.activation(dst[:, 4 * b:4 * b + 4, :], bank[:, 6 + b, :].rearrange("p (c q) -> p c q", c=4), ACT.Copy)\
                    .then_inc(rowsT_hi, 1)

        def sigmoid(s):
            ac.wait_ge(glu_made, s + 1)
            ac.activation(sg[:], glu[:], ACT.Sigmoid, scale=1.702).then_inc(sg_made, 1)

        def y_rows(e, p, wait=True):
            ac.wait_ge(y_made, e + 1)
            if wait:
                ac.wait_ge(y_stored[p], 8 * (e - p))
            ac.activation(ybuf[p][:], yb, ACT.Copy, scale=gate_col[p][:]).then_inc(y_out, 1)

        ac.wait_ge(mem["w_lo_made"], mem["n_units"])
        ac.wait_ge(proj_step, after_out)
        ac.wait_ge(tableT_out, 2)
        ac.wait_ge(b_parts_made, 1)
        for m in range(4):
            split(0, m)
        rows_hi(0, xT_hi[0])
        rows_hi(2, xT_hi[1])
        for m in range(4, GU):
            split(0, m)
        sigmoid(0)

        def whole_step(s, p, last=False):
            for m in range(12):
                if m == 3:
                    if not (isinstance(s, int) and s == 1):
                        y_rows(s - 2, p, wait=not (isinstance(s, int) and s < 4))
                    rows_hi(4 * s, aT_hi)
                    if not last:
                        rows_hi(4 * s + 2, xT_hi[1 - p])
                split(s, m)
            sigmoid(s)

        for s in (1, 2, 3, 4):
            whole_step(s, s % 2)
        with ac.Fori(0, NE // 2 - 3) as pair:
            i = 2 * pair + 5
            whole_step(i, 1)
            whole_step(i + 1, 0)
        whole_step(NE - 1, 1, last=True)
        for m in range(3):
            split(NE, m)
        y_rows(NE - 2, 0)
        rows_hi(4 * NE - 2, aT_hi)
        split(NE, 3)
        y_rows(NE - 1, 1)

        def more_acts(e, column, n):
            def rows(first, dst):
                for b in range(2):
                    ac.wait_ge(more_rowsT, 4 * n + (0 if first else 2) + b + 1)
                    ac.activation(dst[:, 4 * b:4 * b + 4, :], bank[:, 6 + b, :].rearrange("p (c q) -> p c q", c=4), ACT.Copy)\
                        .then_inc(more_rows_hi, 1)

            def splits(first, last):
                for m in range(first, last):
                    ac.wait_ge(more_in[m % RING], 16 * (3 * n + m // RING + 1))
                    ac.wait_ge(more_done, 12 * n + m + 1)
                    ac.activation(hi[m % RING][:], raw[m % RING][:], ACT.Copy).then_inc(more_hi, 1)

            rows(True, xT_hi[0])
            splits(0, GU)
            ac.wait_ge(more_glu, n + 1)
            ac.activation(sg[:], glu[:], ACT.Sigmoid, scale=1.702).then_inc(more_sg, 1)
            rows(False, aT_hi)
            splits(GU, GU + DN)
            ac.wait_ge(more_y, n + 1)
            ac.activation(ybuf[0][:], yb, ACT.Copy, scale=gate_col[0][:]).then_inc(more_y_out, 4)

        more_blocks(ac, more_acts)

    def vector(ve):
        step = mem["step"]
        ve.wait_ge(f_squared, NT)
        ve.tensor_scalar(fstat[:, 1, :], fstat[:, 0, :], 1.0 / D, EPS, ALU.mult, ALU.add).then_inc(f_mean, 1)
        ve.wait_ge(f_root, 1)
        step(ve.reciprocal(fstat[:, 3, :], fstat[:, 2, :]))
        ve.wait_ge(gain_in, 16)
        for t in range(NT):
            ve.scalar_tensor_tensor(h2[:, t, :], x2[:, t, :], fstat[:, 3, t:t + 1], ffn_gain[:], ALU.mult, ALU.mult)\
                .then_inc(h2_made, 1)
        ve.wait_ge(b_hi_made, 1)
        ve.tensor_tensor(b_parts[NE:2 * NE, :], b_raw[NE:2 * NE, :], b_parts[NE:2 * NE, :].bitcast(F32), ALU.subtract)\
            .then_inc(b_parts_made, 1)
        ve.wait_ge(moe_consts, 9)
        step(ve.tensor_copy(iota_e[:], iota_i[:]))
        step(ve.tensor_scalar(iota_slot[:], iota_e[:], float(S), None, ALU.mult))
        ve.tensor_copy(payload[:, :, :, 0], pair_i[:])
        ve.wait_ge(router_in, 32)
        ve.wait_ge(logits_made, 1)
        step(ve.tensor_tensor(logits[:], bank[:, 4, 0:NT * NE].rearrange("p (t e) -> p t e", t=NT),
                              b_router[:].unsqueeze(1).to_broadcast([P, NT, NE]), ALU.add))
        for t in range(NT):
            step(ve.max(top_val[:, t, :], logits[:, t, :]))
            step(ve.max_index(top_idx[:, t, :], top_val[:, t, :], logits[:, t, :]))
        step(ve.tensor_copy(top_f[:], top_idx[:, :, 0:TOPK]))
        ve.tensor_tensor(gate[:], top_val[:, :, 0:TOPK], top_val[:, :, 0:1].to_broadcast([P, NT, TOPK]), ALU.subtract)\
            .then_inc(gate_diff, 1)
        step(ve.tensor_tensor(onehot[:].rearrange("p t k e -> p (t k) e"),
                              iota_e[:].unsqueeze(1).to_broadcast([P, NT * TOPK, NE]),
                              top_f[:].rearrange("p t k -> p (t k)").unsqueeze(2).to_broadcast([P, NT * TOPK, NE]), ALU.is_equal))
        ve.reduce_sum(chosen[:], onehot[:].rearrange("p t k e -> p t e k"), axis=AX.X).then_inc(chosen_made, 1)
        ve.wait_ge(gate_exp, 1)
        step(ve.reduce_sum(gate_sum[:], gate[:], axis=AX.X))
        step(ve.reciprocal(gate_sum[:], gate_sum[:]))
        step(ve.tensor_tensor(payload[:, :, :, 1], gate[:], gate_sum[:].unsqueeze(2).to_broadcast([P, NT, TOPK]), ALU.mult))
        ve.wait_ge(place_made, 1)
        step(ve.tensor_tensor(place[:], bank[:, 5, 0:NT * NE].rearrange("p (t e) -> p t e", t=NT),
                              iota_slot[:].unsqueeze(1).to_broadcast([P, NT, NE]), ALU.add))
        step(ve.reduce_max(busiest_f[:], bank[:, 5, NT * NE:(NT + 1) * NE], axis=AX.X))
        ve.tensor_copy(busiest[:], busiest_f[:]).then_inc(busiest_made, 1)
        for t in range(NT):
            last = ve.tensor_tensor(picked[:, t], onehot[:, t], place[:, t, :].unsqueeze(1).to_broadcast([P, TOPK, NE]), ALU.mult)
        step(last)
        step(ve.reduce_sum(dest_f[:], picked[:].rearrange("p t k e -> p (t k) e"), axis=AX.X))
        ve.tensor_copy(dest[:], dest_f[:]).then_inc(dest_made, 1)
        ve.wait_ge(tableT_made, 1)
        step(ve.tensor_copy(pairT[:], bank[:, 4, 0:P]))
        ve.tensor_copy(gateT[:], bank[:, 4, P:2 * P]).then_inc(tableT_out, 1)
        ve.tensor_single_scalar(tokT[:], pairT[:], PAD_PAIR + S - 1, ALU.bitwise_and).then_inc(tableT_out, 1)

        def split(s, m):
            k = slot(s, m, SPLIT)
            ve.wait_ge(unit_hi, first_unit(s) + m + 1)
            ve.tensor_tensor(lo[k][:], raw[slot(s, m, RAW)][:], hi[k][:].bitcast(F32), ALU.subtract).then_inc(unit_lo, 1)

        def rows_lo(event, dst, dst_hi):
            for b in range(2):
                ve.wait_ge(rowsT_hi, event + b + 1)
                ve.tensor_tensor(dst[:, 4 * b:4 * b + 4, :], bank[:, 6 + b, :].rearrange("p (c q) -> p c q", c=4),
                                 dst_hi[:, 4 * b:4 * b + 4, :].bitcast(F32), ALU.subtract).then_inc(rowsT_lo, 1)

        def swiglu(s, between=None):
            ve.wait_ge(hu_made, s + 1)
            v = hu.rearrange("p (f two) -> p f two", two=2)
            ve.tensor_scalar(glu[:], v[:, :, 0], 7.0, None, ALU.min).then_inc(glu_made, 1)
            if between is not None:
                split(s, between)
            ve.tensor_scalar(lin[:], v[:, :, 1], 7.0, -7.0, ALU.min, ALU.max).then_inc(lin_made, 1)
            ve.wait_ge(glu_made, s + 1)
            ve.wait_ge(lin_made, 2 * s + 1)
            ve.scalar_tensor_tensor(lin[:], lin[:], 1.0, glu[:], ALU.add, ALU.mult).then_inc(lin_made, 1)
            ve.wait_ge(lin_made, 2 * s + 2)
            ve.wait_ge(sg_made, s + 1)
            ve.tensor_tensor(act_rows[:], lin[:], sg[:], ALU.mult).then_inc(act_made, 1)

        for m in range(4):
            split(0, m)
        rows_lo(0, xT_lo[0], xT_hi[0])
        rows_lo(2, xT_lo[1], xT_hi[1])
        for m in range(4, GU):
            split(0, m)
        swiglu(0)

        def whole_step(s, p, last=False):
            for m in range(11):
                if m == 3:
                    rows_lo(4 * s, aT_lo, aT_hi)
                    if not last:
                        rows_lo(4 * s + 2, xT_lo[1 - p], xT_hi[1 - p])
                split(s, m)
            swiglu(s, between=11)

        with ve.Fori(0, NE // 2 - 1) as pair:
            i = 2 * pair + 1
            whole_step(i, 1)
            whole_step(i + 1, 0)
        whole_step(NE - 1, 1, last=True)
        for m in range(3):
            split(NE, m)
        rows_lo(4 * NE - 2, aT_lo, aT_hi)
        split(NE, 3)

        def more_vectors(e, column, n):
            def rows(first, dst, dst_hi):
                for b in range(2):
                    ve.wait_ge(more_rows_hi, 4 * n + (0 if first else 2) + b + 1)
                    ve.tensor_tensor(dst[:, 4 * b:4 * b + 4, :], bank[:, 6 + b, :].rearrange("p (c q) -> p c q", c=4),
                                     dst_hi[:, 4 * b:4 * b + 4, :].bitcast(F32), ALU.subtract).then_inc(more_rows_lo, 1)

            def splits(first, last):
                for m in range(first, last):
                    ve.wait_ge(more_hi, 12 * n + m + 1)
                    ve.tensor_tensor(lo[m % RING][:], raw[m % RING][:], hi[m % RING][:].bitcast(F32), ALU.subtract)\
                        .then_inc(more_lo, 1)

            rows(True, xT_lo[0], xT_hi[0])
            splits(0, GU)
            ve.wait_ge(more_hu, n + 1)
            v = hu.rearrange("p (f two) -> p f two", two=2)
            ve.tensor_scalar(glu[:], v[:, :, 0], 7.0, None, ALU.min).then_inc(more_glu, 1)
            ve.tensor_scalar(lin[:], v[:, :, 1], 7.0, -7.0, ALU.min, ALU.max).then_inc(lin_made, 1)
            ve.wait_ge(more_glu, n + 1)
            ve.wait_ge(lin_made, 2 * NE + 2 * n + 1)
            ve.scalar_tensor_tensor(lin[:], lin[:], 1.0, glu[:], ALU.add, ALU.mult).then_inc(lin_made, 1)
            ve.wait_ge(lin_made, 2 * NE + 2 * n + 2)
            ve.wait_ge(more_sg, n + 1)
            ve.tensor_tensor(act_rows[:], lin[:], sg[:], ALU.mult).then_inc(more_act, 1)
            rows(False, aT_lo, aT_hi)
            splits(GU, GU + DN)

        more_blocks(ve, more_vectors, begin=lambda: ve.sem_inc(more_lo, RING))
        for k in range(TOPK):
            ve.wait_ge(ysum_in[k], 16)
            for t in range(NT):
                if k == TOPK - 1:
                    ve.tensor_tensor(x2[:, t, :], x2[:, t, :], ysum[k][:, t, :], ALU.add).then_inc(summed, 1)
                else:
                    last = ve.tensor_tensor(x2[:, t, :], x2[:, t, :], ysum[k][:, t, :], ALU.add)
            if k < TOPK - 1:
                step(last)

    return dict(sync=sync, pool=pool, tensor=tensor, scalar=scalar, vector=vector)


def program(nc, io, out):
    base = (nc.sbuf_base + 31) // 32 * 32

    def sb(name, shape, at_kb, dtype=F32):
        return nc.alloc_sbuf_tensor_at(name, shape, dtype, offset=base + int(at_kb * KB))

    bank = nc.alloc_psum_tensor("bank", [P, 8, 512], F32)
    mem = dict(ident=sb("ident", [P, P], 16), flip=sb("flip", [P, P], 16.5), x2=sb("x2", [P, NT, D], 172))
    for n in ("consts_made", "x2_made", "dve_step", "act_step"):
        mem[n] = nc.alloc_semaphore(n)
    pre = pre_moe(nc, io, sb, nc.alloc_semaphore, bank, mem)
    exp = moe(nc, io, out, sb, nc.alloc_semaphore, bank, mem)
    with nc.Block() as block:
        @block.sync
        def _(sp):
            pre["sync"](sp)
            exp["sync"](sp)

        @block.gpsimd
        def _(pl):
            pre["pool"](pl)
            exp["pool"](pl)

        @block.tensor
        def _(te):
            pre["tensor"](te)
            exp["tensor"](te)

        @block.scalar
        def _(ac):
            pre["scalar"](ac)
            exp["scalar"](ac)

        @block.vector
        def _(ve):
            pre["vector"](ve)
            exp["vector"](ve)


INPUTS = ["x", "attn_norm", "w_in", "nsa_q_norm", "nsa_k_norm", "cmp_k_w1", "cmp_k_w2", "cmp_v_w1", "cmp_v_w2",
          "dsa_kv_norm", "dsa_w_uk", "dsa_w_uv", "dsa_q_norm", "dsa_k_norm", "w_branch_a", "w_branch_b", "w_out",
          "rel_bias", "ffn_norm", "w_router", "b_router", "w_gate_up", "b_gate_up", "w_down", "b_down"]


def kernel(**inputs):
    import concourse.bacc as bacc
    from concourse.bass_utils import run_bass_kernel_spmd
    nc = bacc.Bacc("TRN2", target_bir_lowering=False, num_devices=1)
    arrays = {n: np.ascontiguousarray(inputs[n]) for n in INPUTS}
    arrays["pe_cols"] = np.ascontiguousarray(np.stack(
        [np.asarray(inputs[n]).reshape(16, P).T for n in ("cmp_k_pe", "cmp_v_pe")], axis=1))
    arrays["b1_cols"] = np.ascontiguousarray(np.stack(
        [np.asarray(inputs[n]).reshape(P) for n in ("cmp_k_b1", "cmp_v_b1")], axis=1))
    arrays["bias_hot"] = bias_one_hot()
    io = {n: nc.dram_tensor(n, a.shape, mybir.dt.from_np(a.dtype), kind="ExternalInput").ap() for n, a in arrays.items()}
    for n, shape in (("vec_dram", (2 * NH, 5 * P)), ("h2_dram", (S, D)), ("table", (NE * S, 2)), ("y_pairs", (N_PAIRS, D))):
        io[n] = nc.dram_tensor(n, shape, F32, kind="Internal").ap()
    out = nc.dram_tensor("out", (1, S, D), F32, kind="ExternalOutput").ap()
    program(nc, io, out)
    return run_bass_kernel_spmd(nc, [arrays], core_ids=[0]).results[0]["out"]
```

```python
import math

import numpy as np

import concourse.bass as bass
from concourse import mybir

F32 = mybir.dt.float32
F32R = mybir.dt.float32r
I32 = mybir.dt.int32
U32 = mybir.dt.uint32
ALU = mybir.AluOpType
ACT = mybir.ActivationFunctionType
AX = mybir.AxisListType

P = 128
S = 512
NT = S // P
D = 1024
DC = D // P
HD = 64
NH = 8
N_CMP = (S - 32) // 16 + 1
N_BUCKETS = 32
MASKED = -1e30
TAKEN = -3e38
KEEP = 128
EPS = 1e-6
NE = 32
TOPK = 4
BLOCK_ROWS = 128
SLOTS = S // BLOCK_ROWS
KB = 1024


def bias_one_hot():
    m = np.arange(5 * P)
    rel = (S - 1) - m
    n = np.maximum(rel, 0)
    exact = N_BUCKETS // 2
    nf = np.maximum(n, 1).astype(np.float32)
    large = exact + (np.log(nf / np.float32(exact)) / np.float32(math.log(128 / exact))
                     * np.float32(N_BUCKETS - exact)).astype(np.int32)
    bucket = np.where(n < exact, n, np.minimum(large, N_BUCKETS - 1))
    hot = (np.arange(N_BUCKETS + 1)[:, None] == np.where(rel < 0, N_BUCKETS, bucket)[None, :])
    return np.ascontiguousarray(hot.astype(np.float32))


def pre_moe(nc, io, sb, sem, bank, mem):
    ident, flip = mem["ident"], mem["flip"]
    iw = sb("iw", [P, NT, NH], 17)
    gates = sb("gates", [P, NT, NH * 3], 17.125)
    row_ok = sb("row_ok", [P, 1], 17.5)
    stat = sb("stat", [P, 4, 32], 17.75)
    neg_max = sb("neg_max", [P, P], 18.25)
    row_sum = sb("row_sum", [P, P], 18.75)
    coef = sb("coef", [P, P], 19.25)
    top8 = sb("top8", [P, 8], 19.75)
    x_in = sb("x_in", [P, NT, D], 0)
    h_rows = sb("h_rows", [P, NT, D], 188)
    bq_rows = sb("bq_rows", [P, NT * NH, HD], 0)
    aq_rows = sb("aq_rows", [P, NT * NH, HD], 8)
    k_rows = sb("k_rows", [P, NT, 5, HD], 188)
    ckv_rows = sb("ckv_rows", [P, NT, P], 193)
    junk = sb("junk", [P, 2048], 195)
    ckvT = sb("ckvT", [P, S], 203)
    craw = [sb("craw_k", [P, S], 193), sb("craw_v", [P, S], 203)]
    cT = sb("cT", [P, 2, 2, S], 195)
    windows = sb("windows", [P, 2, 16, 2 * N_CMP], 166)
    k_square = sb("k_square", [P, 5 * NT, HD], 156)
    w1 = sb("w1", [P, 2, 16, P], 0)
    idx_act = [sb(f"idx_act{i}", [P, S], 2 * i) for i in range(2)]
    hT_hi = sb("hT_hi", [P, DC, S], 20, F32R)
    hT_lo = sb("hT_lo", [P, DC, S], 36, F32R)
    w_raw = [sb(f"w_raw{i}", [P, 4, 512], 52 + 8 * i) for i in range(3)]
    w_hi = [sb(f"w_hi{i}", [P, 4, 512], 76 + 8 * i, F32R) for i in range(2)]
    w_lo = [sb(f"w_lo{i}", [P, 4, 512], 92 + 8 * i, F32R) for i in range(2)]
    bias = sb("bias", [P, 2 * NH, S], 108)
    hankel = [sb(f"hankel{i}", [P, 4, S], 140 + 8 * i) for i in range(2)]
    attn_gain = sb("attn_gain", [P, D], 156)
    square = sb("square", [P, D], 160)
    ckv_gain = sb("ckv_gain", [P, P], 164)
    w_ukv = sb("w_ukv", [P, 2 * HD], 164.5)
    tab = sb("tab", [N_BUCKETS + 1, 2 * NH], 165)
    hot = sb("hot", [N_BUCKETS + 1, 5 * P], 181)
    vec = sb("vec", [2 * NH, 5 * P], 183.5)
    aqT = sb("aqT", [P, 4, S], 140)
    bqT = sb("bqT", [P, 4, S], 148)
    kT = sb("kT", [P, 5, S], 156)
    iqT = sb("iqT", [P, 4, S], 166)
    ikT = sb("ikT", [P, S], 174)
    v_sel = sb("v_sel", [P, NT, 2 * HD], 176)
    v_win = sb("v_win", [P, NT, 2 * HD], 178)
    v_dsa = sb("v_dsa", [P, NT, HD], 180)
    score = [None, sb("score1", [P, 2 * P], 181), sb("score2", [P, 3 * P], 182), sb("score3", [P, 4 * P], 183.5)]
    bq_gain = sb("bq_gain", [P, HD], 186)
    aq_gain = sb("aq_gain", [P, HD], 186.25)
    k_gain = sb("k_gain", [P, 5, HD], 186.5)
    kcT = sb("kcT", [P, 2, N_CMP], 205)
    vc = sb("vc", [N_CMP, 2, HD], 205.25)
    hidT = sb("hidT", [P, 2, 2, N_CMP], 205.75)
    kc_rows = sb("kc_rows", [N_CMP, 2, HD], 206.25)
    w2 = sb("w2", [P, 2, HD], 206.75)
    pe = sb("pe", [P, 2, 16], 207.25)
    b1 = sb("b1", [P, 2], 207.375)
    logit = [sb(f"logit{i}", [P, S], 166 + 2 * i) for i in range(5)]
    pT = [sb(f"pT{i}", [P, NT, 4, P], 84 + 16 * i) for i in range(2)]
    oT_hi = sb("oT_hi", [P, 8, S], 0, F32R)
    oT_lo = sb("oT_lo", [P, 8, S], 188, F32R)
    sig = sb("sig", [P, 2, NT, 512], 108)
    merged = sb("merged", [P, NT, D], 124)
    mT_hi = sb("mT_hi", [P, DC, S], 140, F32R)
    mT_lo = sb("mT_lo", [P, DC, S], 156, F32R)
    x2 = mem["x2"]

    x_loaded = [sem(f"x_loaded{t}") for t in range(NT)]
    gain_loaded, tab_loaded, small_loaded = sem("gain_loaded"), sem("tab_loaded"), sem("small_loaded")
    w_loaded = [sem(f"w_loaded{i}") for i in range(3)]
    consts_made = mem["consts_made"]
    tab_masked, vec_stored = sem("tab_masked"), sem("vec_stored")
    hankel_loaded = [sem(f"hankel_loaded{i}") for i in range(2)]
    ik_copied, w1_loaded, c_copied = sem("ik_copied"), sem("w1_loaded"), sem("c_copied")
    squared, mean_made, root_made, normed = sem("squared"), sem("mean_made"), sem("root_made"), sem("normed")
    h_mean, h_root = sem("h_mean"), sem("h_root")
    hT_made, hT_lo_out, hT_hi_out = sem("hT_made"), sem("hT_lo_out"), sem("hT_hi_out")
    w_hi_made, w_lo_made = sem("w_hi_made"), sem("w_lo_made")
    proj_step, proj_out = sem("proj_step"), sem("proj_out")
    aux_made, aux_out = sem("aux_made"), sem("aux_out")
    idx_made, idx_relu, idx_added, causal_cut = sem("idx_made"), sem("idx_relu"), sem("idx_added"), sem("causal_cut")
    windows_made, gains_scaled = sem("windows_made"), sem("gains_scaled")
    sel_masked = sem("sel_masked")
    s_made, logit_made, exp_made = sem("s_made"), sem("logit_made"), sem("exp_made")
    mask_added, p_scaled = sem("mask_added"), sem("p_scaled")
    coef_made, p_scaled_act = sem("coef_made"), sem("p_scaled_act")
    even_heads = sem("even_heads")
    pT_made, pT_out = sem("pT_made"), sem("pT_out")
    pv_made, o_hi_out, o_lo_out = sem("pv_made"), sem("o_hi_out"), sem("o_lo_out")
    gate_out, branch_out = sem("gate_out"), sem("branch_out")
    mT_made, mT_hi_out, mT_lo_out = sem("mT_made"), sem("mT_hi_out"), sem("mT_lo_out")
    x_reloaded, x2_made = sem("x_reloaded"), mem["x2_made"]
    dve_step, act_step = mem["dve_step"], mem["act_step"]
    SMALL_LOADS = 14

    w_in = io["w_in"][0].rearrange("(c p) n -> p c n", p=P)
    branch = [io[n][0].rearrange("(c p) n -> p c n", p=P) for n in ("w_branch_a", "w_branch_b")]
    w_out = io["w_out"][0].rearrange("(c p) n -> p c n", p=P)
    CKV, IW, IK = 0, P, P + NH
    GROUPS = [[(CKV, 1816, P), (IW, 2520, NH), (IK, 2456, HD)], [(0, 1944, 512)], [(0, 1304, 512)],
              [(0, 0, 512)], [(0, 512, 512)], [(0, 1024, 280)]]
    G_CKV, G_IQ, G_BQ, G_AQ, G_CS, G_W = range(6)
    units = [[(dst, w_in[:, 4 * half:4 * half + 4, src:src + n]) for dst, src, n in g]
             for g in GROUPS for half in range(2)]
    GATE, BRANCH, OUT = "gate", "branch", "out"
    MERGE = []
    for c in range(2):
        for ab in range(2):
            MERGE.append((GATE, ab, c, [len(units), len(units) + 1]))
            col = 2528 + ab * D + c * 512
            units += [[(0, w_in[:, 4 * half:4 * half + 4, col:col + 512])] for half in range(2)]
        for ab in range(2):
            MERGE.append((BRANCH, ab, c, [len(units)]))
            units += [[(0, branch[ab][:, :, c * 512:c * 512 + 512])]]
    for c in range(2):
        MERGE.append((OUT, 0, c, [len(units), len(units) + 1]))
        units += [[(0, w_out[:, 4 * half:4 * half + 4, c * 512:c * 512 + 512])] for half in range(2)]
    N_UNITS = len(units)
    P1_UNITS = 2 * len(GROUPS)
    NG = len(GROUPS)
    group_units = [[2 * g, 2 * g + 1] for g in range(NG)] + [m[3] for m in MERGE]
    steps_before = [sum(len(v) + 3 for v in group_units[:g]) for g in range(len(group_units) + 1)]

    def bank_made(g, t):
        return steps_before[g] + len(group_units[g]) + t

    def unit_used(u):
        g = next(i for i, v in enumerate(group_units) if u in v)
        return steps_before[g + 1] if u == group_units[g][-1] else steps_before[g] + 1

    def unit_loaded(u):
        return 16 * sum(len(units[v]) for v in range(u % 3, u + 1, 3))

    def unit_width(u):
        return max(dst + src.shape[-1] for dst, src in units[u])

    AUX = ["vec0", "vec1", "ik", "ckvT", "kv"] + [f"bias{h}" for h in range(2 * NH)] \
        + [f"bqT{c}" for c in range(4)] + ["ck", "cv"] + [f"aqT{c}" for c in range(4)] \
        + ["hid", "kT0", "kT1", "kcvc", "kT2", "kT3", "kT4", "kcT"]

    def aux(name):
        return bank[:, 6 + AUX.index(name) % 2, :]

    items, batches, groups = [], [], []
    col = 0
    for mixer in ("nsa", "dsa"):
        for qi in range(NT):
            for g4 in range(2):
                g = len(groups)
                first = len(items)
                for kind in (("cmp", "sel", "win") if mixer == "nsa" else ("dsa",)):
                    b = len(batches)
                    n = 1 if kind == "cmp" else 4
                    for h in range(n):
                        width = 4 if kind == "cmp" else 1
                        items.append(dict(kind=kind, qi=qi, g4=g4, h=h, head=4 * g4 + h, batch=b, group=g,
                                          col=col, cols=width, start=h == 0, end=h == n - 1))
                        col += width
                    batches.append(dict(kind=kind, qi=qi, g4=g4, group=g, last=len(items) - 1))
                groups.append(dict(mixer=mixer, qi=qi, g4=g4, last=len(items) - 1,
                                   batches=(batches[-1:] if mixer == "dsa" else batches[-3:])))
    N_ITEMS = len(items)
    ACT_SCALED_END = 52
    NSA_ITEMS = sum(it["kind"] != "dsa" for it in items)
    masks = [n for n, it in enumerate(items) if it["kind"] == "dsa" and it["qi"] > 0]

    ACT_SCALED = [n for n in range(ACT_SCALED_END) if items[n]["kind"] in ("sel", "win") and items[n]["h"] % 2 == 1]

    def scaled_by(engine_items, n):
        return sum(i <= n for i in engine_items)

    def keys(it):
        return 8 * it["qi"] + 7 if it["kind"] == "cmp" else (it["qi"] + 1) * P

    AHEAD = 4
    S_BANKS, PT_BANKS = (0, 1, 2, 5), (3, 4)

    def s_bank(n):
        return bank[:, S_BANKS[n % AHEAD], :]

    def pT_bank(n):
        return bank[:, PT_BANKS[n % 2], :]

    def cview(n):
        it = items[n]
        return logit[n % 5][:, 0:4 * keys(it)].rearrange("p (h k) -> p h k", h=4)

    def sview(n):
        it = items[n]
        return s_bank(n)[:, 0:4 * keys(it)].rearrange("p (h k) -> p h k", h=4)

    def bias_of(it):
        c0 = 384 - it["qi"] * P
        if it["kind"] == "cmp":
            k = keys(it)
            return bias[:, 4 * it["g4"]:4 * it["g4"] + 4, c0 + 31:c0 + 31 + 16 * (k - 1) + 1:16]
        return bias[:, it["head"] + (NH if it["kind"] == "dsa" else 0), c0:S]

    N_RELU = 3 * NH
    ROUNDS = KEEP // 8
    EARLY_ROUNDS = 5
    EARLY_SPLIT = NSA_ITEMS // 2

    def sync(sp):
        for t in range(NT):
            sp.dma_start(x_in[:, t, :], io["x"][0, t * P:(t + 1) * P, :]).then_inc(x_loaded[t], 16)
            if t == 0:
                sp.dma_start(attn_gain[:], io["attn_norm"][0].partition_broadcast(P)).then_inc(gain_loaded, 16)
        for u in range(N_UNITS):
            if u == P1_UNITS:
                sp.wait_ge(aux_made, AUX.index("aqT3") + 1)
                sp.wait_ge(idx_added, N_RELU)
                for kv, name in enumerate(("cmp_k_w1", "cmp_v_w1")):
                    sp.dma_start(w1[:, kv], io[name][0].rearrange("(c p) h -> p c h", p=P)).then_inc(w1_loaded, 16)
                sp.wait_ge(c_copied, 8 * 16)
            if u >= 3:
                sp.wait_ge(w_hi_made, u - 2)
                sp.wait_ge(w_lo_made, u - 2)
            for dst, src in units[u]:
                sp.dma_start(w_raw[u % 3][:, :, dst:dst + src.shape[-1]], src).then_inc(w_loaded[u % 3], 16)
            if u == P1_UNITS + 3:
                sp.wait_ge(o_lo_out, len(groups))
                sp.dma_start(x2[:], io["x"][0].rearrange("(t p) d -> p t d", p=P)).then_inc(x_reloaded, 16)

    def pool(pl):
        pl.memset(ident[:], 1.0).then_inc(consts_made, 1)
        pl.memset(flip[:], 1.0).then_inc(consts_made, 1)
        pl.memset(row_ok[:], 1.0).then_inc(consts_made, 1)
        pl.wait_ge(consts_made, 3)
        pl.affine_select(out=ident[:], in_=ident[:], compare_op=ALU.is_equal, fill=0.0, base=0,
                         pattern=[[-1, P]], channel_multiplier=1).then_inc(consts_made, 1)
        pl.affine_select(out=flip[:], in_=flip[:], compare_op=ALU.is_equal, fill=0.0, base=1 - P,
                         pattern=[[1, P]], channel_multiplier=1).then_inc(consts_made, 1)
        pl.affine_select(out=row_ok[:], in_=row_ok[:], compare_op=ALU.is_ge, fill=0.0, base=-31,
                         pattern=[[0, 1]], channel_multiplier=1).then_inc(consts_made, 1)
        pl.wait_ge(aux_out, AUX.index("vec1") + 1)
        pl.dma_start(io["vec_dram"], vec[:]).then_inc(vec_stored, 16)
        pl.wait_ge(vec_stored, 16)
        for q in range(4):
            if q >= 2:
                pl.wait_ge(aux_made, AUX.index(f"bias{4 * q - 5}") + 1)
            src = bass.AP(io["vec_dram"].tensor, 4 * q * 5 * P, [[1, P], [5 * P, 4], [1, S]])
            pl.dma_start(hankel[q % 2][:], src).then_inc(hankel_loaded[q % 2], 16)
            if q == 1:
                pl.wait_ge(aux_out, AUX.index("ik") + 1)
                pl.dma_start(ikT[HD:P, :], ikT[0:HD, :]).then_inc(ik_copied, 16)
        for qi in range(1, NT):
            pl.wait_ge(idx_added, qi * NH)
            part = score[qi][:, qi * P:(qi + 1) * P]
            pl.affine_select(out=part, in_=part, compare_op=ALU.is_ge, fill=MASKED, base=0,
                             pattern=[[-1, P]], channel_multiplier=1).then_inc(causal_cut, 1)
        pl.wait_ge(aux_out, AUX.index("cv") + 1)
        for kv in range(2):
            for g in range(2):
                pl.dma_start(cT[0:HD, kv, g, :], craw[kv][g * HD:(g + 1) * HD, :]).then_inc(c_copied, 16)
                pl.dma_start(cT[HD:P, kv, g, 0:S - 1], craw[kv][g * HD:(g + 1) * HD, 1:S]).then_inc(c_copied, 16)
        pl.wait_ge(aux_made, AUX.index("hid") + 1)

        def add_mask(n):
            it = items[n]
            pl.wait_ge(sel_masked, it["qi"])
            pl.wait_ge(pT_made, n - 4)
            pl.tensor_tensor(logit[n % 5][:, 0:keys(it)], bias_of(it), score[it["qi"]][:], ALU.add)\
                .then_inc(mask_added, 1)

        for n in masks:
            add_mask(n)

    def tensor(te):
        def mm3(out, a, b, first, last):
            te.matmul(out, a[0], b[0], start=first, stop=False)
            te.matmul(out, a[0], b[1], start=False, stop=False)
            return te.matmul(out, a[1], b[0], start=False, stop=last)

        def transpose(out, a):
            n = a.shape[0]
            return te.matmul(out, a, ident[0:n, 0:n], is_transpose=True, start=True, stop=True)

        def transpose_twice(out, a):
            transpose(out[0:HD], a)
            n = a.shape[0]
            return te.matmul(out[HD:P], a, ident[0:n, 0:n], start=True, stop=True)

        def aux_begin(name):
            n = AUX.index(name)
            if n >= 2:
                te.wait_ge(aux_out, n - 1)
            return aux(name)

        def hT(k, lo, n):
            return hT_hi[:, k, lo:lo + n], hT_lo[:, k, lo:lo + n]

        def wt(u, kk, lo, n):
            return w_hi[u % 2][:, kk, lo:lo + n], w_lo[u % 2][:, kk, lo:lo + n]

        te.wait_ge(tab_loaded, 32)
        te.wait_ge(tab_masked, 1)
        te.matmul(aux_begin("vec0")[0:2 * NH, 0:512], tab[:], hot[:, 0:512], start=True, stop=True).then_inc(aux_made, 1)
        te.matmul(aux_begin("vec1")[0:2 * NH, 0:P], tab[:], hot[:, 512:5 * P], start=True, stop=True).then_inc(aux_made, 1)
        te.wait_ge(consts_made, 6)
        for j in range(8):
            t, half = j // 2, j % 2
            te.wait_ge(normed, t + 1)
            if j >= 4:
                te.wait_ge(hT_lo_out, j - 3)
            for c in range(4):
                last = transpose(bank[:, j % 4, c * P:(c + 1) * P], h_rows[:, t, (4 * half + c) * P:(4 * half + c + 1) * P])
            last.then_inc(hT_made, 1)
        te.wait_ge(hT_lo_out, 8)

        def project(g, u):
            half = u % 2
            te.wait_ge(w_lo_made, u + 1)
            extra = {G_CKV: [("ik", IK, HD)], G_CS: [("ck", 0, P), ("cv", P, P)]}.get(g, [])
            for name, lo, n in extra:
                dst = aux_begin(name) if half == 0 else aux(name)
                for kk in range(4):
                    k = 4 * half + kk
                    m = mm3(dst[0:n, :], wt(u, kk, lo, n), hT(k, 0, S), k == 0, k == 7)
                if half == 1:
                    m.then_inc(aux_made, 1)
            for t in range(4):
                if half == 0 and g > 0:
                    te.wait_ge(proj_out, 4 * (g - 1) + t + 1)
                for kk in range(4):
                    k = 4 * half + kk
                    if g == G_IQ:
                        m = mm3(bank[:, t, :], wt(u, kk, t * P, P), hT(k, 0, S), k == 0, k == 7)
                    else:
                        lo, n = {G_CKV: (0, P + NH), G_BQ: (0, 512), G_AQ: (0, 512), G_CS: (256, 256), G_W: (0, 280)}[g]
                        m = mm3(bank[:, t, 0:n], hT(k, t * P, P), wt(u, kk, lo, n), k == 0, k == 7)
                if half == 1 or t == 3:
                    m.then_inc(proj_step, 1)

        def project_group(g):
            project(g, 2 * g)
            project(g, 2 * g + 1)

        def flip_bias(heads):
            for h in heads:
                dst = aux_begin(f"bias{h}")
                te.wait_ge(hankel_loaded[(h // 4) % 2], 16 * (h // 8 + 1))
                te.matmul(dst, flip[:], hankel[(h // 4) % 2][:, h % 4, :], start=True, stop=True).then_inc(aux_made, 1)

        def transpose_q(name, rows):
            for c in range(4):
                dst = aux_begin(f"{name}{c}")
                for t in range(NT):
                    m = transpose(dst[:, t * P:(t + 1) * P], rows[:, t * NH + 2 * c:t * NH + 2 * c + 2, :].rearrange("p h d -> p (h d)"))
                m.then_inc(aux_made, 1)

        project_group(G_CKV)
        project_group(G_IQ)
        te.wait_ge(normed, NT + 1)
        dst = aux_begin("ckvT")
        for t in range(NT):
            m = transpose(dst[:, t * P:(t + 1) * P], ckv_rows[:, t, :])
        m.then_inc(aux_made, 1)
        dst = aux_begin("kv")
        te.wait_ge(small_loaded, SMALL_LOADS * 16)
        te.wait_ge(aux_out, AUX.index("ckvT") + 1)
        for t in range(NT):
            m = te.matmul(dst[:, t * P:(t + 1) * P], ckvT[:, t * P:(t + 1) * P], w_ukv[:], start=True, stop=True)
        m.then_inc(aux_made, 1)
        flip_bias(range(0, 8))
        project_group(G_BQ)
        flip_bias(range(8, 16))
        project_group(G_AQ)
        te.wait_ge(normed, NT + 2)
        transpose_q("bqT", bq_rows)
        te.wait_ge(proj_out, 8)
        te.wait_ge(ik_copied, 16)
        for n in range(N_RELU):
            qi, h = n // NH + 1, n % NH
            if n >= 2:
                te.wait_ge(idx_relu, n - 1)
            half = slice((h % 2) * HD, (h % 2) * HD + HD)
            te.matmul(bank[:, 4 + n % 2, 0:(qi + 1) * P], iqT[half, h // 2, qi * P:(qi + 1) * P],
                      ikT[half, 0:(qi + 1) * P], start=True, stop=True).then_inc(idx_made, 1)
        project_group(G_CS)
        te.wait_ge(normed, NT + 3)
        transpose_q("aqT", aq_rows)
        project_group(G_W)
        te.wait_ge(w1_loaded, 32)
        te.wait_ge(windows_made, 4)
        dst = aux_begin("hid")
        for kv in range(2):
            for c in range(16):
                m = te.matmul(dst[:, 62 * kv:62 * kv + 62], w1[:, kv, c, :], windows[:, kv, c, :],
                              start=c == 0, stop=c == 15)
        m.then_inc(aux_made, 1)

        def transpose_k(j):
            dst = aux_begin(f"kT{j}")
            for t in range(NT):
                m = transpose_twice(dst[:, t * P:(t + 1) * P], k_rows[:, t, j, :])
            m.then_inc(aux_made, 1)

        te.wait_ge(normed, NT + 4)
        transpose_k(0)
        transpose_k(1)
        dst = aux_begin("kcvc")
        for kv in range(2):
            for g in range(2):
                m = te.matmul(dst[0:N_CMP, (2 * kv + g) * HD:(2 * kv + g + 1) * HD], hidT[:, kv, g, :], w2[:, kv, :],
                              start=True, stop=True)
        m.then_inc(aux_made, 1)
        for j in range(2, 5):
            transpose_k(j)
        dst = aux_begin("kcT")
        te.wait_ge(normed, NT + 5)
        for g in range(2):
            m = transpose_twice(dst[:, g * 32:g * 32 + N_CMP], kc_rows[:, g, :])
        m.then_inc(aux_made, 1)

        te.wait_ge(aux_out, len(AUX))
        te.wait_ge(proj_out, 4 * NG)
        te.wait_ge(idx_relu, N_RELU)

        def scores(n):
            it = items[n]
            if n >= AHEAD:
                te.wait_ge(logit_made, n - AHEAD + 1)
            q0 = it["qi"] * P
            for h in ((0, 2, 1, 3) if it["kind"] == "cmp" else [it["h"]]):
                if it["kind"] == "cmp" and h == 1:
                    te.wait_ge(even_heads, it["group"] + 1)
                head = 4 * it["g4"] + h
                half = slice((head % 2) * HD, (head % 2) * HD + HD)
                q = (bqT if it["kind"] == "dsa" else aqT)[half, head // 2, q0:q0 + P]
                if it["kind"] == "cmp":
                    m = te.matmul(sview(n)[:, h, :], q, kcT[half, it["g4"], 0:keys(it)], start=True, stop=True)
                    if h == 2:
                        m.then_inc(even_heads, 1)
                else:
                    j = {"sel": it["g4"], "win": 2 + it["g4"], "dsa": 4}[it["kind"]]
                    m = te.matmul(s_bank(n)[:, 0:keys(it)], q, kT[half, j, 0:keys(it)], start=True, stop=True)
            m.then_inc(s_made, 1)

        def transposes(n):
            it = items[n]
            if n in ACT_SCALED:
                te.wait_ge(p_scaled_act, scaled_by(ACT_SCALED, n))
            else:
                te.wait_ge(p_scaled, n + 1 - scaled_by(ACT_SCALED, n))
            if n >= 2:
                te.wait_ge(pT_out, n - 1)
            b = pT_bank(n)
            if it["kind"] == "cmp":
                for h in range(4):
                    m = transpose(b[0:keys(it), h * P:(h + 1) * P], cview(n)[:, h, :])
            else:
                for kb in range(it["qi"] + 1):
                    m = transpose(b[:, kb * P:(kb + 1) * P], logit[n % 5][:, kb * P:(kb + 1) * P])
            m.then_inc(pT_made, 1)

        def weigh_values(b):
            ba = batches[b]
            gr = groups[ba["group"]]
            if ba["kind"] in ("cmp", "dsa") and ba["group"] >= 2:
                te.wait_ge(o_lo_out, ba["group"] - 1)
            te.wait_ge(pT_out, ba["last"] + 1)
            dst = bank[:, 6 + ba["group"] % 2, 0:2 * P]
            only = ba["kind"] == "dsa"
            n_kb = 1 if ba["kind"] == "cmp" else ba["qi"] + 1
            for kb in range(n_kb):
                for half in range(2):
                    g = slice(ba["g4"] * HD, ba["g4"] * HD + HD)
                    if ba["kind"] == "cmp":
                        nk = keys(ba)
                        v, p = vc[0:nk, ba["g4"], :], pT[b % 2][0:nk, 0, half:4:2, :]
                    else:
                        v = {"sel": v_sel[:, kb, g], "win": v_win[:, kb, g], "dsa": v_dsa[:, kb, :]}[ba["kind"]]
                        p = pT[b % 2][:, kb, half:4:2, :]
                    m = te.matmul(dst[half * HD:(half + 1) * HD, :].rearrange("p (h q) -> p h q", h=2), v, p,
                                  start=kb == 0 and ba["kind"] in ("cmp", "dsa"),
                                  stop=kb == n_kb - 1 and ba["kind"] in ("win", "dsa"))
            m.then_inc(pv_made, 1)

        for n in range(AHEAD):
            scores(n)
        for n in range(N_ITEMS + 1):
            if n < N_ITEMS:
                transposes(n)
            if n + AHEAD < N_ITEMS:
                scores(n + AHEAD)
            if n >= 1 and items[n - 1]["end"]:
                weigh_values(items[n - 1]["batch"])

        def merge_group(m_):
            kind, ab, c, us = MERGE[m_]
            g = NG + m_
            first_bank = 4 * (m_ % 2)
            if m_ >= 2:
                k2, _, c2, _ = MERGE[m_ - 2]
                te.wait_ge(*((gate_out, 4 * (2 * c2 + m_ % 2 + 1)) if k2 == GATE else (branch_out, 4 * (2 * c2 + m_ % 2 + 1))))
            for i, u in enumerate(us):
                te.wait_ge(w_lo_made, u + 1)
                for t in range(NT):
                    if kind == OUT and c == 0 and i == 0:
                        te.wait_ge(mT_lo_out, 2 * t + 2)
                    dst = bank[:, first_bank + t, :]
                    for kk in range(4):
                        first, last = i == 0 and kk == 0, u == us[-1] and kk == 3
                        if kind == GATE:
                            a = hT(4 * i + kk, t * P, P)
                        elif kind == BRANCH:
                            a = (oT_hi[:, 4 * ab + kk, t * P:(t + 1) * P], oT_lo[:, 4 * ab + kk, t * P:(t + 1) * P])
                        else:
                            a = (mT_hi[:, 4 * i + kk, t * P:(t + 1) * P], mT_lo[:, 4 * i + kk, t * P:(t + 1) * P])
                        m = mm3(dst, a, wt(u, kk, 0, 512), first, last)
                    if u == us[-1] or t == 3:
                        m.then_inc(proj_step, 1)

        te.wait_ge(o_lo_out, len(groups))
        for m_ in range(8):
            merge_group(m_)
        for j in range(8):
            t, half = j // 2, j % 2
            te.wait_ge(branch_out, 12 + t + 1)
            for c in range(4):
                m = transpose(bank[:, j, c * P:(c + 1) * P], merged[:, t, (4 * half + c) * P:(4 * half + c + 1) * P])
            m.then_inc(mT_made, 1)
        merge_group(8)
        merge_group(9)
        mem["transpose"] = transpose

    def scalar(ac):
        smalls = [
            (bq_gain[:], io["dsa_q_norm"][0].partition_broadcast(P)),
            (aq_gain[:], io["nsa_q_norm"][0].partition_broadcast(P)),
            (ckv_gain[:], io["dsa_kv_norm"][0].partition_broadcast(P)),
            (w_ukv[:, 0:HD], io["dsa_w_uk"][0]), (w_ukv[:, HD:2 * HD], io["dsa_w_uv"][0]),
            (w2[:, 0, :], io["cmp_k_w2"][0]), (w2[:, 1, :], io["cmp_v_w2"][0]),
            (pe[:], io["pe_cols"]), (b1[:], io["b1_cols"]),
            (k_gain[:, 4, :], io["dsa_k_norm"][0].partition_broadcast(P)),
        ] + [(k_gain[:, j, :], io["nsa_k_norm"][0].partition_broadcast(P)) for j in range(4)]
        assert len(smalls) == SMALL_LOADS
        ac.dma_start(tab[0:N_BUCKETS, :], io["rel_bias"]).then_inc(tab_loaded, 16)
        ac.dma_start(hot[:], io["bias_hot"]).then_inc(tab_loaded, 16)
        for dst, src in smalls:
            ac.dma_start(dst, src).then_inc(small_loaded, 16)

        def aux_copy(name, dst, src, func=ACT.Copy, inc=True, **kw):
            ac.wait_ge(aux_made, AUX.index(name) + 1)
            i = ac.activation(dst, src, func, **kw)
            if inc:
                i.then_inc(aux_out, 1)

        def root(n, cols, rows=P):
            ac.wait_ge(mean_made, n)
            ac.activation(stat[0:rows, 2, 0:cols], stat[0:rows, 1, 0:cols], ACT.Sqrt).then_inc(root_made, 1)

        def split_unit(u):
            n = unit_width(u)
            ac.wait_ge(w_loaded[u % 3], unit_loaded(u))
            if u >= 2:
                ac.wait_ge(proj_step, unit_used(u - 2))
            ac.activation(w_hi[u % 2][:, :, 0:n], w_raw[u % 3][:, :, 0:n], ACT.Copy).then_inc(w_hi_made, 1)

        for t in range(NT):
            ac.wait_ge(x_loaded[t], 16)
            if t >= 1:
                ac.wait_ge(squared, t)
            ac.activation(square[:], x_in[:, t, :], ACT.Square, accum_out=stat[:, 0, t:t + 1]).then_inc(squared, 1)
            ac.wait_ge(h_mean, t + 1)
            ac.activation(stat[:, 2, t:t + 1], stat[:, 1, t:t + 1], ACT.Sqrt).then_inc(h_root, 1)
        aux_copy("vec0", vec[:, 0:512], aux("vec0")[0:2 * NH, 0:512])
        aux_copy("vec1", vec[:, 512:5 * P], aux("vec1")[0:2 * NH, 0:P])
        split_unit(0)
        for j in range(8):
            t, half = j // 2, j % 2
            ac.wait_ge(hT_made, j + 1)
            ac.activation(hT_hi[:, 4 * half:4 * half + 4, t * P:(t + 1) * P],
                          bank[:, j % 4, :].rearrange("p (c q) -> p c q", c=4), ACT.Copy).then_inc(hT_hi_out, 1)
        split_unit(1)

        def wait_bank(g, t):
            ac.wait_ge(proj_step, bank_made(g, t))

        def square_rows(rows):
            ac.activation(junk[:, 0:rows.shape[1] * rows.shape[2]].rearrange("p (a b) -> p a b", a=rows.shape[1]),
                          rows, ACT.Square).then_inc(squared, 1)

        for g in range(NG):
            if g + 1 < NG:
                split_unit(2 * g + 2)
            for t in range(NT):
                wait_bank(g, t)
                b = bank[:, t, :]
                if g == G_CKV:
                    if t == 0:
                        ac.wait_ge(hT_lo_out, 8)
                    ac.activation(ckv_rows[:, t, :], b[:, 0:P], ACT.Copy).then_inc(act_step, 1)
                    ac.activation(iw[:, t, :], b[:, P:P + NH], ACT.Copy, scale=NH ** -0.5).then_inc(proj_out, 1)
                elif g == G_IQ:
                    ac.activation(iqT[:, t, :], b, ACT.Copy).then_inc(proj_out, 1)
                elif g in (G_BQ, G_AQ):
                    rows = bq_rows if g == G_BQ else aq_rows
                    ac.activation(rows[:, t * NH:(t + 1) * NH, :], b.rearrange("p (h d) -> p h d", h=NH), ACT.Copy).then_inc(proj_out, 1)
                elif g == G_CS:
                    ac.activation(k_rows[:, t, 0:2, :], b[:, 0:P].rearrange("p (h d) -> p h d", h=2), ACT.Copy).then_inc(act_step, 1)
                    ac.activation(v_sel[:, t, :], b[:, P:2 * P], ACT.Copy).then_inc(proj_out, 1)
                else:
                    ac.activation(k_rows[:, t, 2:4, :], b[:, 0:P].rearrange("p (h d) -> p h d", h=2), ACT.Copy).then_inc(act_step, 1)
                    ac.activation(v_win[:, t, :], b[:, P:2 * P], ACT.Copy).then_inc(act_step, 1)
                    ac.activation(gates[:, t, :], b[:, 2 * P:2 * P + 3 * NH], ACT.Sigmoid).then_inc(proj_out, 1)
            if g + 1 < NG:
                split_unit(2 * g + 3)
            if g == G_CKV:
                ac.wait_ge(act_step, 4)
                square_rows(ckv_rows[:])
                root(1, NT)
                aux_copy("ik", ikT[0:HD, :], aux("ik")[0:HD, :])
            elif g == G_IQ:
                aux_copy("ckvT", ckvT[:], aux("ckvT"))
                v = aux("kv").rearrange("p (t n) -> p t n", t=NT)
                aux_copy("kv", k_rows[:, :, 4, :], v[:, :, 0:HD], inc=False)
                aux_copy("kv", v_dsa[:], v[:, :, HD:2 * HD])
                for h in range(8):
                    aux_copy(f"bias{h}", bias[:, h, :], aux(f"bias{h}"))
            elif g == G_BQ:
                ac.wait_ge(proj_out, 12)
                square_rows(bq_rows[:])
                for h in range(8, 16):
                    aux_copy(f"bias{h}", bias[:, h, :], aux(f"bias{h}"))
                root(2, NT * NH)
            elif g == G_AQ:
                ac.wait_ge(proj_out, 16)
                square_rows(aq_rows[:])
                for c in range(4):
                    aux_copy(f"bqT{c}", bqT[:, c, :], aux(f"bqT{c}"))
                root(3, NT * NH)
                ac.wait_ge(aux_made, AUX.index("bqT3") + 1)
                for n in range(N_RELU):
                    w = (n // NH + 2) * P
                    ac.wait_ge(idx_made, n + 1)
                    if n >= 2:
                        ac.wait_ge(idx_added, n - 1)
                    ac.activation(idx_act[n % 2][:, 0:w], bank[:, 4 + n % 2, 0:w], ACT.Relu, scale=HD ** -0.5).then_inc(idx_relu, 1)
            elif g == G_CS:
                ac.wait_ge(mean_made, 3)
                aux_copy("ck", craw[0][:], aux("ck"))
                aux_copy("cv", craw[1][:], aux("cv"))
                for c in range(4):
                    aux_copy(f"aqT{c}", aqT[:, c, :], aux(f"aqT{c}"))
        ac.wait_ge(act_step, 4 + 4 + 8)
        ac.wait_ge(proj_out, 24)
        ac.activation(k_square[:], k_rows[:].rearrange("p t j d -> p (t j) d"), ACT.Square).then_inc(squared, 1)
        root(4, NT * 5)
        for kv in range(2):
            ac.wait_ge(aux_made, AUX.index("hid") + 1)
            i = ac.activation(hidT[:, kv].rearrange("p g j -> p (g j)"), aux("hid")[:, 62 * kv:62 * kv + 62],
                              ACT.Gelu_apprx_tanh, bias=b1[:, kv:kv + 1])
        i.then_inc(aux_out, 1)

        def copy_kT(j):
            if j == 0:
                ac.wait_ge(mean_made, 4)
            aux_copy(f"kT{j}", kT[:, j, :], aux(f"kT{j}"))

        copy_kT(0)
        copy_kT(1)
        v = aux("kcvc")[0:N_CMP, 0:2 * P].rearrange("p (a d) -> p a d", a=4)
        aux_copy("kcvc", kc_rows[:], v[:, 0:2, :], inc=False)
        aux_copy("kcvc", vc[:], v[:, 2:4, :])
        ac.wait_ge(aux_out, AUX.index("kcvc") + 1)
        ac.activation(junk[0:N_CMP, 0:P].rearrange("p (a b) -> p a b", a=2), kc_rows[:], ACT.Square).then_inc(squared, 1)
        root(5, 2, N_CMP)
        for j in range(2, 5):
            copy_kT(j)
        aux_copy("kcT", kcT[:], aux("kcT")[:, 0:64].rearrange("p (g j) -> p g j", g=2)[:, :, 0:N_CMP])

        def move_pT(n):
            it = items[n]
            ac.wait_ge(pT_made, n + 1)
            if it["start"] and it["batch"] >= 2:
                ac.wait_ge(pv_made, it["batch"] - 1)
            if it["kind"] == "cmp":
                dst, src = pT[it["batch"] % 2][0:keys(it), 0, :, :], pT_bank(n)[0:keys(it), :].rearrange("p (h q) -> p h q", h=4)
            else:
                n_kb = it["qi"] + 1
                dst = pT[it["batch"] % 2][:, 0:n_kb, it["h"], :]
                src = pT_bank(n)[:, 0:n_kb * P].rearrange("p (k q) -> p k q", k=n_kb)
            ac.activation(dst, src, ACT.Copy).then_inc(pT_out, 1)

        for n in range(N_ITEMS + 5):
            if n < N_ITEMS:
                it = items[n]
                ac.wait_ge(logit_made, n + 1)
                if it["kind"] == "cmp":
                    ac.activation(cview(n), cview(n), ACT.Exp).then_inc(exp_made, 1)
                else:
                    v = logit[n % 5][:, 0:keys(it)]
                    c = it["col"]
                    ac.activation(v, v, ACT.Exp, bias=neg_max[:, c:c + 1], scale=-1.0,
                                  accum_out=row_sum[:, c:c + 1]).then_inc(exp_made, 1)
            if n - 1 in ACT_SCALED:
                v, c = logit[(n - 1) % 5][:, 0:keys(items[n - 1])], items[n - 1]["col"]
                ac.wait_ge(coef_made, scaled_by(ACT_SCALED, n - 1))
                ac.activation(v, v, ACT.Copy, scale=coef[:, c:c + 1]).then_inc(p_scaled_act, 1)
            if 2 <= n < N_ITEMS + 2:
                move_pT(n - 2)
            if n >= 4:
                for g, gr in enumerate(groups):
                    if gr["last"] == n - 4:
                        ac.wait_ge(pv_made, sum(1 for b in batches if b["group"] <= g))
                        ac.activation(*o_view(oT_hi, g), ACT.Copy).then_inc(o_hi_out, 1)
            if n == EARLY_SPLIT:
                split_unit(P1_UNITS)

        for m_, (kind, ab, c, us) in enumerate(MERGE):
            if m_ == 0:
                split_unit(us[1])
            following = MERGE[m_ + 1][3] if m_ + 1 < len(MERGE) else []
            for u in following[:1]:
                split_unit(u)
            if kind == GATE:
                for t in range(NT):
                    wait_bank(NG + m_, t)
                    if c == 1 and t == 0:
                        ac.wait_ge(branch_out, 4 * (ab + 1))
                    ac.activation(sig[:, ab, t, :], bank[:, 4 * (m_ % 2) + t, :], ACT.Sigmoid).then_inc(gate_out, 1)
            if m_ != 7:
                for u in following[1:]:
                    split_unit(u)
            if m_ == 7:
                for j in range(8):
                    t, half = j // 2, j % 2
                    ac.wait_ge(mT_made, j + 1)
                    ac.activation(mT_hi[:, 4 * half:4 * half + 4, t * P:(t + 1) * P],
                                  bank[:, j, :].rearrange("p (c q) -> p c q", c=4), ACT.Copy).then_inc(mT_hi_out, 1)
                for u in following[1:]:
                    split_unit(u)

    def o_view(dst, g):
        gr = groups[g]
        c0 = (0 if gr["mixer"] == "nsa" else 4) + 2 * gr["g4"]
        return (dst[:, c0:c0 + 2, gr["qi"] * P:(gr["qi"] + 1) * P],
                bank[:, 6 + g % 2, 0:2 * P].rearrange("p (h q) -> p h q", h=2))

    def vector(ve):
        count = [0]

        def step(instruction):
            count[0] += 1
            instruction.then_inc(dve_step, 1)
            ve.wait_ge(dve_step, count[0])

        def mean(n, cols, width, rows=P):
            ve.tensor_scalar(stat[0:rows, 1, 0:cols], stat[0:rows, 0, 0:cols], 1.0 / width, EPS, ALU.mult, ALU.add)\
                .then_inc(mean_made, 1)

        def inverse(n, cols, rows=P):
            ve.wait_ge(root_made, n)
            step(ve.reciprocal(stat[0:rows, 3, 0:cols], stat[0:rows, 2, 0:cols]))

        def norm_rows(n, rows, gain, sq=None, parts=P):
            _, a, b = rows.shape
            sq = junk[:, 0:a * b].rearrange("p (a b) -> p a b", a=a) if sq is None else sq
            ve.wait_ge(squared, NT - 1 + n + 1)
            step(ve.reduce_sum(stat[0:parts, 0, 0:a], sq, axis=AX.X))
            mean(n, a, b, parts)
            inverse(n, a, parts)
            step(ve.tensor_tensor(rows, rows, stat[0:parts, 3, 0:a].unsqueeze(2).to_broadcast([parts, a, b]), ALU.mult))
            ve.tensor_tensor(rows, rows, gain, ALU.mult).then_inc(normed, 1)

        def split_unit(u):
            n = unit_width(u)
            ve.wait_ge(w_hi_made, u + 1)
            ve.tensor_tensor(w_lo[u % 2][:, :, 0:n], w_raw[u % 3][:, :, 0:n], w_hi[u % 2][:, :, 0:n].bitcast(F32),
                             ALU.subtract).then_inc(w_lo_made, 1)

        def top8_of(r):
            if r % ROUNDS == 0:
                ve.wait_ge(causal_cut, r // ROUNDS + 1)
            step(ve.max(top8[:], score[r // ROUNDS + 1][:]))

        def take_top8(r):
            sc = score[r // ROUNDS + 1][:]
            step(ve.match_replace(sc, top8[:], sc, TAKEN))
            if r % ROUNDS == ROUNDS - 1:
                ve.tensor_scalar(sc, sc, TAKEN / 2, MASKED, ALU.is_gt, ALU.mult).then_inc(sel_masked, 1)

        mem["step"] = step
        ve.memset(tab[N_BUCKETS:N_BUCKETS + 1, :], MASKED).then_inc(tab_masked, 1)
        for t in range(NT):
            ve.wait_ge(squared, t + 1)
            ve.tensor_scalar(stat[:, 1, t:t + 1], stat[:, 0, t:t + 1], 1.0 / D, EPS, ALU.mult, ALU.add).then_inc(h_mean, 1)
            ve.wait_ge(h_root, t + 1)
            step(ve.reciprocal(stat[:, 3, t:t + 1], stat[:, 2, t:t + 1]))
            ve.wait_ge(gain_loaded, 16)
            ve.scalar_tensor_tensor(h_rows[:, t, :], x_in[:, t, :], stat[:, 3, t:t + 1], attn_gain[:], ALU.mult, ALU.mult)\
                .then_inc(normed, 1)
        ve.wait_ge(small_loaded, 16 * SMALL_LOADS)
        ve.tensor_scalar(bq_gain[:], bq_gain[:], HD ** -0.5, None, ALU.mult).then_inc(gains_scaled, 1)
        ve.tensor_scalar(aq_gain[:], aq_gain[:], HD ** -0.5, None, ALU.mult).then_inc(gains_scaled, 1)
        split_unit(0)
        for j in range(8):
            t, half = j // 2, j % 2
            ve.wait_ge(hT_hi_out, j + 1)
            v = (slice(None), slice(4 * half, 4 * half + 4), slice(t * P, (t + 1) * P))
            ve.tensor_tensor(hT_lo[v], bank[:, j % 4, :].rearrange("p (c q) -> p c q", c=4), hT_hi[v].bitcast(F32),
                             ALU.subtract).then_inc(hT_lo_out, 1)
        split_unit(1)
        split_unit(2)
        split_unit(3)
        norm_rows(1, ckv_rows[:], ckv_gain[:].unsqueeze(1).to_broadcast([P, NT, P]))
        split_unit(4)
        split_unit(5)
        split_unit(6)
        split_unit(7)
        ve.wait_ge(gains_scaled, 2)
        norm_rows(2, bq_rows[:], bq_gain[:].unsqueeze(1).to_broadcast([P, NT * NH, HD]))
        split_unit(8)
        split_unit(9)
        norm_rows(3, aq_rows[:], aq_gain[:].unsqueeze(1).to_broadcast([P, NT * NH, HD]))
        for n in range(N_RELU):
            qi, h = n // NH + 1, n % NH
            w = (qi + 1) * P
            ve.wait_ge(idx_relu, n + 1)
            if h == 0:
                if qi == 1:
                    ve.wait_ge(aux_made, AUX.index("bias15") + 1)
                ve.tensor_scalar(score[qi][:], idx_act[n % 2][:, 0:w], iw[:, qi, h:h + 1], None, ALU.mult).then_inc(idx_added, 1)
            else:
                ve.wait_ge(idx_added, n)
                ve.scalar_tensor_tensor(score[qi][:], idx_act[n % 2][:, 0:w], iw[:, qi, h:h + 1], score[qi][:],
                                        ALU.mult, ALU.add).then_inc(idx_added, 1)
        split_unit(10)
        split_unit(11)
        ve.wait_ge(idx_made, N_RELU)
        ve.wait_ge(c_copied, 8 * 16)
        for kv in range(2):
            for a in range(2):
                src = cT[:, kv, :, 16 * a:16 * a + 16 * N_CMP].rearrange("p g (j b two) -> p b g j two", b=8, two=2)[:, :, :, :, 0]
                ve.tensor_tensor(windows[:, kv, 8 * a:8 * a + 8, :].rearrange("p b (g j) -> p b g j", g=2), src,
                                 pe[:, kv, 8 * a:8 * a + 8].unsqueeze(2).unsqueeze(3).to_broadcast([P, 8, 2, N_CMP]),
                                 ALU.add).then_inc(windows_made, 1)
        k_flat = k_rows[:].rearrange("p t j d -> p (t j) d")
        ve.wait_ge(squared, NT + 4)
        step(ve.reduce_sum(stat[:, 0, 0:5 * NT], k_square[:], axis=AX.X))
        mean(4, 5 * NT, HD)
        inverse(4, 5 * NT)
        step(ve.tensor_tensor(k_flat, k_flat, stat[:, 3, 0:5 * NT].unsqueeze(2).to_broadcast([P, 5 * NT, HD]), ALU.mult))
        ve.tensor_tensor(k_rows[:], k_rows[:], k_gain[:].unsqueeze(1).to_broadcast([P, NT, 5, HD]), ALU.mult).then_inc(normed, 1)
        for n in range(EARLY_ROUNDS):
            top8_of(n)
            take_top8(n)
        norm_rows(5, kc_rows[:], k_gain[0:N_CMP, 0:2, :], sq=junk[0:N_CMP, 0:P].rearrange("p (a b) -> p a b", a=2), parts=N_CMP)

        def make_logit(n):
            it = items[n]
            w = keys(it)
            if n in masks:
                ve.wait_ge(mask_added, masks.index(n) + 1)
            elif n >= 5:
                ve.wait_ge(pT_made, n - 4)
            ve.wait_ge(s_made, n + 1)
            c = it["col"]
            if it["kind"] == "cmp":
                step(ve.tensor_tensor(cview(n), sview(n), bias_of(it), ALU.add))
                step(ve.reduce_max(neg_max[:, c:c + 4], cview(n), axis=AX.X))
                ve.tensor_tensor(cview(n), cview(n), neg_max[:, c:c + 4].unsqueeze(2).to_broadcast([P, 4, w]), ALU.subtract)\
                    .then_inc(logit_made, 1)
            else:
                add = logit[n % 5][:, 0:w] if n in masks else bias_of(it)
                ve.tensor_tensor_reduce(out=logit[n % 5][:, 0:w], in0=s_bank(n)[:, 0:w], in1=add, scale=-1.0,
                                        scalar=-TAKEN, op0=ALU.add, op1=ALU.min, accum_out=neg_max[:, c:c + 1])\
                    .then_inc(logit_made, 1)

        def scale_p(n):
            it = items[n]
            c, w = it["col"], it["cols"]
            ve.wait_ge(exp_made, n + 1)
            co = coef[:, c:c + w]
            if it["kind"] == "cmp":
                step(ve.reduce_sum(row_sum[:, c:c + 4], cview(n), axis=AX.X))
            step(ve.reciprocal(co, row_sum[:, c:c + w]))
            if it["kind"] == "cmp":
                h0 = 12 * it["g4"]
                step(ve.tensor_tensor(co, co, gates[:, it["qi"], h0:h0 + 10:3], ALU.mult))
                if it["qi"] == 0:
                    step(ve.tensor_scalar(co, co, row_ok[:], None, ALU.mult))
                ve.tensor_tensor(cview(n), cview(n), co.unsqueeze(2).to_broadcast([P, 4, keys(it)]), ALU.mult)\
                    .then_inc(p_scaled, 1)
            else:
                v = logit[n % 5][:, 0:keys(it)]
                g = 3 * it["head"] + {"sel": 1, "win": 2}.get(it["kind"], 0)
                gate = gates[:, it["qi"], g:g + 1]
                if n in ACT_SCALED:
                    ve.tensor_scalar(co, co, gate, None, ALU.mult).then_inc(coef_made, 1)
                elif it["kind"] == "dsa":
                    ve.tensor_scalar(v, v, co, None, ALU.mult).then_inc(p_scaled, 1)
                else:
                    ve.tensor_scalar(v, v, co, gate, ALU.mult, ALU.mult).then_inc(p_scaled, 1)

        ve.wait_ge(idx_made, N_RELU)
        ve.wait_ge(proj_out, 4 * NG)
        ve.wait_ge(aux_out, len(AUX))
        for n in range(N_ITEMS + 5):
            if EARLY_ROUNDS + n < 3 * ROUNDS:
                top8_of(EARLY_ROUNDS + n)
            if n < N_ITEMS:
                make_logit(n)
            if EARLY_ROUNDS + n < 3 * ROUNDS:
                take_top8(EARLY_ROUNDS + n)
            if 1 <= n <= N_ITEMS:
                scale_p(n - 1)
            if n >= 4:
                for g, gr in enumerate(groups):
                    if gr["last"] == n - 4:
                        ve.wait_ge(o_hi_out, g + 1)
                        dst, src = o_view(oT_lo, g)
                        ve.tensor_tensor(dst, src, o_view(oT_hi, g)[0].bitcast(F32), ALU.subtract).then_inc(o_lo_out, 1)
            if n == EARLY_SPLIT:
                split_unit(P1_UNITS)

        for m_, (kind, ab, c, us) in enumerate(MERGE):
            if m_ == 0:
                split_unit(us[1])
            following = MERGE[m_ + 1][3] if m_ + 1 < len(MERGE) else []
            for u in following[:1]:
                split_unit(u)
            if m_ == len(MERGE) - 1:
                mem["split_biases"](ve)
            cols = slice(c * 512, c * 512 + 512)
            for t in range(NT):
                src = bank[:, 4 * (m_ % 2) + t, :]
                if kind == BRANCH:
                    ve.wait_ge(gate_out, 4 * (2 * c + ab) + t + 1)
                    ve.wait_ge(proj_step, bank_made(NG + m_, t))
                    if ab == 0:
                        ve.tensor_tensor(merged[:, t, cols], src, sig[:, 0, t, :], ALU.mult).then_inc(branch_out, 1)
                    else:
                        step(ve.tensor_tensor(sig[:, 1, t, :], src, sig[:, 1, t, :], ALU.mult))
                        ve.tensor_tensor(merged[:, t, cols], merged[:, t, cols], sig[:, 1, t, :], ALU.add).then_inc(branch_out, 1)
                elif kind == OUT:
                    ve.wait_ge(x_reloaded, 16)
                    ve.wait_ge(proj_step, bank_made(NG + m_, t))
                    ve.tensor_tensor(x2[:, t, cols], src, x2[:, t, cols], ALU.add).then_inc(x2_made, 1)
                    if c == 1 and t > 0:
                        mem["norm_x2"](ve, t - 1)
            if m_ == 7:
                for j in range(8):
                    t, half = j // 2, j % 2
                    ve.wait_ge(mT_hi_out, j + 1)
                    v = (slice(None), slice(4 * half, 4 * half + 4), slice(t * P, (t + 1) * P))
                    ve.tensor_tensor(mT_lo[v], bank[:, j, :].rearrange("p (c q) -> p c q", c=4), mT_hi[v].bitcast(F32),
                                     ALU.subtract).then_inc(mT_lo_out, 1)
            for u in following[1:]:
                split_unit(u)

    mem.update(proj_step=proj_step, mT_lo_out=mT_lo_out, w_lo_made=w_lo_made, n_units=N_UNITS,
               after_branches=steps_before[NG + 8], after_out=steps_before[NG + 10])
    return dict(sync=sync, pool=pool, tensor=tensor, scalar=scalar, vector=vector)


def moe(nc, io, out, sb, sem, bank, mem):
    ident, x2 = mem["ident"], mem["x2"]
    dve_step = mem["dve_step"]
    tri = sb("tri", [P, P], 0)
    ones = sb("ones", [P, P], 0.5)
    tokT = sb("tokT", [P, P], 1.5, I32)
    gateT = sb("gateT", [P, P], 2)
    hot64 = sb("hot64", [2 * NE, NE], 2.5)
    b_raw = sb("b_raw", [2 * NE, 3 * D], 4)
    b_parts = sb("b_parts", [2 * NE, 3 * D], 188, F32R)
    ffn_gain = sb("ffn_gain", [P, D], 124)
    square = sb("ffn_square", [P, D], 128)
    h2 = sb("h2", [P, NT, D], 108)
    h2T = sb("h2T", [P, DC, S], 156)
    w_router = sb("w_router_sb", [P, DC, NE], 132)
    b_router = sb("b_router_sb", [P, NE], 133)
    fstat = sb("fstat", [P, 4, NT], 133.25)
    onehot = sb("onehot", [P, NT, TOPK, NE], 200)
    picked = sb("picked", [P, NT, TOPK, NE], 202)
    logits = sb("logits", [P, NT, NE], 204)
    chosen = sb("chosen", [P, NT, NE], 204.5)
    place = sb("place", [P, NT, NE], 205)
    top_val = sb("top_val", [P, NT, 8], 205.5)
    top_idx = sb("top_idx", [P, NT, 8], 205.75, U32)
    top_f = sb("top_f", [P, NT, TOPK], 206)
    gate = sb("gate", [P, NT, TOPK], 206.125)
    gate_sum = sb("gate_sum", [P, NT], 206.25)
    row_of = sb("row_of", [P, NT * TOPK], 206.375)
    token_i = sb("token_i", [P, NT, TOPK], 206.5, I32)
    token_f = sb("token_f", [P, NT, TOPK], 206.625)
    gate_lo = sb("gate_lo", [P, NT, TOPK], 206.75)
    gate_hi = sb("gate_hi", [P, NT, TOPK], 206.875, F32R)
    iota_row_i = sb("iota_row_i", [P, S], 136, I32)
    iota_row = sb("iota_row", [P, S], 100)
    row_hot = sb("row_hot", [P, NT * TOPK, S], 68, F32R)
    entries = sb("entries", [P, NT * TOPK, 3, NE], 102, F32R)
    table = sb("table", [3 * NE, S], 140)
    busiest_f = sb("busiest_f", [P, 1], 3.75)
    busiest = sb("busiest", [P, 1], 3.78125, I32)
    RAW, SPLIT = 8, 4
    raw = [sb(f"raw{i}", [P, 2048], 20 + 8 * i if i < 6 else 172 + 8 * (i - 6)) for i in range(RAW)]
    hi = [sb(f"hi{i}", [P, 2048], 68 + 8 * i, F32R) for i in range(SPLIT)]
    lo = [sb(f"lo{i}", [P, 2048], 100 + 8 * i, F32R) for i in range(SPLIT)]
    xg = [sb(f"xg{i}", [P, D], 132 + 4 * i) for i in range(2)]
    xT_hi = [sb(f"xT_hi{i}", [P, DC, P], 140 + 4 * i, F32R) for i in range(2)]
    xT_lo = [sb(f"xT_lo{i}", [P, DC, P], 148 + 4 * i, F32R) for i in range(2)]
    aT_hi = sb("aT_hi", [P, DC, P], 156, F32R)
    aT_lo = sb("aT_lo", [P, DC, P], 160, F32R)
    sg = sb("sg", [P, D], 164)
    lin = sb("lin", [P, D], 168)
    ybuf = [sb(f"ybuf{i}", [P, D], 4 + 4 * i) for i in range(2)]
    glu = sb("glu", [P, D], 12)
    act_rows = sb("act_rows", [P, D], 200)
    pick = [sb(f"pick{i}", [2 * NE, P], 204 + 0.5 * i, F32R) for i in range(2)]
    tok_col = [sb(f"tok_col{i}", [P, 1], 205 + i / 32, I32) for i in range(2)]
    dest_col = [sb(f"dest_col{i}", [P, 1], 205.125 + i / 32, I32) for i in range(2)]
    gate_col = [sb(f"gate_col{i}", [P, 1], 205.25 + i / 32) for i in range(2)]
    hu = bank[:, 0:4, :].rearrange("p b n -> p (b n)")
    yb = bank[:, 4:6, :].rearrange("p b n -> p (b n)")

    gain_in, router_in, bias_in = sem("ffn_gain_in"), sem("router_in"), sem("bias_in")
    moe_consts = sem("moe_consts")
    f_squared, f_mean, f_root, h2_made, h2_stored = sem("f_squared"), sem("f_mean"), sem("f_root"), sem("h2_made"), sem("h2_stored")
    h2T_made, h2T_out, logits_made = sem("h2T_made"), sem("h2T_out"), sem("logits_made")
    gate_diff, gate_exp, chosen_made, place_made = sem("gate_diff"), sem("gate_exp"), sem("chosen_made"), sem("place_made")
    entries_made, row_hot_made = sem("entries_made"), sem("row_hot_made")
    table_made, table_out = sem("table_made"), sem("table_out")
    tableT_made, tableT_out = sem("tableT_made"), sem("tableT_out")
    b_hi_made, b_parts_made = sem("b_hi_made"), sem("b_parts_made")
    unit_in = [sem(f"unit_in{i}") for i in range(RAW)]
    unit_hi, unit_lo, unit_done = sem("unit_hi"), sem("unit_lo"), sem("unit_done")
    early_cols, late_cols = sem("early_cols"), sem("late_cols")
    xg_cleared = sem("xg_cleared")
    gathered = [sem(f"gathered{i}") for i in range(2)]
    rowsT_made, rowsT_hi, rowsT_lo = sem("rowsT_made"), sem("rowsT_hi"), sem("rowsT_lo")
    hu_made, glu_made, sg_made, act_made = sem("hu_made"), sem("glu_made"), sem("sg_made"), sem("act_made")
    lin_made = sem("lin_made")
    y_made, y_out = sem("y_made"), sem("y_out")
    y_stored = [sem(f"y_stored{i}") for i in range(2)]
    busiest_made = sem("busiest_made")
    MORE = SLOTS - 1
    RING = 4
    more_in = [sem(f"more_in{i}") for i in range(RING)]
    more_hi, more_lo, more_done = sem("more_hi"), sem("more_lo"), sem("more_done")
    more_cols, more_gathered, more_stored = sem("more_cols"), sem("more_gathered"), sem("more_stored")
    more_rowsT, more_rows_hi, more_rows_lo = sem("more_rowsT"), sem("more_rows_hi"), sem("more_rows_lo")
    more_hu, more_glu, more_sg, more_act = sem("more_hu"), sem("more_glu"), sem("more_sg"), sem("more_act")
    more_y, more_y_out = sem("more_y"), sem("more_y_out")
    x2_stored = sem("x2_stored")
    proj_step, after_branches = mem["proj_step"], mem["after_branches"]
    after_out = mem["after_out"]

    gate_up = io["w_gate_up"][0].rearrange("e (c p) n -> e p c n", p=P)
    down = io["w_down"][0].rearrange("e (c p) n -> e p c n", p=P)
    out_rows = out[0]

    GU, DN = DC, DC // 2
    AHEAD = 2

    def first_unit(s):
        return 12 * s - 4 if not isinstance(s, int) or s > 0 else 0

    def slot(s, p, m, n):
        if isinstance(s, int):
            return (first_unit(s) + m) % n
        return (m + 8 if p else m - 4) % n

    def unit_loaded(s, p, m):
        if isinstance(s, int):
            return 16 * ((first_unit(s) + m) // RAW + 1)
        if p:
            return 24 * (s - 1) + 16 * ((m + 8) // RAW + 1)
        return 24 * s + 16 * ((m - 4) // RAW + 1)


    def more_blocks(eng, body, begin=None):
        eng.wait_ge(busiest_made, 1)
        most = eng.value_load(busiest[0:1, 0:1], min_val=0, max_val=S)
        with eng.If(most > BLOCK_ROWS):
            for p in range(2):
                eng.wait_ge(y_stored[p], 16 * NE // 2)
            if begin is not None:
                begin()
            with eng.Fori(0, NE) as e:
                for b in range(1, SLOTS):
                    body(e, SLOTS * e + b, MORE * e + (b - 1))

    def load_unit(sp, s, p, m, e_gu, e_dn, m_dn=None):
        u = first_unit(s) + m
        if not (isinstance(s, int) and s == 0 and m < RAW):
            sp.wait_ge(unit_hi, u - RAW + 1)
            sp.wait_ge(unit_lo, u - RAW + 1)
        k = slot(s, p, m, RAW)
        if m_dn is None and m < GU:
            sp.dma_start(raw[k][:], gate_up[bass.ds(e_gu, 1), :, m, :].rearrange("a p n -> (a p) n")).then_inc(unit_in[k], 16)
        else:
            j = m - GU if m_dn is None else m_dn
            sp.dma_start(raw[k][:].rearrange("p (c n) -> p c n", c=2),
                         down[bass.ds(e_dn, 1), :, 2 * j:2 * j + 2, :].rearrange("a p c n -> (a p) c n")).then_inc(unit_in[k], 16)

    def sync(sp):
        sp.wait_ge(proj_step, after_branches)
        sp.dma_start(b_raw[0:NE, 0:2 * D], io["b_gate_up"][0]).then_inc(bias_in, 16)
        sp.dma_start(b_raw[NE:2 * NE, 0:2 * D], io["b_gate_up"][0]).then_inc(bias_in, 16)
        sp.dma_start(b_raw[0:NE, 2 * D:3 * D], io["b_down"][0]).then_inc(bias_in, 16)
        sp.dma_start(b_raw[NE:2 * NE, 2 * D:3 * D], io["b_down"][0]).then_inc(bias_in, 16)
        for m in range(4):
            load_unit(sp, 0, 0, m, 0, 0)
        sp.wait_ge(mem["mT_lo_out"], 8)
        sp.dma_start(ffn_gain[:], io["ffn_norm"][0].partition_broadcast(P)).then_inc(gain_in, 16)
        sp.dma_start(w_router[:], io["w_router"][0].rearrange("(c p) e -> p c e", p=P)).then_inc(router_in, 16)
        sp.dma_start(b_router[:], io["b_router"][0].partition_broadcast(P)).then_inc(router_in, 16)
        sp.wait_ge(mem["w_lo_made"], mem["n_units"])
        for m in range(4, 6):
            load_unit(sp, 0, 0, m, 0, 0)
        for t in range(NT):
            sp.wait_ge(h2_made, t + 1)
            sp.dma_start(io["h2_dram"][t * P:(t + 1) * P, :], h2[:, t, :]).then_inc(h2_stored, 16)
        sp.dma_start(out_rows.rearrange("(t p) d -> p t d", p=P), x2[:]).then_inc(x2_stored, 16)
        sp.wait_ge(x2_stored, 16)
        for m in range(6, 8):
            load_unit(sp, 0, 0, m, 0, 0)
        with sp.Fori(0, NE // 2 - 1) as pair:
            i = 2 * pair + 1
            for p, s in ((1, i), (0, i + 1)):
                for m in range(12):
                    load_unit(sp, s, p, m, s, s - 1)
        for m in range(12):
            load_unit(sp, NE - 1, 1, m, NE - 1, NE - 2)
        for m in range(4):
            load_unit(sp, NE, 0, m, 0, NE - 1, m_dn=m)

        def more_loads(e, column, n):
            for m in range(GU + DN):
                sp.wait_ge(more_lo, 12 * n + m + 1)
                if m < GU:
                    sp.dma_start(raw[m % RING][:], gate_up[bass.ds(e, 1), :, m, :].rearrange("a p n -> (a p) n"))\
                        .then_inc(more_in[m % RING], 16)
                else:
                    j = m - GU
                    sp.dma_start(raw[m % RING][:].rearrange("p (c n) -> p c n", c=2),
                                 down[bass.ds(e, 1), :, 2 * j:2 * j + 2, :].rearrange("a p c n -> (a p) c n"))\
                        .then_inc(more_in[m % RING], 16)

        more_blocks(sp, more_loads)

    def pool(pl):
        pl.wait_ge(proj_step, after_branches)
        pl.memset(tri[:], 1.0).then_inc(moe_consts, 1)
        pl.memset(ones[:], 1.0).then_inc(moe_consts, 1)
        pl.memset(hot64[:], 0.0).then_inc(moe_consts, 1)
        pl.iota(token_i[:], pattern=[[P, NT], [0, TOPK]], base=-S, channel_multiplier=1).then_inc(moe_consts, 1)
        pl.wait_ge(moe_consts, 4)
        pl.affine_select(out=tri[:], in_=tri[:], compare_op=ALU.is_gt, fill=0.0, base=0,
                         pattern=[[1, P]], channel_multiplier=-1).then_inc(moe_consts, 1)
        pl.affine_select(out=hot64[:], in_=hot64[:], compare_op=ALU.not_equal, fill=1.0, base=0,
                         pattern=[[-1, NE]], channel_multiplier=1).then_inc(moe_consts, 1)
        pl.wait_ge(moe_consts, 6)
        pl.affine_select(out=hot64[:], in_=hot64[:], compare_op=ALU.not_equal, fill=1.0, base=-NE,
                         pattern=[[-1, NE]], channel_multiplier=1).then_inc(moe_consts, 1)
        pl.wait_ge(mem["mT_lo_out"], 8)
        pl.iota(iota_row_i[:], pattern=[[1, S]], base=0, channel_multiplier=0).then_inc(moe_consts, 1)

        def wait_step(semaphore, value, met=(b_parts_made, 1)):
            value = value if isinstance(value, int) else pl.snap(value)
            pl.wait_ge(*met)
            pl.wait_ge(semaphore, value)

        def token_col(e, p):
            pl.tensor_copy(tok_col[p][:], tokT[:, bass.ds(SLOTS * e, 1)]).then_inc(early_cols, 1)
            pl.wait_ge(early_cols, e + 1)

        def early(e, p):
            pl.indirect_dma_start(xg[p][:], None, io["h2_dram"], bass.IndirectOffsetOnAxis(tok_col[p][:], 0),
                                  bounds_check=S - 1, oob_is_err=False).then_inc(gathered[p], 16)

        def late(e, p):
            pl.tensor_copy(dest_col[p][:], tokT[:, bass.ds(SLOTS * e, 1)]).then_inc(late_cols, 1)
            pl.tensor_copy(gate_col[p][:], gateT[:, bass.ds(SLOTS * e, 1)]).then_inc(late_cols, 1)
            pl.tensor_copy(pick[p][:], hot64[:, bass.ds(e, 1)].to_broadcast([2 * NE, P])).then_inc(late_cols, 1)

        def store(e, p):
            wait_step(y_out, e + 1)
            pl.indirect_dma_start(out_rows, bass.IndirectOffsetOnAxis(dest_col[p][:], 0), ybuf[p][:], None,
                                  bounds_check=S - 1, oob_is_err=False, compute_op=ALU.add).then_inc(y_stored[p], 16)

        def stored_before(e, p):
            wait_step(y_stored[p], 8 * (e - p))

        pl.wait_ge(table_out, 1)
        pl.memset(xg[0][:], 0.0).then_inc(xg_cleared, 1)
        pl.memset(xg[1][:], 0.0).then_inc(xg_cleared, 1)
        pl.wait_ge(xg_cleared, 2)
        pl.wait_ge(tableT_out, 2)
        pl.wait_ge(h2_stored, 16 * NT)
        pl.wait_ge(b_parts_made, 1)
        token_col(0, 0)
        early(0, 0)
        token_col(1, 1)
        late(0, 0)
        early(1, 1)
        pl.wait_ge(rowsT_made, 2)
        token_col(2, 0)
        late(1, 1)
        early(2, 0)
        pl.wait_ge(rowsT_made, 4)
        token_col(3, 1)
        early(3, 1)
        pl.wait_ge(x2_stored, 16)
        store(0, 0)
        with pl.Fori(0, NE // 2 - 2) as pair:
            i = 2 * pair + 2
            for p, s in ((0, i), (1, i + 1)):
                stored_before(s, p)
                wait_step(rowsT_made, 4 * s)
                token_col(s + 2, p)
                late(s, p)
                early(s + 2, p)
                store(s - 1, 1 - p)
        for s in (NE - 2, NE - 1):
            stored_before(s, s % 2)
            late(s, s % 2)
            store(s - 1, 1 - s % 2)
        stored_before(NE, 0)
        store(NE - 1, 1)
        for p in range(2):
            pl.wait_ge(y_stored[p], 16 * NE // 2)

        def more_rows(e, column, n):
            pl.tensor_copy(tok_col[0][:], tokT[:, bass.ds(column, 1)]).then_inc(more_cols, 1)
            pl.wait_ge(more_cols, 4 * n + 1)
            pl.tensor_copy(gate_col[0][:], gateT[:, bass.ds(column, 1)]).then_inc(more_cols, 1)
            pl.tensor_copy(dest_col[0][:], tokT[:, bass.ds(column, 1)]).then_inc(more_cols, 1)
            pl.tensor_copy(pick[0][:], hot64[:, bass.ds(e, 1)].to_broadcast([2 * NE, P])).then_inc(more_cols, 1)
            pl.indirect_dma_start(xg[0][:], None, io["h2_dram"], bass.IndirectOffsetOnAxis(tok_col[0][:], 0),
                                  bounds_check=S - 1, oob_is_err=False).then_inc(more_gathered, 16)
            wait_step(more_y_out, 4 * n + 1)
            pl.indirect_dma_start(out_rows, bass.IndirectOffsetOnAxis(dest_col[0][:], 0), ybuf[0][:], None,
                                  bounds_check=S - 1, oob_is_err=False, compute_op=ALU.add).then_inc(more_stored, 16)
            wait_step(more_stored, 16 * n + 16)

        more_blocks(pl, more_rows)

    def tensor(te):
        def mm3(out, a, b, first, last=False):
            te.matmul(out, a[0], b[0], start=first, stop=False)
            te.matmul(out, a[0], b[1], start=False, stop=False)
            return te.matmul(out, a[1], b[0], start=False, stop=last)

        def transpose(out, a):
            return te.matmul(out, a, ident[:], is_transpose=True, start=True, stop=True)

        for j in range(8):
            t, half = j // 2, j % 2
            te.wait_ge(h2_made, t + 1)
            if j >= 4:
                te.wait_ge(h2T_out, j - 3)
            for c in range(4):
                m = transpose(bank[:, j % 4, c * P:(c + 1) * P], h2[:, t, (4 * half + c) * P:(4 * half + c + 1) * P])
            m.then_inc(h2T_made, 1)
        te.wait_ge(h2T_out, 8)
        te.wait_ge(router_in, 32)
        for t in range(NT):
            for k in range(DC):
                m = te.matmul(bank[:, 4, t * NE:(t + 1) * NE], h2T[:, k, t * P:(t + 1) * P], w_router[:, k, :],
                              start=k == 0, stop=k == DC - 1)
        m.then_inc(logits_made, 1)
        te.wait_ge(moe_consts, 7)
        te.wait_ge(chosen_made, 1)
        for t in range(NT):
            for u in range(t + 1):
                m = te.matmul(bank[:, 5, t * NE:(t + 1) * NE], (ones if u < t else tri)[:], chosen[:, u, :],
                              start=u == 0, stop=u == t)
        for u in range(NT):
            m = te.matmul(bank[:, 5, NT * NE:(NT + 1) * NE], ones[:], chosen[:, u, :], start=u == 0, stop=u == NT - 1)
        m.then_inc(place_made, 1)
        te.wait_ge(entries_made, 3)
        for j in range(NT * TOPK):
            te.wait_ge(row_hot_made, j + 1)
            m = te.matmul(bank[0:3 * NE, 6, :], entries[:, j].rearrange("p c e -> p (c e)"), row_hot[:, j, :],
                          start=j == 0, stop=j == NT * TOPK - 1)
        m.then_inc(table_made, 1)
        te.wait_ge(table_out, 1)
        for b in range(SLOTS):
            m = te.matmul(bank[:, 4, b * 3 * NE:(b + 1) * 3 * NE], table[:, b * P:(b + 1) * P], ident[0:3 * NE, 0:3 * NE],
                          is_transpose=True, start=True, stop=True)
        m.then_inc(tableT_made, 1)

        def rows_out(dst_event, src, s_is_first):
            for b in range(2):
                if not (s_is_first and b < 2 and isinstance(dst_event, int) and dst_event == 0):
                    te.wait_ge(rowsT_lo, dst_event + b - 1)
                for c in range(4):
                    m = transpose(bank[:, 6 + b, c * P:(c + 1) * P], src[:, (4 * b + c) * P:(4 * b + c + 1) * P])
                m.then_inc(rowsT_made, 1)

        def x_transpose(e_round, p, event, first=False):
            te.wait_ge(gathered[p], e_round)
            rows_out(event, xg[p], first)

        def gate_up_step(s, p, x_event_end, between=None):
            te.wait_ge(rowsT_lo, x_event_end)
            for m in range(GU):
                if m == 2 and between is not None:
                    between()
                k = slot(s, p, m, SPLIT)
                te.wait_ge(unit_lo, first_unit(s) + m + 1)
                for n in range(4):
                    c = slice(n * 512, n * 512 + 512)
                    i = mm3(bank[:, n, :], (xT_hi[p][:, m, :], xT_lo[p][:, m, :]), (hi[k][:, c], lo[k][:, c]), m == 0)
                i.then_inc(unit_done, 1)
            te.wait_ge(late_cols, 3 * (s + 1))
            for n in range(4):
                i = te.matmul(bank[:, n, :], pick[p][:], b_parts[:, n * 512:n * 512 + 512], start=False, stop=True)
            i.then_inc(hu_made, 1)

        def down_step(s, p, a_event, m0=GU):
            te.wait_ge(rowsT_lo, a_event + 2)
            if not (isinstance(s, int) and s == 1):
                te.wait_ge(y_out, s - 1)
            for m in range(DN):
                k = slot(s, 1 - p, m0 + m, SPLIT)
                te.wait_ge(unit_lo, first_unit(s) + m0 + m + 1)
                for c in range(2):
                    for n in range(2):
                        w = slice(c * D + n * 512, c * D + n * 512 + 512)
                        i = mm3(bank[:, 4 + n, :], (aT_hi[:, 2 * m + c, :], aT_lo[:, 2 * m + c, :]),
                                (hi[k][:, w], lo[k][:, w]), m == 0 and c == 0)
                i.then_inc(unit_done, 1)
            for n in range(2):
                i = te.matmul(bank[:, 4 + n, :], pick[p][:], b_parts[:, 2 * D + n * 512:2 * D + n * 512 + 512],
                              start=False, stop=True)
            i.then_inc(y_made, 1)

        te.wait_ge(b_parts_made, 1)
        te.wait_ge(tableT_out, 2)
        x_transpose(16, 0, 0, True)
        gate_up_step(0, 0, 2, lambda: x_transpose(16, 1, 2))

        def whole_step(s, p):
            def transposes():
                te.wait_ge(act_made, s)
                rows_out(4 * s, act_rows, False)
                x_transpose(8 * (s + 1) + (16 if p else 8), 1 - p, 4 * s + 2)

            te.wait_ge(lin_made, 2 * s - 1)
            gate_up_step(s, p, 4 * s, transposes)
            down_step(s, 1 - p, 4 * s)

        whole_step(1, 1)
        whole_step(2, 0)
        with te.Fori(0, NE // 2 - 2) as pair:
            i = 2 * pair + 3
            whole_step(i, 1)
            whole_step(i + 1, 0)
        te.wait_ge(act_made, NE - 1)
        rows_out(4 * (NE - 1), act_rows, False)
        gate_up_step(NE - 1, 1, 4 * (NE - 1))
        down_step(NE - 1, 0, 4 * (NE - 1))
        te.wait_ge(act_made, NE)
        rows_out(4 * NE - 2, act_rows, False)
        down_step(NE, 1, 4 * NE - 2, m0=0)

        def more_rows_out(n, src, first):
            for b in range(2):
                for c in range(4):
                    i = transpose(bank[:, 6 + b, c * P:(c + 1) * P], src[:, (4 * b + c) * P:(4 * b + c + 1) * P])
                i.then_inc(more_rowsT, 1)
            te.wait_ge(more_rows_lo, 4 * n + (2 if first else 4))

        def more_products(e, column, n):
            te.wait_ge(more_gathered, 16 * n + 16)
            more_rows_out(n, xg[0], True)
            for m in range(GU):
                te.wait_ge(more_lo, RING + 12 * n + m + 1)
                for q in range(4):
                    c = slice(q * 512, q * 512 + 512)
                    i = mm3(bank[:, q, :], (xT_hi[0][:, m, :], xT_lo[0][:, m, :]), (hi[m % RING][:, c], lo[m % RING][:, c]), m == 0)
                i.then_inc(more_done, 1)
            te.wait_ge(more_cols, 4 * n + 4)
            for q in range(4):
                i = te.matmul(bank[:, q, :], pick[0][:], b_parts[:, q * 512:q * 512 + 512], start=False, stop=True)
            i.then_inc(more_hu, 1)
            te.wait_ge(more_act, n + 1)
            more_rows_out(n, act_rows, False)
            for m in range(DN):
                k = (GU + m) % RING
                te.wait_ge(more_lo, RING + 12 * n + GU + m + 1)
                for c in range(2):
                    for q in range(2):
                        w = slice(c * D + q * 512, c * D + q * 512 + 512)
                        i = mm3(bank[:, 4 + q, :], (aT_hi[:, 2 * m + c, :], aT_lo[:, 2 * m + c, :]),
                                (hi[k][:, w], lo[k][:, w]), m == 0 and c == 0)
                i.then_inc(more_done, 1)
            for q in range(2):
                i = te.matmul(bank[:, 4 + q, :], pick[0][:], b_parts[:, 2 * D + q * 512:2 * D + q * 512 + 512],
                              start=False, stop=True)
            i.then_inc(more_y, 1)

        more_blocks(te, more_products, begin=lambda: te.sem_inc(more_done, RING))

    def scalar(ac):
        ac.wait_ge(bias_in, 64)
        ac.activation(b_parts[:], b_raw[:], ACT.Copy).then_inc(b_hi_made, 1)
        for t in range(NT):
            ac.wait_ge(mem["x2_made"], NT + t + 1)
            if t:
                ac.wait_ge(f_squared, t)
            else:
                ac.wait_ge(mem["mT_lo_out"], 8)
            ac.activation(square[:], x2[:, t, :], ACT.Square, accum_out=fstat[:, 0, t:t + 1]).then_inc(f_squared, 1)
            ac.wait_ge(f_mean, t + 1)
            ac.activation(fstat[:, 2, t:t + 1], fstat[:, 1, t:t + 1], ACT.Sqrt).then_inc(f_root, 1)
        for j in range(8):
            t, half = j // 2, j % 2
            ac.wait_ge(h2T_made, j + 1)
            ac.activation(h2T[:, 4 * half:4 * half + 4, t * P:(t + 1) * P],
                          bank[:, j % 4, :].rearrange("p (c q) -> p c q", c=4), ACT.Copy).then_inc(h2T_out, 1)
        ac.wait_ge(gate_diff, 1)
        ac.activation(gate[:], gate[:], ACT.Exp).then_inc(gate_exp, 1)
        ac.wait_ge(table_made, 1)
        ac.activation(table[:], bank[0:3 * NE, 6, :], ACT.Copy).then_inc(table_out, 1)

        def split(s, p, m):
            k = slot(s, p, m, SPLIT)
            ac.wait_ge(unit_in[slot(s, p, m, RAW)], unit_loaded(s, p, m))
            if not (isinstance(s, int) and s == 0 and m < SPLIT):
                ac.wait_ge(unit_done, first_unit(s) + m - SPLIT + 1)
            ac.activation(hi[k][:], raw[slot(s, p, m, RAW)][:], ACT.Copy).then_inc(unit_hi, 1)

        def rows_hi(event, dst):
            for b in range(2):
                ac.wait_ge(rowsT_made, event + b + 1)
                ac.activation(dst[:, 4 * b:4 * b + 4, :], bank[:, 6 + b, :].rearrange("p (c q) -> p c q", c=4), ACT.Copy)\
                    .then_inc(rowsT_hi, 1)

        def sigmoid(s):
            ac.wait_ge(glu_made, s + 1)
            ac.activation(sg[:], glu[:], ACT.Sigmoid, scale=1.702).then_inc(sg_made, 1)

        def y_rows(e, p, wait=True):
            ac.wait_ge(y_made, e + 1)
            if wait:
                ac.wait_ge(y_stored[p], 8 * (e - p))
            ac.activation(ybuf[p][:], yb, ACT.Copy, scale=gate_col[p][:]).then_inc(y_out, 1)

        ac.wait_ge(mem["w_lo_made"], mem["n_units"])
        ac.wait_ge(proj_step, after_out)
        ac.wait_ge(tableT_out, 2)
        ac.wait_ge(b_parts_made, 1)
        for m in range(4):
            split(0, 0, m)
        rows_hi(0, xT_hi[0])
        rows_hi(2, xT_hi[1])
        for m in range(4, GU):
            split(0, 0, m)
        for m in range(AHEAD):
            split(1, 1, m)
        sigmoid(0)

        def whole_step(s, p, last=False):
            for m in range(AHEAD if isinstance(s, int) and s == 1 else 0, 12):
                if m == 3:
                    if not (isinstance(s, int) and s == 1):
                        y_rows(s - 2, p, wait=not (isinstance(s, int) and s < 4))
                    rows_hi(4 * s, aT_hi)
                    if not last:
                        rows_hi(4 * s + 2, xT_hi[1 - p])
                split(s, p, m)
            sigmoid(s)

        for s in (1, 2, 3, 4):
            whole_step(s, s % 2)
        with ac.Fori(0, NE // 2 - 3) as pair:
            i = 2 * pair + 5
            whole_step(i, 1)
            whole_step(i + 1, 0)
        whole_step(NE - 1, 1, last=True)
        for m in range(3):
            split(NE, 0, m)
        y_rows(NE - 2, 0)
        rows_hi(4 * NE - 2, aT_hi)
        split(NE, 0, 3)
        y_rows(NE - 1, 1)

        def more_acts(e, column, n):
            def rows(first, dst):
                for b in range(2):
                    ac.wait_ge(more_rowsT, 4 * n + (0 if first else 2) + b + 1)
                    ac.activation(dst[:, 4 * b:4 * b + 4, :], bank[:, 6 + b, :].rearrange("p (c q) -> p c q", c=4), ACT.Copy)\
                        .then_inc(more_rows_hi, 1)

            def splits(first, last):
                for m in range(first, last):
                    ac.wait_ge(more_in[m % RING], 16 * (3 * n + m // RING + 1))
                    ac.wait_ge(more_done, 12 * n + m + 1)
                    ac.activation(hi[m % RING][:], raw[m % RING][:], ACT.Copy).then_inc(more_hi, 1)

            rows(True, xT_hi[0])
            splits(0, GU)
            ac.wait_ge(more_glu, n + 1)
            ac.activation(sg[:], glu[:], ACT.Sigmoid, scale=1.702).then_inc(more_sg, 1)
            rows(False, aT_hi)
            splits(GU, GU + DN)
            ac.wait_ge(more_y, n + 1)
            ac.activation(ybuf[0][:], yb, ACT.Copy, scale=gate_col[0][:]).then_inc(more_y_out, 4)

        more_blocks(ac, more_acts)

    def norm_x2(ve, t):
        step = mem["step"]
        ve.wait_ge(f_squared, t + 1)
        ve.tensor_scalar(fstat[:, 1, t:t + 1], fstat[:, 0, t:t + 1], 1.0 / D, EPS, ALU.mult, ALU.add).then_inc(f_mean, 1)
        ve.wait_ge(f_root, t + 1)
        step(ve.reciprocal(fstat[:, 3, t:t + 1], fstat[:, 2, t:t + 1]))
        ve.wait_ge(gain_in, 16)
        ve.scalar_tensor_tensor(h2[:, t, :], x2[:, t, :], fstat[:, 3, t:t + 1], ffn_gain[:], ALU.mult, ALU.mult)\
            .then_inc(h2_made, 1)

    def split_biases(ve):
        ve.wait_ge(b_hi_made, 1)
        ve.tensor_tensor(b_parts[NE:2 * NE, :], b_raw[NE:2 * NE, :], b_parts[NE:2 * NE, :].bitcast(F32), ALU.subtract)\
            .then_inc(b_parts_made, 1)

    mem["norm_x2"] = norm_x2
    mem["split_biases"] = split_biases

    def vector(ve):
        step = mem["step"]
        norm_x2(ve, NT - 1)
        ve.wait_ge(moe_consts, 8)
        ve.wait_ge(proj_step, after_out)
        step(ve.tensor_copy(iota_row[:], iota_row_i[:]))
        step(ve.tensor_copy(token_f[:], token_i[:]))
        ve.wait_ge(router_in, 32)
        ve.wait_ge(logits_made, 1)
        step(ve.tensor_tensor(logits[:], bank[:, 4, 0:NT * NE].rearrange("p (t e) -> p t e", t=NT),
                              b_router[:].unsqueeze(1).to_broadcast([P, NT, NE]), ALU.add))
        for t in range(NT):
            step(ve.max(top_val[:, t, :], logits[:, t, :]))
            step(ve.max_index(top_idx[:, t, :], top_val[:, t, :], logits[:, t, :]))
        step(ve.tensor_copy(top_f[:], top_idx[:, :, 0:TOPK]))
        ve.tensor_tensor(gate[:], top_val[:, :, 0:TOPK], top_val[:, :, 0:1].to_broadcast([P, NT, TOPK]), ALU.subtract)\
            .then_inc(gate_diff, 1)
        step(ve.tensor_tensor(onehot[:].rearrange("p t k e -> p (t k) e"),
                              iota_row[:, 0:NE].unsqueeze(1).to_broadcast([P, NT * TOPK, NE]),
                              top_f[:].rearrange("p t k -> p (t k)").unsqueeze(2).to_broadcast([P, NT * TOPK, NE]), ALU.is_equal))
        ve.reduce_sum(chosen[:], onehot[:].rearrange("p t k e -> p t e k"), axis=AX.X).then_inc(chosen_made, 1)
        ve.wait_ge(gate_exp, 1)
        step(ve.reduce_sum(gate_sum[:], gate[:], axis=AX.X))
        step(ve.reciprocal(gate_sum[:], gate_sum[:]))
        step(ve.tensor_tensor(gate[:], gate[:], gate_sum[:].unsqueeze(2).to_broadcast([P, NT, TOPK]), ALU.mult))
        step(ve.tensor_copy(gate_hi[:], gate[:]))
        step(ve.tensor_tensor(gate_lo[:], gate[:], gate_hi[:].bitcast(F32), ALU.subtract))
        for part, value in enumerate((token_f[:], gate_hi[:].bitcast(F32), gate_lo[:])):
            ve.tensor_tensor(entries[:, :, part, :], onehot[:].rearrange("p t k e -> p (t k) e"),
                             value.rearrange("p t k -> p (t k)").unsqueeze(2).to_broadcast([P, NT * TOPK, NE]), ALU.mult)\
                .then_inc(entries_made, 1)
        ve.wait_ge(place_made, 1)
        step(ve.tensor_copy(place[:], bank[:, 5, 0:NT * NE].rearrange("p (t e) -> p t e", t=NT)))
        for t in range(NT):
            last = ve.tensor_tensor(picked[:, t], onehot[:, t], place[:, t, :].unsqueeze(1).to_broadcast([P, TOPK, NE]), ALU.mult)
        step(last)
        step(ve.reduce_sum(row_of[:], picked[:].rearrange("p t k e -> p (t k) e"), axis=AX.X))
        for j in range(NT * TOPK):
            ve.tensor_scalar(row_hot[:, j, :], iota_row[:], row_of[:, j:j + 1], None, ALU.is_equal).then_inc(row_hot_made, 1)
        step(ve.reduce_max(busiest_f[:], bank[:, 5, NT * NE:(NT + 1) * NE], axis=AX.X))
        ve.tensor_copy(busiest[:], busiest_f[:]).then_inc(busiest_made, 1)
        ve.wait_ge(tableT_made, 1)
        tableT = bank[:, 4, 0:SLOTS * 3 * NE].rearrange("p (b c e) -> p c e b", b=SLOTS, c=3)
        ve.tensor_scalar(tokT[:].rearrange("p (e b) -> p e b", b=SLOTS), tableT[:, 0], float(S), None, ALU.add).then_inc(tableT_out, 1)
        step(ve.tensor_copy(gateT[:].rearrange("p (e b) -> p e b", b=SLOTS), tableT[:, 1]))
        ve.tensor_tensor(gateT[:].rearrange("p (e b) -> p e b", b=SLOTS), gateT[:].rearrange("p (e b) -> p e b", b=SLOTS),
                         tableT[:, 2], ALU.add).then_inc(tableT_out, 1)

        def split(s, p, m):
            k = slot(s, p, m, SPLIT)
            ve.wait_ge(unit_hi, first_unit(s) + m + 1)
            ve.tensor_tensor(lo[k][:], raw[slot(s, p, m, RAW)][:], hi[k][:].bitcast(F32), ALU.subtract).then_inc(unit_lo, 1)

        def rows_lo(event, dst, dst_hi):
            for b in range(2):
                ve.wait_ge(rowsT_hi, event + b + 1)
                ve.tensor_tensor(dst[:, 4 * b:4 * b + 4, :], bank[:, 6 + b, :].rearrange("p (c q) -> p c q", c=4),
                                 dst_hi[:, 4 * b:4 * b + 4, :].bitcast(F32), ALU.subtract).then_inc(rowsT_lo, 1)

        def swiglu(s, p, between=None):
            ve.wait_ge(hu_made, s + 1)
            v = hu.rearrange("p (f two) -> p f two", two=2)
            ve.tensor_scalar(glu[:], v[:, :, 0], 7.0, None, ALU.min).then_inc(glu_made, 1)
            if between is not None:
                split(s, p, between)
            ve.tensor_scalar(lin[:], v[:, :, 1], 7.0, -7.0, ALU.min, ALU.max).then_inc(lin_made, 1)
            ve.wait_ge(glu_made, s + 1)
            ve.wait_ge(lin_made, 2 * s + 1)
            ve.scalar_tensor_tensor(lin[:], lin[:], 1.0, glu[:], ALU.add, ALU.mult).then_inc(lin_made, 1)
            ve.wait_ge(lin_made, 2 * s + 2)
            ve.wait_ge(sg_made, s + 1)
            ve.tensor_tensor(act_rows[:], lin[:], sg[:], ALU.mult).then_inc(act_made, 1)

        ve.wait_ge(h2_stored, 16 * NT)
        for m in range(4):
            split(0, 0, m)
        rows_lo(0, xT_lo[0], xT_hi[0])
        rows_lo(2, xT_lo[1], xT_hi[1])
        for m in range(4, GU):
            split(0, 0, m)
        for m in range(AHEAD):
            split(1, 1, m)
        swiglu(0, 0)

        def whole_step(s, p, last=False):
            for m in range(AHEAD if isinstance(s, int) and s == 1 else 0, 11):
                if m == 3:
                    rows_lo(4 * s, aT_lo, aT_hi)
                    if not last:
                        rows_lo(4 * s + 2, xT_lo[1 - p], xT_hi[1 - p])
                split(s, p, m)
            swiglu(s, p, between=11)

        whole_step(1, 1)
        whole_step(2, 0)
        with ve.Fori(0, NE // 2 - 2) as pair:
            i = 2 * pair + 3
            whole_step(i, 1)
            whole_step(i + 1, 0)
        whole_step(NE - 1, 1, last=True)
        for m in range(3):
            split(NE, 0, m)
        rows_lo(4 * NE - 2, aT_lo, aT_hi)
        split(NE, 0, 3)

        def more_vectors(e, column, n):
            def rows(first, dst, dst_hi):
                for b in range(2):
                    ve.wait_ge(more_rows_hi, 4 * n + (0 if first else 2) + b + 1)
                    ve.tensor_tensor(dst[:, 4 * b:4 * b + 4, :], bank[:, 6 + b, :].rearrange("p (c q) -> p c q", c=4),
                                     dst_hi[:, 4 * b:4 * b + 4, :].bitcast(F32), ALU.subtract).then_inc(more_rows_lo, 1)

            def splits(first, last):
                for m in range(first, last):
                    ve.wait_ge(more_hi, 12 * n + m + 1)
                    ve.tensor_tensor(lo[m % RING][:], raw[m % RING][:], hi[m % RING][:].bitcast(F32), ALU.subtract)\
                        .then_inc(more_lo, 1)

            rows(True, xT_lo[0], xT_hi[0])
            splits(0, GU)
            ve.wait_ge(more_hu, n + 1)
            v = hu.rearrange("p (f two) -> p f two", two=2)
            ve.tensor_scalar(glu[:], v[:, :, 0], 7.0, None, ALU.min).then_inc(more_glu, 1)
            ve.tensor_scalar(lin[:], v[:, :, 1], 7.0, -7.0, ALU.min, ALU.max).then_inc(lin_made, 1)
            ve.wait_ge(more_glu, n + 1)
            ve.wait_ge(lin_made, 2 * NE + 2 * n + 1)
            ve.scalar_tensor_tensor(lin[:], lin[:], 1.0, glu[:], ALU.add, ALU.mult).then_inc(lin_made, 1)
            ve.wait_ge(lin_made, 2 * NE + 2 * n + 2)
            ve.wait_ge(more_sg, n + 1)
            ve.tensor_tensor(act_rows[:], lin[:], sg[:], ALU.mult).then_inc(more_act, 1)
            rows(False, aT_lo, aT_hi)
            splits(GU, GU + DN)

        more_blocks(ve, more_vectors, begin=lambda: ve.sem_inc(more_lo, RING))

    return dict(sync=sync, pool=pool, tensor=tensor, scalar=scalar, vector=vector)


def program(nc, io, out):
    base = (nc.sbuf_base + 31) // 32 * 32

    def sb(name, shape, at_kb, dtype=F32):
        return nc.alloc_sbuf_tensor_at(name, shape, dtype, offset=base + int(at_kb * KB))

    bank = nc.alloc_psum_tensor("bank", [P, 8, 512], F32)
    mem = dict(ident=sb("ident", [P, P], 16), flip=sb("flip", [P, P], 16.5), x2=sb("x2", [P, NT, D], 172))
    for n in ("consts_made", "x2_made", "dve_step", "act_step"):
        mem[n] = nc.alloc_semaphore(n)
    pre = pre_moe(nc, io, sb, nc.alloc_semaphore, bank, mem)
    exp = moe(nc, io, out, sb, nc.alloc_semaphore, bank, mem)
    with nc.Block() as block:
        @block.sync
        def _(sp):
            pre["sync"](sp)
            exp["sync"](sp)

        @block.gpsimd
        def _(pl):
            pre["pool"](pl)
            exp["pool"](pl)

        @block.tensor
        def _(te):
            pre["tensor"](te)
            exp["tensor"](te)

        @block.scalar
        def _(ac):
            pre["scalar"](ac)
            exp["scalar"](ac)

        @block.vector
        def _(ve):
            pre["vector"](ve)
            exp["vector"](ve)


INPUTS = ["x", "attn_norm", "w_in", "nsa_q_norm", "nsa_k_norm", "cmp_k_w1", "cmp_k_w2", "cmp_v_w1", "cmp_v_w2",
          "dsa_kv_norm", "dsa_w_uk", "dsa_w_uv", "dsa_q_norm", "dsa_k_norm", "w_branch_a", "w_branch_b", "w_out",
          "rel_bias", "ffn_norm", "w_router", "b_router", "w_gate_up", "b_gate_up", "w_down", "b_down"]


def kernel(**inputs):
    import concourse.bacc as bacc
    from concourse.bass_utils import run_bass_kernel_spmd
    nc = bacc.Bacc("TRN2", target_bir_lowering=False, num_devices=1)
    arrays = {n: np.ascontiguousarray(inputs[n]) for n in INPUTS}
    arrays["pe_cols"] = np.ascontiguousarray(np.stack(
        [np.asarray(inputs[n]).reshape(16, P).T for n in ("cmp_k_pe", "cmp_v_pe")], axis=1))
    arrays["b1_cols"] = np.ascontiguousarray(np.stack(
        [np.asarray(inputs[n]).reshape(P) for n in ("cmp_k_b1", "cmp_v_b1")], axis=1))
    arrays["bias_hot"] = bias_one_hot()
    io = {n: nc.dram_tensor(n, a.shape, mybir.dt.from_np(a.dtype), kind="ExternalInput").ap() for n, a in arrays.items()}
    for n, shape in (("vec_dram", (2 * NH, 5 * P)), ("h2_dram", (S, D))):
        io[n] = nc.dram_tensor(n, shape, F32, kind="Internal").ap()
    out = nc.dram_tensor("out", (1, S, D), F32, kind="ExternalOutput").ap()
    program(nc, io, out)
    return run_bass_kernel_spmd(nc, [arrays], core_ids=[0]).results[0]["out"]
```
